# Optimizing a Trainium2 kernel written in Bass

```python
import jax, jax.numpy as jnp
from jax import lax
import numpy as np

D_MODEL = 1024
BATCH = 1
SEQ = 1024
DEPTH = 1

CTX_LEN = 256
GRID_W = 64
MIX_WIDTH = D_MODEL
POOL_WIDTH = MIX_WIDTH // 2
POOL_GROUPS = 4
POOL_GROUP_W = POOL_WIDTH // POOL_GROUPS
POOL_WINDOWS = (2, 4, 8, 16)
GLA_WIDTH = MIX_WIDTH - POOL_WIDTH
GLA_HEADS = 4
GLA_DV = GLA_WIDTH // GLA_HEADS
GLA_DK = GLA_DV // 2
GLA_QK = GLA_HEADS * GLA_DK
GATE_RANK = 16
GATE_NORM = 16.0
CHUNK = 32
N_EXPERTS = 16
N_GROUPS = 4
EXPERTS_PER_GROUP = N_EXPERTS // N_GROUPS
TOP_K = 2
D_EXPERT = D_MODEL // 2
MOE_BLOCK = 128
N_MOD = 6
EPS = 1e-6
IN_SPLITS = (POOL_WIDTH, POOL_WIDTH + GLA_QK, POOL_WIDTH + 2 * GLA_QK,
             POOL_WIDTH + 2 * GLA_QK + GLA_WIDTH, POOL_WIDTH + 2 * GLA_QK + 2 * GLA_WIDTH)
IN_WIDTH = IN_SPLITS[-1] + 2 * GATE_RANK

kernel_name = "hybrid_pool_gla_moe_prefix_dit"

def _rmsnorm(x, gain):
    xf = x.astype(jnp.float32)
    y = xf * lax.rsqrt(jnp.mean(xf * xf, axis=-1, keepdims=True) + EPS)
    return (y * gain.astype(jnp.float32)).astype(x.dtype)

def _modulation(cvec, w_mod, b_mod):
    return jnp.split(jax.nn.silu(cvec) @ w_mod + b_mod, N_MOD, axis=-1)

def _box_mean(u, axis, w):
    L = u.shape[axis]
    idx = np.arange(L)
    lo = np.clip(idx - w // 2, 0, L)
    hi = np.clip(idx + w - w // 2, 0, L)
    pad = [(0, 0)] * u.ndim
    pad[axis] = (1, 0)
    cs = jnp.pad(jnp.cumsum(u, axis=axis), pad)
    total = jnp.take(cs, hi, axis=axis) - jnp.take(cs, lo, axis=axis)
    cnt = (hi - lo).astype(np.float32).reshape((L,) + (1,) * (u.ndim - axis - 1))
    return total / cnt

def _pool_mixer(u, w_pool, pool_scale, grid):
    B, L, _ = u.shape
    uf = u.astype(jnp.float32)
    if grid:
        rows = L // GRID_W
        ug = uf.reshape(B, rows, GRID_W, POOL_GROUPS, POOL_GROUP_W)
        means = [_box_mean(_box_mean(ug[..., g, :], 1, w), 2, w) for g, w in enumerate(POOL_WINDOWS)]
    else:
        ug = uf.reshape(B, L, POOL_GROUPS, POOL_GROUP_W)
        means = [_box_mean(ug[..., g, :], 1, w) for g, w in enumerate(POOL_WINDOWS)]
    pooled = jnp.stack(means, axis=-2).reshape(B, L, POOL_GROUPS, POOL_GROUP_W) \
        - uf.reshape(B, L, POOL_GROUPS, POOL_GROUP_W)
    mixed = jnp.einsum('blgc,gcd->blgd', pooled, w_pool)
    return (mixed.reshape(B, L, POOL_WIDTH) * pool_scale).astype(u.dtype)

def _split_proj(p, w_gk2, b_gk):
    B, L, _ = p.shape
    u, q, k, v, g, r = jnp.split(p, IN_SPLITS, axis=-1)
    heads = lambda t, d: t.reshape(B, L, GLA_HEADS, d).transpose(0, 2, 1, 3)
    q = heads(q, GLA_DK) * (GLA_DK ** -0.5)
    k = heads(k, GLA_DK)
    v = heads(v, GLA_DV)
    r = r.reshape(B, L, 2, GATE_RANK)
    logit = jnp.einsum('blnr,nrk->nblk', r, w_gk2) + b_gk[:, None, None, :]
    lg = jax.nn.log_sigmoid(logit.astype(jnp.float32)) / GATE_NORM
    lg = lg.reshape(2, B, L, GLA_HEADS, GLA_DK).transpose(0, 1, 3, 2, 4)
    return u, q, k, v, g, lg

def _gla_chunked(q, k, v, lg, s0):
    B, H, L, dk = q.shape
    dv = v.shape[-1]
    n = L // CHUNK
    q = q.reshape(B, H, n, CHUNK, dk)
    k = k.reshape(B, H, n, CHUNK, dk)
    v = v.reshape(B, H, n, CHUNK, dv)
    b = jnp.cumsum(lg.reshape(B, H, n, CHUNK, dk), axis=3)
    b_last = b[:, :, :, -1:, :]
    mask = np.tril(np.ones((CHUNK, CHUNK), dtype=bool))[:, :, None]
    decay = jnp.exp(jnp.where(mask, b[..., :, None, :] - b[..., None, :, :], -jnp.inf))
    scores = jnp.einsum('bhnid,bhnjd,bhnijd->bhnij', q, k, decay)
    o_intra = jnp.einsum('bhnij,bhnje->bhnie', scores, v)
    kv = jnp.einsum('bhncd,bhnce->bhnde', k * jnp.exp(b_last - b), v)
    chunk_decay = jnp.exp(b_last[:, :, :, 0, :])

    def step(S, inp):
        a, kvn = inp
        return a[..., None] * S + kvn, S

    s_final, s_prev = lax.scan(step, s0, (jnp.moveaxis(chunk_decay, 2, 0), jnp.moveaxis(kv, 2, 0)))
    s_prev = jnp.moveaxis(s_prev, 0, 2)
    o_inter = jnp.einsum('bhncd,bhnde->bhnce', q * jnp.exp(b), s_prev)
    return (o_intra + o_inter).reshape(B, H, L, dv), s_final

def _mix_out(u, o, g, grid, w_pool, pool_scale, gla_gain, w_out):
    B, L, _ = u.shape
    pool = _pool_mixer(u, w_pool, pool_scale, grid)
    o = _rmsnorm(o, gla_gain).transpose(0, 2, 1, 3).reshape(B, L, GLA_WIDTH)
    gla = (o * jax.nn.silu(g)).astype(u.dtype)
    return jnp.concatenate([pool, gla], axis=-1) @ w_out

def _mixer(hx, hc, w_in, w_gk2, b_gk, w_pool, pool_scale, gla_gain, w_out, need_ctx):
    ux, qx, kx, vx, gx, lgx = _split_proj(hx @ w_in, w_gk2, b_gk)
    uc, qc, kc, vc, gc, lgc = _split_proj(hc @ w_in, w_gk2, b_gk)
    B = hx.shape[0]
    zero = jnp.zeros((B, GLA_HEADS, GLA_DK, GLA_DV), jnp.float32)
    flip = lambda t: jnp.flip(t, axis=2)
    oc_f, s_f = _gla_chunked(qc, kc, vc, lgc[0], zero)
    ox_f, _ = _gla_chunked(qx, kx, vx, lgx[0], s_f)
    oc_b, s_b = _gla_chunked(flip(qc), flip(kc), flip(vc), flip(lgc[1]), zero)
    ox_b, _ = _gla_chunked(flip(qx), flip(kx), flip(vx), flip(lgx[1]), s_b)
    yx = _mix_out(ux, ox_f + flip(ox_b), gx, True, w_pool, pool_scale, gla_gain, w_out)
    yc = _mix_out(uc, oc_f + flip(oc_b), gc, False, w_pool, pool_scale, gla_gain, w_out) if need_ctx else None
    return yx, yc

def _moe(xf, w_router, router_bias, w1, w3, w2):
    T, D = xf.shape
    s = jax.nn.sigmoid((xf @ w_router).astype(jnp.float32))
    sb = (s + router_bias).reshape(T, N_GROUPS, EXPERTS_PER_GROUP)
    group_score = lax.top_k(sb, 2)[0].sum(-1)
    gsel = jnp.argmax(group_score, axis=-1)
    in_group = jnp.take_along_axis(sb, gsel[:, None, None], axis=1)[:, 0]
    _, loc = lax.top_k(in_group, TOP_K)
    eidx = gsel[:, None] * EXPERTS_PER_GROUP + loc
    wts = jnp.take_along_axis(s, eidx, axis=1)
    wts = wts / jnp.sum(wts, axis=-1, keepdims=True)
    flat_e = eidx.reshape(-1)
    order = jnp.argsort(flat_e)
    se = flat_e[order]
    tok = order // TOP_K
    counts = jnp.bincount(flat_e, length=N_EXPERTS)
    padded = (counts + MOE_BLOCK - 1) // MOE_BLOCK * MOE_BLOCK
    start = jnp.cumsum(counts) - counts
    pend = jnp.cumsum(padded)
    pstart = pend - padded
    dest = pstart[se] + (jnp.arange(T * TOP_K) - start[se])
    n_blocks = (T * TOP_K + N_EXPERTS * (MOE_BLOCK - 1) + MOE_BLOCK - 1) // MOE_BLOCK
    xb = jnp.zeros((n_blocks * MOE_BLOCK, D), xf.dtype).at[dest].set(xf[tok])
    block_e = jnp.clip(jnp.searchsorted(pend, jnp.arange(n_blocks) * MOE_BLOCK, side='right'), 0, N_EXPERTS - 1)

    def expert_block(args):
        xblk, e = args
        return (jax.nn.silu(xblk @ w1[e]) * (xblk @ w3[e])) @ w2[e]

    yb = lax.map(expert_block, (xb.reshape(n_blocks, MOE_BLOCK, D), block_e)).reshape(-1, D)
    y = (yb[dest] * wts.reshape(-1)[order][:, None]).astype(xf.dtype)
    return jnp.zeros_like(xf).at[tok].add(y)

def setup_inputs(seed: int = 0) -> dict:
    key = jax.random.key(seed)
    ks = jax.random.split(key, 22)
    nrm = lambda kk, shape, scale: scale * jax.random.normal(kk, shape, jnp.float32)
    return {
        "x": nrm(ks[0], (BATCH, SEQ, D_MODEL), 1.0),
        "c": nrm(ks[1], (BATCH, D_MODEL), 1.0),
        "ctx": nrm(ks[2], (BATCH, CTX_LEN, D_MODEL), 1.0),
        "c_ctx": nrm(ks[3], (D_MODEL,), 1.0),
        "w_mod": nrm(ks[4], (DEPTH, D_MODEL, N_MOD * D_MODEL), 0.5 * D_MODEL ** -0.5),
        "b_mod": nrm(ks[5], (DEPTH, N_MOD * D_MODEL), 0.02),
        "norm1": 1.0 + nrm(ks[6], (DEPTH, D_MODEL), 0.05),
        "norm2": 1.0 + nrm(ks[7], (DEPTH, D_MODEL), 0.05),
        "w_in": nrm(ks[8], (DEPTH, D_MODEL, IN_WIDTH), D_MODEL ** -0.5),
        "w_gk2": nrm(ks[9], (DEPTH, 2, GATE_RANK, GLA_QK), GATE_RANK ** -0.5),
        "b_gk": nrm(ks[10], (DEPTH, 2, GLA_QK), 0.5),
        "w_pool": nrm(ks[11], (DEPTH, POOL_GROUPS, POOL_GROUP_W, POOL_GROUP_W), POOL_GROUP_W ** -0.5),
        "pool_scale": 1.0 + nrm(ks[12], (DEPTH, POOL_WIDTH), 0.1),
        "gla_gain": 1.0 + nrm(ks[13], (DEPTH, GLA_DV), 0.05),
        "w_out": nrm(ks[14], (DEPTH, MIX_WIDTH, D_MODEL), MIX_WIDTH ** -0.5),
        "w_router": nrm(ks[15], (D_MODEL, N_EXPERTS), D_MODEL ** -0.5),
        "router_bias": nrm(ks[16], (N_EXPERTS,), 0.01),
        "w1": nrm(ks[17], (DEPTH, N_EXPERTS, D_MODEL, D_EXPERT), D_MODEL ** -0.5),
        "w3": nrm(ks[18], (DEPTH, N_EXPERTS, D_MODEL, D_EXPERT), D_MODEL ** -0.5),
        "w2": nrm(ks[19], (DEPTH, N_EXPERTS, D_EXPERT, D_MODEL), D_EXPERT ** -0.5),
        "norm_f": 1.0 + nrm(ks[20], (D_MODEL,), 0.05),
    }

def reference(x, c, ctx, c_ctx, w_mod, b_mod, norm1, norm2, w_in, w_gk2, b_gk, w_pool, pool_scale,
              gla_gain, w_out, w_router, router_bias, w1, w3, w2, norm_f):
    B, S, D = x.shape
    for l in range(DEPTH):
        keep_ctx = l < DEPTH - 1
        sx1, cx1, gx1, sx2, cx2, gx2 = [m[:, None, :] for m in _modulation(c, w_mod[l], b_mod[l])]
        sc1, cc1, gc1, sc2, cc2, gc2 = _modulation(c_ctx, w_mod[l], b_mod[l])
        hx = _rmsnorm(x, norm1[l]) * (1.0 + cx1) + sx1
        hc = _rmsnorm(ctx, norm1[l]) * (1.0 + cc1) + sc1
        yx, yc = _mixer(hx, hc, w_in[l], w_gk2[l], b_gk[l], w_pool[l], pool_scale[l], gla_gain[l], w_out[l],
                        keep_ctx)
        x = x + gx1 * yx
        hx = _rmsnorm(x, norm2[l]) * (1.0 + cx2) + sx2
        if keep_ctx:
            ctx = ctx + gc1 * yc
            hc = _rmsnorm(ctx, norm2[l]) * (1.0 + cc2) + sc2
            tokens = jnp.concatenate([hx.reshape(-1, D), hc.reshape(-1, D)], axis=0)
            out = _moe(tokens, w_router, router_bias, w1[l], w3[l], w2[l])
            x = x + gx2 * out[:B * S].reshape(x.shape)
            ctx = ctx + gc2 * out[B * S:].reshape(ctx.shape)
        else:
            x = x + gx2 * _moe(hx.reshape(-1, D), w_router, router_bias, w1[l], w3[l], w2[l]).reshape(x.shape)
    return _rmsnorm(x, norm_f)


_drawn_inputs = setup_inputs


def setup_inputs(seed=0):
    import zlib

    import numpy as np

    out = dict(_drawn_inputs(seed))
    spreads = {}
    factors = {'ctx': 4.025, 'c_ctx': 4.714, 'gla_gain': 3.256}
    for name, (base, spread) in spreads.items():
        noise = np.random.default_rng([zlib.crc32(name.encode()), seed]).standard_normal(out[name].shape)
        drawn = base * np.exp(spread * noise) if base else spread * noise
        out[name] = __import__('jax').numpy.asarray(drawn.astype(out[name].dtype))
    for name, factor in factors.items():
        out[name] = (out[name] * factor).astype(out[name].dtype)
    return out
```

```python
from contextlib import ExitStack

import numpy as np

import concourse.bass as bass
from concourse import mybir

F32 = mybir.dt.float32
I32 = mybir.dt.int32
ALU = mybir.AluOpType
ACT = mybir.ActivationFunctionType
AX = mybir.AxisListType

P = 128
D = 1024
KC = D // P
NX = 8
NCT = 2
NT = NX + NCT
N_MOD = 6
EPS = 1e-6
GRID_W = 64
GRID_H = NX * P // GRID_W
WINDOWS = (2, 4, 8, 16)
NG = len(WINDOWS)
HALF = 512
HEADS = 4
DV = 128
DK = 64
QK = HEADS * DK
RANK2 = 32
GATE_NORM = 16.0
COL_U, COL_Q, COL_V, COL_G, COL_R = 0, HALF, HALF + 2 * QK, 2 * HALF + 2 * QK, 3 * HALF + 2 * QK
MID = P // 2
NE = 16
NGR = 4
MAXB = 31
NB = MAXB + 1
UNIT = KC * HALF
EXPERT = 3 * UNIT
BIG = 1.0e30


def box_inverse_counts():
    out = np.zeros((NG, GRID_H + GRID_W), np.float32)
    for g, w in enumerate(WINDOWS):
        for base, n in ((0, GRID_H), (GRID_H, GRID_W)):
            i = np.arange(n)
            count = np.clip(i + w - w // 2, 0, n) - np.clip(i - w // 2, 0, n)
            out[g, base:base + n] = (1.0 / count).astype(np.float32)
    return out.reshape(1, -1)


def hybrid_block(nc, x, c, ctx_in, c_ctx, w_mod, b_mod, norm1, norm2, w_in, w_gk2, b_gk, w_pool,
                 pool_scale, gla_gain, w_out, w_router, router_bias, w1, w3, w2, norm_f, inv_counts, out):
    with ExitStack() as stack:
        def sb(name, shape, dt=F32):
            return stack.enter_context(nc.sbuf_tensor(name, shape, dt))

        def sem(name):
            return stack.enter_context(nc.semaphore(name))

        ARENA = 49152
        arena = sb("arena", [P, ARENA])

        def at(off, pattern=None, n=None, **dims):
            v = arena[:, off:off + n]
            return v.rearrange(pattern, **dims) if pattern else v

        RING = 3
        ring = [at(s * UNIT, "p (k n) -> p k n", UNIT, k=KC) for s in range(RING)]
        O_HX = RING * UNIT
        hxT = at(O_HX, "p (k t) -> p k t", KC * NT * P, k=KC)
        O_QB = O_HX + KC * NT * P
        qbd = at(O_QB, "p (t d a h i) -> p t d a h i", NX * 1024, t=NX, d=2, a=2, h=2)
        O_K = O_QB + NX * 1024
        kdec = at(O_K, "p (t d a i) -> p t d a i", NT * HALF, t=NT, d=2, a=2)
        O_V = O_K + NT * HALF
        vals = at(O_V, "p (t n) -> p t n", NT * HALF, t=NT)
        O_G = O_V + NT * HALF
        gate = at(O_G, "p (t n) -> p t n", NX * HALF, t=NX)
        O_U = O_G + NX * HALF
        uT = at(O_U, "p (g t) -> p g t", NG * NX * P, g=NG)
        rows = at(O_K, "p (s n) -> p s n", NT * D, s=NT)
        absl = at(O_G, "p (s n) -> p s n", 1024, s=2)
        minl = at(O_G + 1024, "p (s n) -> p s n", 1024, s=2)
        spl = at(O_G + 2048, "p (s n) -> p s n", 1024, s=2)
        rT = at(O_U, None, NT * P)[0:33]
        w_r = at(O_U + 1280, "p (k n) -> p k n", KC * RANK2, k=KC)
        w_gk = at(O_U + 1536, "p (d n) -> p d n", 2 * QK, d=2)[0:33]
        small_rows = at(O_U + 2048, None, P)[0:85]
        sq0 = at(O_U + 2176, None, D)
        boxa = at(O_HX, "p (r w) -> p r w", 2048, r=32)
        boxb = at(O_HX + 2048, "p (r w) -> p r w", 2048, r=32)
        state_in = at(O_HX + 4096, "p (t d a n) -> p t d a n", NX * HALF, t=NX, d=2, a=2)
        ktok = at(O_HX + 8192, "p (d a n) -> p d a n", HALF, d=2, a=2)
        smask = at(O_HX + 8704, "p (d n) -> p d n", 1024, d=2)
        onorm = at(O_HX + 9728, None, HALF)
        x2 = at(O_QB + 2048, "p (t n) -> p t n", NX * D, t=NX)
        assert O_QB + 2048 == 2 * EXPERT
        O_B = 2 * EXPERT + NX * D
        g1b, a2b, s2b, g2b = (at(O_B + i * D, None, D) for i in range(4))
        xres = at(O_B + 4 * D, "p (s n) -> p s n", 2 * D, s=2)
        hx2 = at(O_B + 6 * D, "p (s n) -> p s n", 2 * D, s=2)
        assert O_B + 8 * D == O_G
        sq = at(0, None, D)
        hx2T = at(D, None, D)
        cmpb = at(O_B + 4 * D, "p (b e) -> p b e", NB * NE, b=NB)
        onehot = at(O_B + 5 * D, "p (s n) -> p s n", 2 * P, s=2)
        slotv = at(O_B + 5 * D + 2 * P, "p (s w b) -> p s w b", 4 * NB, s=2, w=2)
        xg = at(O_G, "p (s n) -> p s n", 2 * D, s=2)
        xT = at(O_G + 2 * D, "p (s n) -> p s n", 2 * D, s=2)
        hsil = at(O_U, None, HALF)
        hid = at(O_U + HALF, None, HALF)
        hT = at(O_U + D, "p (k n) -> p k n", HALF, k=4)
        ysb = at(O_U + D + HALF, "p (s n) -> p s n", 2 * D, s=2)
        y1 = at(O_G, "p (s n) -> p s n", 2 * D, s=2)
        y2 = at(O_G + 2 * D, "p (s n) -> p s n", 2 * D, s=2)
        fin = at(O_B, "p (s n) -> p s n", 2 * D, s=2)
        nfb = at(O_B + 4 * D, None, D)

        ident = sb("ident", [P, P])
        mask = sb("mask", [P, 2, P])
        tri = sb("tri", [P, 2, P])
        midc = sb("midc", [P, 2])
        small = sb("small", [P, 85])
        silu_c = sb("silu_c", [P, KC, 2])
        mod = sb("mod", [P, N_MOD, KC, 2])
        a1 = sb("a1", [P, KC, 2])
        bcols = sb("bcols", [P, 4, KC])
        brows = sb("brows", [32, P])
        stat = sb("stat", [P, 4 * NT + 8])
        expo = sb("expo", [P, 4])
        dec1 = sb("dec1", [P, NT, 2, 2])
        dec2 = sb("dec2", [P, NT, 2, 2])
        dec = sb("dec", [P, NT, 2, 2])
        state = sb("state", [P, 2, 2, DV])
        ost = sb("ost", [P, 12])
        wp = sb("wp", [P, NG, P])
        icnt = sb("icnt", [P, NG, GRID_H + GRID_W])
        w_rt = sb("w_rt", [P, KC, NE])
        bias_b = sb("bias_b", [P, NE])

        ps = stack.enter_context(nc.psum_tensor("ps", [P, 8, 512], F32))

        hx_dram = nc.dram_tensor("hx_rows", [NX * P, D], F32).ap()
        y_dram = nc.dram_tensor("y_rows", [NB * P, D], F32).ap()
        b_dram = nc.dram_tensor("mod_rows", [32, P], F32).ap()

        names = """consts small_loaded small_turned small_ready silu_ready mod_used mod_added mod_ready mod_late_ready
            bcols_ready brows_turned brows_ready brows_stored bcast_loaded
            ss_ready pow_ready scaled turned hx_a hx_v
            rw_loaded gk_loaded r_done rT_ready lg_done lg_min lg_exp lg_ln sp_ready cum_done cum_read
            proj_done ev_a ev_v pool_w_loaded dec_ready zeroed
            kt_done kt_ready kv_done state_step state_saved s_chain
            sc_done sc_masked o_done osq_ready oss_ready opow_ready on_ready og_ready ot_done mixg_ready
            u_ready box_chain pooled mixp_done mixp_ready
            y_done gated x2_ready ss2_ready pow2_ready hx2_ready hx2_turned hx2T_ready logit_done sig_ready
            r_chain route_ready rank_done slots_done table_ready
            tok_ready tok_seen x_turned xT_ready xT_ready_v l1a l1b silu_a silu_b hid_a hid_b hta htb hT_a hT_b
            l2_done y_filled y_ready
            fin_add fss_ready fpow_ready fout_ready""".split()
        S = {n: sem(n) for n in names}
        row_loaded = [sem(f"row_loaded{t}") for t in range(NT)]
        ring_loaded = [sem(f"ring_loaded{i}") for i in range(RING)]
        res_loaded, hx2_stored, y_stored, fin_loaded, stored, moe_w13, moe_w2, gathered = (
            [sem(f"{n}{i}") for i in range(2)]
            for n in ("res_loaded", "hx2_stored", "y_stored", "fin_loaded", "stored", "moe_w13_", "moe_w2_", "gathered"))

        def link(eng, chain, ins):
            name, count = chain
            count[0] += 1
            ins.then_inc(S[name], 1)
            eng.wait_ge(S[name], count[0])

        wmod_v = w_mod[0].rearrange("(k p) n -> p k n", p=P)
        win_v = w_in[0].rearrange("(k p) n -> p k n", p=P)
        wout_v = w_out[0].rearrange("(k p) n -> p k n", p=P)
        units = ([("mod", j) for j in range(4)] + [("v", 0), ("qk", 0), ("g", 0), ("u", 0)]
                 + [("mod", j) for j in range(4, 12)] + [("out", 0), ("out", 1)])
        unit_no = {u: n for n, u in enumerate(units)}

        def unit_src(u):
            kind, j = u
            if kind == "mod":
                return wmod_v[:, :, j * HALF:(j + 1) * HALF]
            if kind == "out":
                return wout_v[:, :, j * HALF:(j + 1) * HALF]
            col = {"v": COL_V, "qk": COL_Q, "g": COL_G, "u": COL_U}[kind]
            return win_v[:, :, col:col + HALF]

        def unit_used(u):
            if u[0] == "mod":
                return S["mod_used"], u[1] + 1
            last = {"v": ("v", NT - 1), "qk": ("q", 1, 1), "g": ("g", NX - 1), "u": ("u", NG - 1, 1)}[u[0]]
            return S["proj_done"], group_no[last] + 1

        def unit_ready(eng, u):
            eng.wait_ge(ring_loaded[unit_no[u] % RING], 16 * (unit_no[u] // RING + 1))
            return ring[unit_no[u] % RING]

        tok_groups = [(0, 4), (4, 4), (8, 2)]
        groups = ([("v", t) for t in range(NT)] + [("k", a, g) for g in range(3) for a in range(2)]
                  + [("q", a, g) for g in range(2) for a in range(2)] + [("g", t) for t in range(NX)]
                  + [("u", p, g) for p in range(NG) for g in range(2)])
        PB = 4
        evac = {}
        na = nv = 0
        for n, g in enumerate(groups):
            on_act = g[0] == "g" or (g[0] == "v" and g[1] % 2 == 0) or (g[0] == "u")
            if on_act:
                na += 1
                evac[n] = ("ev_a", na)
            else:
                nv += 1
                evac[n] = ("ev_v", nv)
        group_no = {g: n for n, g in enumerate(groups)}

        def evacuated(g):
            s, v = evac[group_no[g]]
            return S[s], v

        def steps():
            fwd = [NX, NX + 1] + list(range(NX))
            bwd = [NX + 1, NX] + list(range(NX - 1, -1, -1))
            return list(zip(fwd, bwd))

        NTE = NX * NE
        rt = {}
        rt_at = O_U
        for n, shape in dict(s=[NX, NE], sbias=[NX, NE], hi=[32, 2], lo=[32, 2], t1=[32, 1], t2=[32, 1],
                             gm=[NX, 1], geq=[NX, NGR], goh=[NX, NGR], mb=[NX, NE], mx=[NX, 1], eq=[NX, NE],
                             oh1=[NX, NE], oh2=[NX, NE], sel=[NX, NE], pre=[NX + 1, NE], tot=[1, NE],
                             nbl=[1, NE], cb=[1, NE], cb2=[1, NE], base=[1, NE], rank=[NX, NE],
                             s12=[2, NX], ssum=[NX, 1], wk=[2, NX], dest=[2, NX],
                             blkf=[2, NX], posf=[2, NX], prior=[NX, 2 * NGR]).items():
            width = shape[0] * shape[1]
            rt[n] = at(rt_at, "p (a b) -> p a b", width, a=shape[0])
            rt_at += width
        assert rt_at <= ARENA
        cmp16 = sb("cmp16", [P, NE, KC])
        desti = sb("desti", [P, 2, NX], I32)
        blki = sb("blki", [P, 2, NX], I32)
        posi = sb("posi", [P, 2, NX], I32)
        iota_p = sb("iota_p", [P, P])
        iota_e = sb("iota_e", [P, NE])
        tokid = sb("tokid", [P, NX])
        thresh = sb("thresh", [P, KC])
        ones = sb("ones", [P, P])
        strict = sb("strict", [P, P])
        slot_tok = sb("slot_tok", [P, NB + 1], I32)
        block_tok = sb("block_tok", [P, 2], I32)
        slot_w = sb("slot_w", [P, NB])
        ebf = sb("ebf", [P, NB])
        tabs = sb("tabs", [P, 4 * NB + NE + 1], I32)
        T_E, T_PAR, T_EVEN, T_ODD, T_FIRST, T_NB = 0, NB, 2 * NB, 3 * NB, 4 * NB, 4 * NB + NE

        block = stack.enter_context(nc.Block())

        @block.sync
        def _(sp):
            sp.dma_start(small_rows[0:8, :], c.rearrange("o (k p) -> (o k) p", p=P)).then_inc(S["small_loaded"], 16)
            sp.dma_start(small_rows[8:16, :], c_ctx.rearrange("(k p) -> k p", p=P)).then_inc(S["small_loaded"], 16)
            sp.dma_start(small_rows[16:24, :], norm1.rearrange("o (k p) -> (o k) p", p=P)).then_inc(S["small_loaded"], 16)
            sp.dma_start(small_rows[24:32, :], norm2.rearrange("o (k p) -> (o k) p", p=P)).then_inc(S["small_loaded"], 16)
            sp.dma_start(small_rows[32:80, :], b_mod.rearrange("o (k p) -> (o k) p", p=P)).then_inc(S["small_loaded"], 16)
            sp.dma_start(small_rows[80:84, :], pool_scale.rearrange("o (k p) -> (o k) p", p=P)).then_inc(S["small_loaded"], 16)
            sp.dma_start(small_rows[84:85, :], gla_gain).then_inc(S["small_loaded"], 16)
            for n, u in enumerate(units):
                if n >= RING:
                    sp.wait_ge(*unit_used(units[n - RING]))
                sp.dma_start(ring[n % RING], unit_src(u)).then_inc(ring_loaded[n % RING], 16)

            def load_expert(e, par):
                at_half = (1 - par) * EXPERT
                for i, w in enumerate((w1, w3)):
                    sp.dma_start(at(at_half + i * UNIT, "p (k n) -> p k n", UNIT, k=KC),
                                 w[0, bass.ds(e, 1)].rearrange("o (k p) n -> p (o k) n", p=P)).then_inc(moe_w13[par], 16)
                sp.dma_start(at(at_half + 2 * UNIT, "p (k n) -> p k n", UNIT, k=4),
                             w2[0, bass.ds(e, 1)].rearrange("o (k p) n -> p (o k) n", p=P)).then_inc(moe_w2[par], 16)

            for par in range(2):
                sp.sem_inc(moe_w13[par], 32)
                sp.sem_inc(moe_w2[par], 16)
            sp.wait_ge(S["ot_done"], NX)
            sp.wait_ge(S["mixp_done"], 2 * NG)
            load_expert(0, 0)
            for t in range(NX):
                sp.wait_ge(S["hx2_ready"], t + 1)
                sp.dma_start(hx_dram[t * P:(t + 1) * P, :], hx2[:, t % 2, :]).then_inc(hx2_stored[t % 2], 16)
            sp.wait_ge(S["logit_done"], NX)
            load_expert(1, 1)
            sp.wait_ge(S["table_ready"], 1)
            with sp.Fori(1, NE // 2) as pair:
                for par in range(2):
                    e = pair * 2 + par
                    first = sp.value_load(tabs[0:1, bass.ds(e + (T_FIRST - 1), 1)], min_val=1, max_val=MAXB)
                    sp.wait_ge(S["l2_done"], first)
                    load_expert(e, par)
            for t in range(NX):
                sp.wait_ge(S["fout_ready"], t + 1)
                sp.dma_start(out[0, t * P:(t + 1) * P, :], fin[:, t % 2, :]).then_inc(stored[t % 2], 16)
            for par in range(2):
                sp.wait_ge(stored[par], 16 * NX // 2)

        @block.gpsimd
        def _(pool):
            cc = ("consts", [0])
            link(pool, cc, pool.memset(ident[:, :], 0.0))
            link(pool, cc, pool.memset(mask[:, :, :], 1.0))
            link(pool, cc, pool.memset(tri[:, :, :], -1.0 / GATE_NORM))
            link(pool, cc, pool.memset(midc[:, :], 0.0))
            link(pool, cc, pool.memset(ones[:, :], 1.0))
            link(pool, cc, pool.memset(strict[:, :], 1.0))
            link(pool, cc, pool.memset(expo[:, :], -0.5))
            link(pool, cc, pool.memset(rT[32:33, :], 1.0))
            link(pool, cc, pool.memset(w_gk[0:32, :, :], 0.0))
            link(pool, cc, pool.iota(iota_p[:, :], pattern=[[1, P]], base=0, channel_multiplier=0,
                      allow_small_or_imprecise_dtypes=True))
            link(pool, cc, pool.iota(iota_e[:, :], pattern=[[-1, NE]], base=NE, channel_multiplier=0,
                      allow_small_or_imprecise_dtypes=True))
            link(pool, cc, pool.iota(tokid[:, :], pattern=[[P, NX]], base=0, channel_multiplier=1,
                      allow_small_or_imprecise_dtypes=True))
            link(pool, cc, pool.iota(thresh[:, :], pattern=[[P, KC]], base=0, channel_multiplier=0,
                      allow_small_or_imprecise_dtypes=True))
            link(pool, cc, pool.affine_select(out=ident[:, :], in_=ident[:, :], compare_op=ALU.not_equal, fill=1.0, base=0,
                               pattern=[[-1, P]], channel_multiplier=1))
            for m in (mask, tri):
                link(pool, cc, pool.affine_select(out=m[:, 0, :], in_=m[:, 0, :], compare_op=ALU.is_ge, fill=0.0, base=0,
                                   pattern=[[1, P]], channel_multiplier=-1))
                link(pool, cc, pool.affine_select(out=m[:, 1, :], in_=m[:, 1, :], compare_op=ALU.is_ge, fill=0.0, base=0,
                                   pattern=[[-1, P]], channel_multiplier=1))
            link(pool, cc, pool.affine_select(out=strict[:, :], in_=strict[:, :], compare_op=ALU.is_gt, fill=0.0, base=0,
                               pattern=[[1, P]], channel_multiplier=-1))
            link(pool, cc, pool.memset(midc[0:MID, 0:1], -1.0 / GATE_NORM))
            link(pool, cc, pool.memset(midc[MID:P, 1:2], -1.0 / GATE_NORM))
            for d in range(2):
                link(pool, cc, pool.tensor_scalar(tri[:, d, :], tri[:, d, :], midc[:, d:d + 1], None, ALU.subtract))
            for d in range(2):
                pool.dma_start(w_gk[16 * d:16 * d + 16, d, :], w_gk2[0, d]).then_inc(S["gk_loaded"], 16)
            pool.dma_start(w_gk[32:33, :, :], b_gk).then_inc(S["gk_loaded"], 16)
            pool.dma_start(w_r[:, :, :], win_v[:, :, COL_R:COL_R + RANK2]).then_inc(S["rw_loaded"], 16)
            pool.dma_start(wp[:, :, :], w_pool[0].rearrange("g c n -> c g n")).then_inc(S["pool_w_loaded"], 16)
            pool.dma_start(icnt[:, :, :].rearrange("p g n -> p (g n)"),
                           inv_counts.partition_broadcast(P)).then_inc(S["pool_w_loaded"], 16)
            pool.dma_start(w_rt[:, :, :], w_router.rearrange("(k p) e -> p k e", p=P)).then_inc(S["pool_w_loaded"], 16)
            pool.dma_start(bias_b[:, :], router_bias.rearrange("(o e) -> o e", o=1).partition_broadcast(P))\
                .then_inc(S["pool_w_loaded"], 16)
            pool.memset(qbd[0:DK, :, :, :, 1, :].rearrange("p t d a i -> p (t d a) i"), 0.0).then_inc(S["zeroed"], 1)
            pool.wait_ge(S["zeroed"], 1)
            pool.memset(qbd[DK:P, :, :, :, 0, :].rearrange("p t d a i -> p (t d a) i"), 0.0).then_inc(S["zeroed"], 1)
            pool.wait_ge(S["zeroed"], 2)
            for t in range(NT):
                pool.wait_ge(S["ss_ready"], t + 1)
                pool.tensor_scalar(stat[:, NT + t:NT + t + 1], stat[:, t:t + 1], 1.0 / D, EPS, ALU.mult, ALU.add)\
                    .then_inc(S["box_chain"], 1)
                pool.wait_ge(S["box_chain"], t + 1)
                pool.tensor_tensor(stat[:, 2 * NT + t:2 * NT + t + 1], stat[:, NT + t:NT + t + 1], expo[:, 0:1], ALU.pow)\
                    .then_inc(S["pow_ready"], 1)
                pool.wait_ge(S["pow_ready"], t + 1)
            bc = ("box_chain", [NT])
            pool.wait_ge(S["pool_w_loaded"], 64)
            for g, w in enumerate(WINDOWS):
                h = w // 2
                pool.wait_ge(*evacuated(("u", g, 1)))
                if g == 0:
                    pool.wait_ge(*evacuated(("u", NG - 1, 1)))
                link(pool, bc, pool.memset(boxa[:, :, :], 0.0))
                link(pool, bc, pool.tensor_copy(boxa[:, 8:8 + GRID_H, :], uT[:, g, :].rearrange("p (r w) -> p r w", w=GRID_W)))
                src, dst, L = boxa, boxb, 2
                while L <= w:
                    lo, n = 8 - h, GRID_H + w - L
                    link(pool, bc, pool.tensor_tensor(dst[:, lo:lo + n, :], src[:, lo:lo + n, :],
                                                      src[:, lo + L // 2:lo + L // 2 + n, :], ALU.add))
                    src, dst, L = dst, src, 2 * L
                wide = dst.rearrange("p r w -> p (r w)")[:, 0:GRID_H * 80].rearrange("p (r w) -> p r w", w=80)
                link(pool, bc, pool.memset(wide, 0.0))
                link(pool, bc, pool.tensor_tensor(
                    wide[:, :, 8:8 + GRID_W], src[:, 8 - h:8 - h + GRID_H, :],
                    icnt[:, g, 0:GRID_H].unsqueeze(2).broadcast_to([P, GRID_H, GRID_W]), ALU.mult))
                src_full = src.rearrange("p r w -> p (r w)")[:, 0:GRID_H * 80].rearrange("p (r w) -> p r w", w=80)
                src, dst, L = wide, src_full, 2
                while L <= w:
                    lo, n = 8 - h, GRID_W + w - L
                    link(pool, bc, pool.tensor_tensor(dst[:, :, lo:lo + n], src[:, :, lo:lo + n],
                                                      src[:, :, lo + L // 2:lo + L // 2 + n], ALU.add))
                    src, dst, L = dst, src, 2 * L
                link(pool, bc, pool.tensor_tensor(
                    dst[:, :, 0:GRID_W], src[:, :, 8 - h:8 - h + GRID_W],
                    icnt[:, g, GRID_H:].unsqueeze(1).broadcast_to([P, GRID_H, GRID_W]), ALU.mult))
                ug = uT[:, g, :].rearrange("p (r w) -> p r w", w=GRID_W)
                bc[1][0] += 1
                pool.tensor_tensor(ug, dst[:, :, 0:GRID_W], ug, ALU.subtract).then_inc(S["pooled"], 1)
                bc[1][0] -= 1
                pool.wait_ge(S["pooled"], g + 1)
            for t in range(NX):
                pool.wait_ge(S["oss_ready"], t + 1)
                link(pool, bc, pool.tensor_scalar(ost[:, 4:8], ost[:, 0:4], 1.0 / DV, EPS, ALU.mult, ALU.add))
                pool.tensor_tensor(ost[:, 8:12], ost[:, 4:8], expo[:, 0:4], ALU.pow).then_inc(S["opow_ready"], 1)
                pool.wait_ge(S["opow_ready"], t + 1)
            for t in range(NX):
                pool.wait_ge(S["ss2_ready"], t + 1)
                link(pool, bc, pool.tensor_scalar(stat[:, NT + t:NT + t + 1], stat[:, t:t + 1], 1.0 / D, EPS, ALU.mult, ALU.add))
                pool.tensor_tensor(stat[:, 2 * NT + t:2 * NT + t + 1], stat[:, NT + t:NT + t + 1], expo[:, 0:1], ALU.pow)\
                    .then_inc(S["pow2_ready"], 1)
                pool.wait_ge(S["pow2_ready"], t + 1)
            pool.wait_ge(S["table_ready"], 1)
            for par in range(2):
                pool.wait_ge(hx2_stored[par], 16 * NX // 2)
            nb = pool.value_load(tabs[0:1, T_NB:T_NB + 1], min_val=1, max_val=MAXB)

            def gather(b, slot):
                pool.wait_ge(S["x_turned"], b + 1)
                pool.tensor_copy(block_tok[:, slot:slot + 1], slot_tok[:, bass.ds(b, 1)]).then_inc(S["tok_ready"], 1)
                pool.wait_ge(S["tok_ready"], b + 1)
                pool.sem_inc(S["tok_seen"], 1)
                pool.indirect_dma_start(out=xg[:, slot, :], out_offset=None, in_=hx_dram,
                                        in_offset=bass.IndirectOffsetOnAxis(ap=block_tok[:, slot:slot + 1], axis=0))\
                    .then_inc(gathered[slot], 16)

            gather(0, 0)
            with pool.Fori(0, NB // 2) as pair:
                i = pair * 2
                for s in range(2):
                    with pool.If(i + s < nb):
                        gather(i + (s + 1), 1 - s)
            for par in range(2):
                pool.wait_ge(y_stored[par], 16 * NB // 2 + 16)
            for t in range(NX):
                if t >= 2:
                    pool.wait_ge(S["fin_add"], 2 * (t - 1))
                for k, buf in enumerate((y1, y2)):
                    pool.indirect_dma_start(out=buf[:, t % 2, :], out_offset=None, in_=y_dram,
                                            in_offset=bass.IndirectOffsetOnAxis(ap=desti[:, k, t:t + 1], axis=0))\
                        .then_inc(fin_loaded[t % 2], 16)
                if t >= 1:
                    pool.wait_ge(S["fss_ready"], t)
                    link(pool, bc, pool.tensor_scalar(stat[:, NT + t - 1:NT + t], stat[:, t - 1:t], 1.0 / D, EPS, ALU.mult, ALU.add))
                    pool.tensor_tensor(stat[:, 2 * NT + t - 1:2 * NT + t], stat[:, NT + t - 1:NT + t], expo[:, 0:1], ALU.pow)\
                        .then_inc(S["fpow_ready"], 1)
                    pool.wait_ge(S["fpow_ready"], t)
            t = NX
            pool.wait_ge(S["fss_ready"], t)
            link(pool, bc, pool.tensor_scalar(stat[:, NT + t - 1:NT + t], stat[:, t - 1:t], 1.0 / D, EPS, ALU.mult, ALU.add))
            pool.tensor_tensor(stat[:, 2 * NT + t - 1:2 * NT + t], stat[:, NT + t - 1:NT + t], expo[:, 0:1], ALU.pow)\
                .then_inc(S["fpow_ready"], 1)

        @block.scalar
        def _(act):
            def row_src(t):
                return x[0, t * P:(t + 1) * P, :] if t < NX else ctx_in[0, (t - NX) * P:(t - NX + 1) * P, :]

            for t in range(NT):
                act.dma_start(rows[:, t, :], row_src(t)).then_inc(row_loaded[t], 16)
            act.wait_ge(S["small_ready"], 1)
            act.activation(silu_c[:, :, :], small[:, 0:16].rearrange("p (w k) -> p k w", w=2), ACT.Silu)\
                .then_inc(S["silu_ready"], 1)
            for t in range(NT):
                act.wait_ge(row_loaded[t], 16)
                act.activation(sq0, rows[:, t, :], ACT.Square, accum_out=stat[:, t:t + 1])\
                    .then_inc(S["ss_ready"], 1)
                act.wait_ge(S["ss_ready"], t + 1)
            act.wait_ge(S["mod_ready"], 2)
            for t in range(NT):
                which = 0 if t < NX else 1
                act.wait_ge(S["turned"], t + 1)
                for k in range(4, KC):
                    ins = act.activation(hxT[:, k, t * P:(t + 1) * P], ps[:, 2 * (t % 2) + 1, (k - 4) * P:(k - 3) * P],
                                         ACT.Identity, bias=mod[:, 0, k, which:which + 1], scale=a1[:, k, which:which + 1])
                ins.then_inc(S["hx_a"], 1)

            def ev(n):
                act.wait_ge(S["proj_done"], n + 1)

            def decays(t):
                act.wait_ge(S["lg_min"], 2 * (t + 1))
                act.activation(absl[:, t % 2, :], absl[:, t % 2, :], ACT.Exp, scale=-1.0).then_inc(S["lg_exp"], 1)
                act.wait_ge(S["lg_exp"], t + 1)
                act.activation(absl[:, t % 2, :], absl[:, t % 2, :], ACT.Ln, bias=1.0).then_inc(S["lg_ln"], 1)

            def decay_exp(t):
                act.wait_ge(S["cum_done"], t + 1)
                cum = ps[:, 5, :].rearrange("p (d a i) -> p d a i", d=2, a=2)
                if t < NX:
                    act.activation(qbd[0:DK, t, :, :, 0, :].rearrange("p d a i -> p (d a) i"), ps[0:DK, 5, :].rearrange("p (c i) -> p c i", i=P), ACT.Exp)
                    act.activation(qbd[DK:P, t, :, :, 1, :].rearrange("p d a i -> p (d a) i"), ps[DK:P, 5, :].rearrange("p (c i) -> p c i", i=P), ACT.Exp)
                act.activation(kdec[:, t].rearrange("p d a i -> p (d a i)"), ps[:, 5, :], ACT.Exp, scale=-1.0)
                act.activation(dec2[:, t, 0, :], cum[:, 0, :, P - 1], ACT.Exp)
                act.activation(dec2[:, t, 1, :], cum[:, 1, :, 0], ACT.Exp)
                act.activation(dec1[:, t].rearrange("p d a -> p (d a)"), ps[:, 6, 256:260], ACT.Exp)\
                    .then_inc(S["cum_read"], 1)

            act.wait_ge(S["zeroed"], 2)
            for t in range(NT + 2):
                if t < NT:
                    decays(t)
                if t >= 1 and t - 1 < NT:
                    decay_exp(t - 1)
                for n, g in enumerate(groups):
                    if g == ("v", t) and t % 2 == 0:
                        ev(n)
                        if t == 0:
                            act.wait_ge(S["turned"], NT)
                        act.activation(vals[:, t, :], ps[:, n % PB, :], ACT.Copy).then_inc(S["ev_a"], 1)
            for n, g in enumerate(groups):
                if g[0] == "g":
                    ev(n)
                    if g[1] == 0:
                        act.wait_ge(S["sp_ready"], NT)
                        act.wait_ge(S["cum_done"], NT)
                    act.activation(gate[:, g[1], :], ps[:, n % PB, :], ACT.Silu).then_inc(S["ev_a"], 1)
                if g[0] == "u":
                    ev(n)
                    act.activation(uT[:, g[1], g[2] * HALF:(g[2] + 1) * HALF], ps[:, n % PB, :], ACT.Copy)\
                        .then_inc(S["ev_a"], 1)
            for n in range(NT):
                act.wait_ge(S["kt_done"], n + 1)
                if n >= 1:
                    act.wait_ge(S["kv_done"], n)
                act.activation(ktok.rearrange("p d a n -> p (d a n)"), ps[:, 4, :], ACT.Copy).then_inc(S["kt_ready"], 1)
            for t in range(NX):
                act.wait_ge(S["o_done"], t + 1)
                if t >= 1:
                    act.wait_ge(S["oss_ready"], t)
                act.activation(sq[:, 0:HALF], ps[:, 2, :], ACT.Square).then_inc(S["osq_ready"], 1)
                act.wait_ge(S["ot_done"], t + 1)
                act.activation(gate[:, t, :], ps[:, 3, :], ACT.Copy, scale=small[:, 84:85]).then_inc(S["mixg_ready"], 1)
            for g in range(NG):
                for h in range(2):
                    act.wait_ge(S["mixp_done"], 2 * g + h + 1)
                    act.activation(uT[:, g, h * HALF:(h + 1) * HALF], ps[:, 4 + h, :], ACT.Copy,
                                   scale=small[:, 80 + g:81 + g]).then_inc(S["mixp_ready"], 1)
            act.wait_ge(S["brows_ready"], 1)
            act.dma_start(b_dram, brows[:, :]).then_inc(S["brows_stored"], 16)
            act.wait_ge(S["brows_stored"], 16)
            act.wait_ge(S["sc_done"], 2 * NX)
            act.wait_ge(S["o_done"], NX)
            for i, dst in enumerate((g1b, a2b, s2b, g2b)):
                act.dma_start(dst, b_dram[8 * i:8 * i + 8, :].rearrange("(o k) p -> o (k p)", o=1).partition_broadcast(P))\
                    .then_inc(S["bcast_loaded"], 16)
            for t in range(2):
                act.dma_start(xres[:, t, :], row_src(t)).then_inc(res_loaded[t % 2], 16)
            for t in range(NX):
                act.wait_ge(S["x2_ready"], 2 * (t + 1))
                if t + 2 < NX:
                    act.dma_start(xres[:, t % 2, :], row_src(t + 2)).then_inc(res_loaded[t % 2], 16)
                if t >= 1:
                    act.wait_ge(S["ss2_ready"], t)
                act.activation(sq[:, :], x2[:, t, :], ACT.Square, accum_out=stat[:, t:t + 1]).then_inc(S["ss2_ready"], 1)
                for blk in (NE + t, NE + NX + t):
                    act.dma_start(y_dram[blk * P:(blk + 1) * P, :], x2[:, t, :]).then_inc(S["y_filled"], 16)
                act.wait_ge(S["hx2_turned"], t + 1)
                if t >= 1:
                    act.wait_ge(S["logit_done"], t)
                for h in range(2):
                    act.activation(hx2T[:, h * HALF:(h + 1) * HALF], ps[:, 4 + h, :], ACT.Copy).then_inc(S["hx2T_ready"], 1)
            act.wait_ge(S["logit_done"], NX)
            act.activation(rt["s"].rearrange("p t e -> p (t e)"), ps[:, 6, 0:NTE], ACT.Sigmoid).then_inc(S["sig_ready"], 1)
            act.wait_ge(S["table_ready"], 1)
            nb = act.value_load(tabs[0:1, T_NB:T_NB + 1], min_val=1, max_val=MAXB)

            def turn_out(b, slot):
                act.wait_ge(S["x_turned"], b + 3)
                act.activation(xT[:, slot, HALF:D], ps[:, 1, :], ACT.Copy).then_inc(S["xT_ready"], 1)

            turn_out(0, 0)
            act.wait_ge(S["y_filled"], 16 * 2 * NX)
            for par in range(2):
                act.sem_inc(y_stored[par], 16)
            with act.Fori(0, NB // 2) as pair:
                i = pair * 2
                for s in range(2):
                    with act.If(i + s < nb):
                        b = i + s
                        act.wait_ge(S["l1a"], b + 1)
                        act.activation(hsil[:, 0:256], ps[:, 2, 0:256], ACT.Silu).then_inc(S["silu_a"], 1)
                        turn_out(b + 1, 1 - s)
                        act.wait_ge(S["hta"], b + 1)
                        act.activation(hT[:, 0:2, :].rearrange("p k n -> p (k n)"), ps[:, 2, 0:256], ACT.Copy).then_inc(S["hT_a"], 1)
                        act.wait_ge(S["l1b"], b + 1)
                        act.activation(hsil[:, 256:512], ps[:, 4, 0:256], ACT.Silu).then_inc(S["silu_b"], 1)
                        act.wait_ge(S["htb"], b + 1)
                        act.activation(hT[:, 2:4, :].rearrange("p k n -> p (k n)"), ps[:, 4, 0:256], ACT.Copy).then_inc(S["hT_b"], 1)
                        act.wait_ge(S["y_ready"], 2 * i + (2 * s + 4))
                        act.dma_start(y_dram[bass.ds(b * P, P), :], ysb[:, s, :]).then_inc(y_stored[s], 16)
                    with act.Else():
                        act.sem_inc(y_stored[s], 16)
            for par in range(2):
                act.wait_ge(y_stored[par], 16 * NB // 2 + 16)
            act.dma_start(nfb, norm_f.rearrange("(o n) -> o n", o=1).partition_broadcast(P)).then_inc(S["bcast_loaded"], 16)
            for t in range(NX):
                act.wait_ge(S["fin_add"], 2 * (t + 1))
                if t >= 1:
                    act.wait_ge(S["fss_ready"], t)
                act.activation(sq[:, :], x2[:, t, :], ACT.Square, accum_out=stat[:, t:t + 1]).then_inc(S["fss_ready"], 1)

        @block.vector
        def _(dve):
            dve.wait_ge(S["small_turned"], 1)
            dve.tensor_copy(small[:, :], ps[:, 7, 0:85]).then_inc(S["small_ready"], 1)
            for t in range(NT):
                dve.wait_ge(S["pow_ready"], t + 1)
                dve.tensor_scalar(rows[:, t, :], rows[:, t, :], stat[:, 2 * NT + t:2 * NT + t + 1], None, ALU.mult)\
                    .then_inc(S["scaled"], 1)
            dve.wait_ge(S["mod_used"], 4)
            b_cols = small[:, 32:80].rearrange("p (s k) -> p s k", s=N_MOD)
            for w in range(2):
                dve.tensor_tensor(mod[:, 0:2, :, w], ps[:, 6, 0:32].rearrange("p (s k w) -> p s k w", s=2, w=2)[:, :, :, w],
                                  b_cols[:, 0:2, :], ALU.add).then_inc(S["mod_added"], 1)
            dve.wait_ge(S["mod_added"], 2)
            for w in range(2):
                dve.scalar_tensor_tensor(out=a1[:, :, w], in0=mod[:, 1, :, w], scalar=1.0, in1=small[:, 16:24],
                                         op0=ALU.add, op1=ALU.mult).then_inc(S["mod_ready"], 1)
            dve.wait_ge(S["mod_ready"], 2)
            for t in range(NT):
                which = 0 if t < NX else 1
                dve.wait_ge(S["turned"], t + 1)
                for k in range(4):
                    ins = dve.tensor_scalar(hxT[:, k, t * P:(t + 1) * P], ps[:, 2 * (t % 2), k * P:(k + 1) * P],
                                            a1[:, k, which:which + 1], mod[:, 0, k, which:which + 1], ALU.mult, ALU.add)
                ins.then_inc(S["hx_v"], 1)
            for g, (t0, n) in enumerate(tok_groups):
                dve.wait_ge(S["r_done"], g + 1)
                dve.tensor_copy(rT[0:32, t0 * P:(t0 + n) * P], ps[0:32, g, 0:n * P]).then_inc(S["rT_ready"], 1)
            sc = ("s_chain", [0])
            for t in range(NT + 1):
                if t < NT:
                    dve.wait_ge(S["lg_done"], t + 1)
                    dve.tensor_scalar(minl[:, t % 2, :], ps[:, 4, :], 0.0, None, ALU.min).then_inc(S["lg_min"], 1)
                    dve.wait_ge(S["lg_min"], 2 * t + 1)
                    dve.scalar_tensor_tensor(out=absl[:, t % 2, :], in0=minl[:, t % 2, :], scalar=-2.0, in1=ps[:, 4, :],
                                             op0=ALU.mult, op1=ALU.add).then_inc(S["lg_min"], 1)
                    dve.wait_ge(S["lg_ln"], t + 1)
                    if t >= 2:
                        dve.wait_ge(S["cum_done"], t - 1)
                    dve.tensor_tensor(spl[:, t % 2, :], absl[:, t % 2, :], minl[:, t % 2, :], ALU.subtract).then_inc(S["sp_ready"], 1)
                    if t % 2 == 1:
                        n = group_no[("v", t)]
                        dve.wait_ge(S["proj_done"], n + 1)
                        dve.tensor_copy(vals[:, t, :], ps[:, n % PB, :]).then_inc(S["ev_v"], 1)
            dve.wait_ge(S["cum_read"], NT)
            for n, g in enumerate(groups):
                if g[0] == "k":
                    a, gr = g[1], g[2]
                    t0, m = tok_groups[gr]
                    dve.wait_ge(S["proj_done"], n + 1)
                    for d in range(2):
                        kd = kdec[:, t0:t0 + m, d, a, :]
                        ins = dve.tensor_tensor(kd, ps[:, n % PB, 0:m * P].rearrange("p (t i) -> p t i", i=P), kd, ALU.mult)
                    ins.then_inc(S["ev_v"], 1)
                if g[0] == "q":
                    a, gr = g[1], g[2]
                    t0, m = tok_groups[gr]
                    dve.wait_ge(S["proj_done"], n + 1)
                    for d in range(2):
                        for h in range(2):
                            qd = qbd[DK * h:DK * h + DK, t0:t0 + m, d, a, h, :]
                            ins = dve.scalar_tensor_tensor(out=qd, in0=ps[DK * h:DK * h + DK, n % PB, 0:m * P].rearrange("p (t i) -> p t i", i=P),
                                                           scalar=DK ** -0.5, in1=qd, op0=ALU.mult, op1=ALU.mult)
                    ins.then_inc(S["ev_v"], 1)
            dve.tensor_tensor(dec[:, :, :, :].rearrange("p t d a -> p (t d a)"), dec1[:, :, :, :].rearrange("p t d a -> p (t d a)"),
                              dec2[:, :, :, :].rearrange("p t d a -> p (t d a)"), ALU.mult).then_inc(S["dec_ready"], 1)
            dve.wait_ge(S["dec_ready"], 1)
            dve.wait_ge(S["mod_used"], 12)
            for w in range(2):
                ins = dve.tensor_tensor(mod[:, 2:6, :, w], ps[:, 7, 0:64].rearrange("p (s k w) -> p s k w", s=4, w=2)[:, :, :, w],
                                        b_cols[:, 2:6, :], ALU.add)
            ins.then_inc(S["mod_late_ready"], 1)
            dve.wait_ge(S["mod_late_ready"], 1)
            dve.tensor_copy(bcols[:, 0, :], mod[:, 2, :, 0]).then_inc(S["bcols_ready"], 1)
            dve.scalar_tensor_tensor(out=bcols[:, 1, :], in0=mod[:, 4, :, 0], scalar=1.0, in1=small[:, 24:32],
                                     op0=ALU.add, op1=ALU.mult).then_inc(S["bcols_ready"], 1)
            dve.tensor_copy(bcols[:, 2, :], mod[:, 3, :, 0]).then_inc(S["bcols_ready"], 1)
            dve.tensor_copy(bcols[:, 3, :], mod[:, 5, :, 0]).then_inc(S["bcols_ready"], 1)
            dve.wait_ge(S["brows_turned"], 1)
            dve.tensor_copy(brows[:, :], ps[0:32, 6, 384:512]).then_inc(S["brows_ready"], 1)
            dve.wait_ge(*evacuated(("u", NG - 1, 1)))
            for n, tt in enumerate(steps()):
                dve.wait_ge(S["kv_done"], n + 1)
                if n >= 1:
                    dve.wait_ge(S["state_step"], n)
                for d in range(2):
                    t = tt[d]
                    for a in range(2):
                        kv = ps[:, 5, (2 * d + a) * P:(2 * d + a + 1) * P]
                        if n >= NCT:
                            dve.tensor_scalar(state_in[:, t, d, a, :], state[:, d, a, :], dec1[:, t, d, a:a + 1], None, ALU.mult)\
                                .then_inc(S["state_saved"], 1)
                        if n >= 1:
                            link(dve, sc, dve.tensor_scalar(state[:, d, a, :], state[:, d, a, :], dec[:, t, d, a:a + 1], None, ALU.mult))
                            ins = dve.scalar_tensor_tensor(out=state[:, d, a, :], in0=kv, scalar=dec2[:, t, d, a:a + 1],
                                                           in1=state[:, d, a, :], op0=ALU.mult, op1=ALU.add)
                        else:
                            ins = dve.tensor_scalar(state[:, d, a, :], kv, dec2[:, t, d, a:a + 1], None, ALU.mult)
                ins.then_inc(S["state_step"], 1)
            for t in range(NX):
                for d in range(2):
                    dve.wait_ge(S["sc_done"], 2 * t + d + 1)
                    dve.tensor_tensor(smask[:, d, :].rearrange("p (h i) -> p h i", i=P), ps[:, d, :].rearrange("p (h i) -> p h i", i=P),
                                      mask[:, d, :].unsqueeze(1).broadcast_to([P, HEADS, P]), ALU.mult).then_inc(S["sc_masked"], 1)
                dve.wait_ge(S["osq_ready"], t + 1)
                dve.tensor_reduce(ost[:, 0:4], sq[:, 0:HALF].rearrange("p (h n) -> p h n", h=HEADS), AX.X, ALU.add).then_inc(S["oss_ready"], 1)
                dve.wait_ge(S["opow_ready"], t + 1)
                if t >= 1:
                    dve.wait_ge(S["ot_done"], t)
                dve.tensor_tensor(onorm.rearrange("p (h n) -> p h n", h=HEADS), ps[:, 2, :].rearrange("p (h n) -> p h n", h=HEADS),
                                  ost[:, 8:12].unsqueeze(2).broadcast_to([P, HEADS, DV]), ALU.mult).then_inc(S["on_ready"], 1)
                dve.wait_ge(S["on_ready"], t + 1)
                dve.tensor_tensor(onorm, onorm, gate[:, t, :], ALU.mult).then_inc(S["og_ready"], 1)
            dve.wait_ge(S["bcast_loaded"], 64)
            for t in range(NX):
                dve.wait_ge(res_loaded[t % 2], 16 * (t // 2 + 1))
                for h in range(2):
                    cols = slice(h * HALF, (h + 1) * HALF)
                    dve.wait_ge(S["y_done"], 2 * t + h + 1)
                    dve.tensor_tensor(x2[:, t, cols], ps[:, 2 * (t % 2) + h, :], g1b[:, cols], ALU.mult).then_inc(S["gated"], 1)
                for h in range(2):
                    cols = slice(h * HALF, (h + 1) * HALF)
                    dve.wait_ge(S["gated"], 2 * t + h + 1)
                    dve.tensor_tensor(x2[:, t, cols], x2[:, t, cols], xres[:, t % 2, cols], ALU.add).then_inc(S["x2_ready"], 1)
                dve.wait_ge(S["pow2_ready"], t + 1)
                if t >= 2:
                    dve.wait_ge(hx2_stored[t % 2], 16 * (t // 2))
                    dve.wait_ge(S["hx2_turned"], t - 1)
                link(dve, sc, dve.scalar_tensor_tensor(out=hx2[:, t % 2, :], in0=x2[:, t, :], scalar=stat[:, 2 * NT + t:2 * NT + t + 1],
                                                       in1=a2b, op0=ALU.mult, op1=ALU.mult))
                dve.tensor_tensor(hx2[:, t % 2, :], hx2[:, t % 2, :], s2b, ALU.add).then_inc(S["hx2_ready"], 1)
            rc = ("r_chain", [0])
            v = lambda ins: link(dve, rc, ins)
            R = rt
            dve.wait_ge(S["sig_ready"], 1)
            v(dve.tensor_tensor(R["sbias"], R["s"], bias_b[:, :].unsqueeze(1).broadcast_to([P, NX, NE]), ALU.add))
            G = R["sbias"].rearrange("p t (g j) -> p (t g) j", j=4)
            v(dve.tensor_tensor(R["hi"], G[:, :, 0:2], G[:, :, 2:4], ALU.max))
            v(dve.tensor_tensor(R["lo"], G[:, :, 0:2], G[:, :, 2:4], ALU.min))
            v(dve.tensor_tensor(R["t1"], R["hi"][:, :, 0:1], R["hi"][:, :, 1:2], ALU.max))
            v(dve.tensor_tensor(R["t2"], R["hi"][:, :, 0:1], R["hi"][:, :, 1:2], ALU.min))
            v(dve.tensor_tensor(R["hi"][:, :, 0:1], R["lo"][:, :, 0:1], R["lo"][:, :, 1:2], ALU.max))
            v(dve.tensor_tensor(R["t2"], R["t2"], R["hi"][:, :, 0:1], ALU.max))
            v(dve.tensor_tensor(R["t1"], R["t1"], R["t2"], ALU.add))
            gsc = R["t1"].rearrange("p (t g) o -> p t (g o)", g=NGR)

            def first_best(oh, values, eq, weights, shape):
                v(dve.tensor_reduce(R["mx"], values, AX.X, ALU.max))
                v(dve.tensor_tensor(eq, values, R["mx"].broadcast_to(shape), ALU.is_equal))
                v(dve.tensor_tensor(eq, eq, weights.unsqueeze(1).broadcast_to(shape), ALU.mult))
                v(dve.tensor_reduce(R["mx"], eq, AX.X, ALU.max))
                v(dve.tensor_tensor(oh, eq, R["mx"].broadcast_to(shape), ALU.is_equal))

            first_best(R["goh"], gsc, R["geq"], iota_e[:, NE - NGR:NE], [P, NX, NGR])
            mb4 = R["mb"].rearrange("p t (g j) -> p (t g) j", j=4)
            goh = R["goh"].rearrange("p t g -> p (t g)").unsqueeze(2).broadcast_to([P, NX * NGR, 4])
            v(dve.tensor_tensor(mb4, G, goh, ALU.mult))
            v(dve.tensor_scalar(R["goh"], R["goh"], BIG, -BIG, ALU.mult, ALU.add))
            v(dve.tensor_tensor(mb4, mb4, goh, ALU.add))
            first_best(R["oh1"], R["mb"], R["eq"], iota_e[:, :], [P, NX, NE])
            v(dve.scalar_tensor_tensor(out=R["mb"], in0=R["oh1"], scalar=-BIG, in1=R["mb"], op0=ALU.mult, op1=ALU.add))
            first_best(R["oh2"], R["mb"], R["eq"], iota_e[:, :], [P, NX, NE])
            v(dve.tensor_tensor(R["sel"], R["oh1"], R["oh2"], ALU.add))
            v(dve.memset(R["pre"][:, 0, :], 0.0))
            for t in range(NX):
                v(dve.tensor_tensor(R["pre"][:, t + 1, :], R["pre"][:, t, :], R["sel"][:, t, :], ALU.add))
            dve.sem_inc(S["route_ready"], 1)
            for k, oh in enumerate(("oh1", "oh2")):
                v(dve.tensor_tensor(R["eq"], R["s"], R[oh], ALU.mult))
                v(dve.tensor_reduce(R["s12"][:, k, :], R["eq"], AX.X, ALU.add))
            v(dve.tensor_tensor(R["ssum"].rearrange("p t o -> p (t o)"), R["s12"][:, 0, :], R["s12"][:, 1, :], ALU.add))
            v(dve.reciprocal(R["ssum"], R["ssum"]))
            v(dve.tensor_tensor(R["wk"], R["s12"], R["ssum"].rearrange("p t o -> p (o t)").unsqueeze(1).broadcast_to([P, 2, NX]), ALU.mult))
            dve.wait_ge(S["rank_done"], 1)
            v(dve.tensor_copy(R["rank"].rearrange("p t e -> p (t e)"), ps[:, 7, 0:NTE]))
            v(dve.tensor_copy(R["tot"].rearrange("p o e -> p (o e)"), ps[:, 7, NTE:NTE + NE]))
            v(dve.tensor_tensor(cmp16[:, :, :], R["tot"].rearrange("p o e -> p (o e)").unsqueeze(2).broadcast_to([P, NE, KC]),
                                thresh[:, :].unsqueeze(1).broadcast_to([P, NE, KC]), ALU.is_gt))
            nbl = R["nbl"].rearrange("p o e -> p (o e)")
            v(dve.tensor_reduce(nbl, cmp16[:, :, :], AX.X, ALU.add))
            v(dve.tensor_scalar(nbl, nbl, 1.0, None, ALU.max))
            cb, cb2 = (R[n].rearrange("p o e -> p (o e)") for n in ("cb", "cb2"))
            v(dve.tensor_copy(cb, nbl))
            for sh in (1, 2, 4, 8):
                v(dve.tensor_copy(cb2[:, 0:sh], cb[:, 0:sh]))
                v(dve.tensor_tensor(cb2[:, sh:NE], cb[:, sh:NE], cb[:, 0:NE - sh], ALU.add))
                cb, cb2 = cb2, cb
            first = R["base"].rearrange("p o e -> p (o e)")
            v(dve.tensor_tensor(first, cb, nbl, ALU.subtract))
            v(dve.tensor_copy(tabs[:, T_FIRST:T_FIRST + NE], first))
            v(dve.tensor_copy(tabs[:, T_NB:T_NB + 1], cb[:, NE - 1:NE]))
            v(dve.tensor_tensor(cmpb, iota_p[:, 0:NB].unsqueeze(2).broadcast_to([P, NB, NE]),
                                cb.unsqueeze(1).broadcast_to([P, NB, NE]), ALU.is_ge))
            v(dve.tensor_reduce(ebf[:, :], cmpb, AX.X, ALU.add))
            v(dve.tensor_scalar(tabs[:, T_E:T_E + NB], ebf[:, :], float(NE - 1), None, ALU.min))
            v(dve.tensor_scalar(tabs[:, T_PAR:T_PAR + NB], tabs[:, T_E:T_E + NB], 1, 1, ALU.bitwise_and, ALU.bitwise_xor))
            v(dve.tensor_scalar(tabs[:, T_EVEN:T_EVEN + NB], ebf[:, :], float(NE - 1), 2.0, ALU.min, ALU.add))
            v(dve.tensor_scalar(tabs[:, T_ODD:T_ODD + NB], ebf[:, :], float(NE - 1), 1.0, ALU.min, ALU.add))
            v(dve.tensor_scalar(tabs[:, T_EVEN:T_EVEN + 2 * NB], tabs[:, T_EVEN:T_EVEN + 2 * NB], 1, None,
                                ALU.logical_shift_right))
            v(dve.scalar_tensor_tensor(out=R["rank"], in0=R["base"].broadcast_to([P, NX, NE]), scalar=float(P), in1=R["rank"],
                                       op0=ALU.mult, op1=ALU.add))
            for k, oh in enumerate(("oh1", "oh2")):
                v(dve.tensor_tensor(R["eq"], R["rank"], R[oh], ALU.mult))
                v(dve.tensor_reduce(R["dest"][:, k, :], R["eq"], AX.X, ALU.add))
            v(dve.tensor_copy(desti[:, :, :], R["dest"]))
            v(dve.tensor_scalar(blki[:, :, :], desti[:, :, :], 7, None, ALU.logical_shift_right))
            v(dve.tensor_scalar(posi[:, :, :], desti[:, :, :], P - 1, None, ALU.bitwise_and))
            v(dve.tensor_copy(R["blkf"], blki[:, :, :]))
            v(dve.tensor_copy(R["posf"], posi[:, :, :]))
            for n in range(2 * NX):
                t, k = n // 2, n % 2
                if n >= 2:
                    dve.wait_ge(S["rank_done"], n)
                dve.tensor_scalar(onehot[:, n % 2, :], iota_p[:, :], R["posf"][:, k, t:t + 1], None, ALU.is_equal)
                dve.tensor_scalar(slotv[:, n % 2, 0, :], iota_p[:, 0:NB], R["blkf"][:, k, t:t + 1], tokid[:, t:t + 1],
                                  ALU.is_equal, ALU.mult)
                dve.tensor_scalar(slotv[:, n % 2, 1, :], iota_p[:, 0:NB], R["blkf"][:, k, t:t + 1], R["wk"][:, k, t:t + 1],
                                  ALU.is_equal, ALU.mult).then_inc(S["slots_done"], 1)
            dve.wait_ge(S["rank_done"], 2 * NX + 1)
            v(dve.tensor_copy(slot_tok[:, 0:NB], ps[:, 6, 256:256 + NB]))
            dve.tensor_copy(slot_w[:, :], ps[:, 6, 256 + NB:256 + 2 * NB]).then_inc(S["table_ready"], 1)
            dve.wait_ge(S["table_ready"], 1)
            nb = dve.value_load(tabs[0:1, T_NB:T_NB + 1], min_val=1, max_val=MAXB)

            def turn_out(b, slot):
                dve.wait_ge(S["x_turned"], b + 3)
                dve.tensor_copy(xT[:, slot, 0:HALF], ps[:, 0, :]).then_inc(S["xT_ready_v"], 1)

            turn_out(0, 0)
            with dve.Fori(0, NB // 2) as pair:
                i = pair * 2
                for s in range(2):
                    with dve.If(i + s < nb):
                        b = i + s
                        dve.wait_ge(S["silu_a"], b + 1)
                        dve.tensor_tensor(hid[:, 0:256], hsil[:, 0:256], ps[:, 3, 0:256], ALU.mult).then_inc(S["hid_a"], 1)
                        turn_out(b + 1, 1 - s)
                        dve.wait_ge(S["silu_b"], b + 1)
                        dve.tensor_tensor(hid[:, 256:512], hsil[:, 256:512], ps[:, 5, 0:256], ALU.mult).then_inc(S["hid_b"], 1)
                        dve.wait_ge(S["l2_done"], b + 1)
                        dve.wait_ge(y_stored[s], 16 * pair + 16)
                        for h in range(2):
                            cols = slice(h * HALF, (h + 1) * HALF)
                            dve.scalar_tensor_tensor(out=ysb[:, s, cols], in0=ps[:, 6 + h, :], scalar=slot_w[:, bass.ds(b, 1)],
                                                     in1=g2b[:, cols], op0=ALU.mult, op1=ALU.mult).then_inc(S["y_ready"], 1)
            for t in range(NX + 1):
                if t < NX:
                    dve.wait_ge(fin_loaded[t % 2], 32 * (t // 2 + 1))
                    for k, buf in enumerate((y1, y2)):
                        dve.tensor_tensor(x2[:, t, :], x2[:, t, :], buf[:, t % 2, :], ALU.add).then_inc(S["fin_add"], 1)
                        dve.wait_ge(S["fin_add"], 2 * t + k + 1)
                if t >= 1:
                    u = t - 1
                    dve.wait_ge(S["fpow_ready"], u + 1)
                    if u == 0:
                        dve.wait_ge(S["bcast_loaded"], 80)
                    if u >= 2:
                        dve.wait_ge(stored[u % 2], 16 * (u // 2))
                    dve.scalar_tensor_tensor(out=fin[:, u % 2, :], in0=x2[:, u, :], scalar=stat[:, 2 * NT + u:2 * NT + u + 1],
                                             in1=nfb, op0=ALU.mult, op1=ALU.mult).then_inc(S["fout_ready"], 1)

        @block.tensor
        def _(pe):
            pe.wait_ge(S["small_loaded"], 16 * 7)
            pe.wait_ge(S["consts"], 23)
            pe.transpose(ps[:, 7, 0:85], small_rows[:, :], ident[0:85, 0:85]).then_inc(S["small_turned"], 1)

            def turn_rows(t):
                pe.wait_ge(S["scaled"], t + 1)
                if t >= 2:
                    pe.wait_ge(S["hx_a"], t - 1)
                    pe.wait_ge(S["hx_v"], t - 1)
                for k in range(KC):
                    ins = pe.transpose(ps[:, 2 * (t % 2) + k // 4, (k % 4) * P:(k % 4 + 1) * P],
                                       rows[:, t, k * P:(k + 1) * P], ident[:, :])
                ins.then_inc(S["turned"], 1)

            def modulation(j, bank, base):
                w = unit_ready(pe, ("mod", j))
                for m in range(4):
                    col = base + 2 * m
                    for k in range(KC):
                        ins = pe.matmul(ps[:, bank, col:col + 2], w[:, k, m * P:(m + 1) * P], silu_c[:, k, :],
                                        start=(k == 0), stop=(k == KC - 1))
                ins.then_inc(S["mod_used"], 1)

            turn_rows(0)
            pe.wait_ge(S["silu_ready"], 1)
            modulation(0, 6, 0)
            turn_rows(1)
            for j in range(1, 4):
                modulation(j, 6, 8 * j)
            for t in range(2, NT):
                turn_rows(t)

            pe.wait_ge(S["rw_loaded"], 16)
            for g, (t0, n) in enumerate(tok_groups):
                pe.wait_ge(S["hx_a"], NT)
                pe.wait_ge(S["hx_v"], NT)
                for k in range(KC):
                    ins = pe.matmul(ps[0:32, g, 0:n * P], w_r[:, k, :], hxT[:, k, t0 * P:(t0 + n) * P],
                                    start=(k == 0), stop=(k == KC - 1))
                ins.then_inc(S["r_done"], 1)
            pe.wait_ge(S["rT_ready"], 3)
            pe.wait_ge(S["gk_loaded"], 48)

            def proj(n):
                g = groups[n]
                if n >= PB:
                    s, v = evac[n - PB]
                    pe.wait_ge(S[s], v)
                bank = n % PB
                if g[0] in "vg":
                    w = unit_ready(pe, (g[0], 0))
                    for k in range(KC):
                        ins = pe.matmul(ps[:, bank, :], hxT[:, k, g[1] * P:(g[1] + 1) * P], w[:, k, :],
                                        start=(k == 0), stop=(k == KC - 1))
                else:
                    kind, a, gr = g
                    w = unit_ready(pe, ("u" if kind == "u" else "qk", 0))
                    col = {"q": 0, "k": QK, "u": 0}[kind] + a * P
                    t0, m = tok_groups[gr]
                    for k in range(KC):
                        ins = pe.matmul(ps[:, bank, 0:m * P], w[:, k, col:col + P], hxT[:, k, t0 * P:(t0 + m) * P],
                                        start=(k == 0), stop=(k == KC - 1))
                ins.then_inc(S["proj_done"], 1)

            def logits(t):
                if t >= 1:
                    pe.wait_ge(S["lg_min"], 2 * t)
                pe.matmul(ps[:, 4, :], rT[:, t * P:(t + 1) * P], w_gk[:, :, :].rearrange("p d n -> p (d n)"),
                          start=True, stop=True).then_inc(S["lg_done"], 1)

            def cumulate(t):
                pe.wait_ge(S["sp_ready"], t + 1)
                if t >= 1:
                    pe.wait_ge(S["cum_read"], t)
                for d in range(2):
                    for a in range(2):
                        col = (2 * d + a) * P
                        pe.matmul(ps[:, 6, 256 + 2 * d + a:257 + 2 * d + a], spl[:, t % 2, col:col + P], midc[:, d:d + 1],
                                  start=True, stop=True)
                        ins = pe.matmul(ps[:, 5, col:col + P], spl[:, t % 2, col:col + P], tri[:, d, :], start=True, stop=True)
                ins.then_inc(S["cum_done"], 1)

            logits(0)
            for t in range(NT):
                proj(t)
                cumulate(t)
                if t + 1 < NT:
                    logits(t + 1)
            for n in range(NT, len(groups)):
                proj(n)
            for j in range(4, 12):
                modulation(j, 7, 8 * (j - 4))
            pe.wait_ge(S["bcols_ready"], 4)
            pe.transpose(ps[0:32, 6, 384:512], bcols[:, :, :].rearrange("p v k -> p (v k)"), ident[:, :]).then_inc(S["brows_turned"], 1)

            pe.wait_ge(S["ev_v"], nv)
            pe.wait_ge(S["ev_a"], na)
            for n, tt in enumerate(steps()):
                if n >= 1:
                    pe.wait_ge(S["kt_ready"], n)
                for d in range(2):
                    for a in range(2):
                        ins = pe.transpose(ps[:, 4, (2 * d + a) * P:(2 * d + a + 1) * P], kdec[:, tt[d], d, a, :], ident[:, :])
                ins.then_inc(S["kt_done"], 1)
                pe.wait_ge(S["kt_ready"], n + 1)
                if n >= 1:
                    pe.wait_ge(S["state_step"], n)
                for d in range(2):
                    for a in range(2):
                        for h in range(2):
                            head = 2 * a + h
                            ins = pe.matmul(ps[DK * h:DK * h + DK, 5, (2 * d + a) * P:(2 * d + a + 1) * P],
                                            ktok[:, d, a, DK * h:DK * h + DK], vals[:, tt[d], head * DV:(head + 1) * DV],
                                            start=True, stop=True)
                ins.then_inc(S["kv_done"], 1)
            pe.wait_ge(S["state_saved"], 4 * NX)
            pe.wait_ge(S["state_step"], NT)
            for t in range(NX):
                for d in range(2):
                    if t >= 1:
                        pe.wait_ge(S["sc_masked"], 2 * (t - 1) + d + 1)
                    for a in range(2):
                        ins = pe.matmul(ps[:, d, a * 256:(a + 1) * 256], kdec[:, t, d, a, :],
                                        qbd[:, t, d, a].rearrange("p h i -> p (h i)"), start=True, stop=True)
                    ins.then_inc(S["sc_done"], 1)
                pe.wait_ge(S["sc_masked"], 2 * t + 2)
                if t >= 1:
                    pe.wait_ge(S["on_ready"], t)
                for a in range(2):
                    for h in range(2):
                        head = 2 * a + h
                        o = ps[:, 2, head * DV:(head + 1) * DV]
                        for d in range(2):
                            pe.matmul(o, smask[:, d, head * P:(head + 1) * P], vals[:, t, head * DV:(head + 1) * DV],
                                      start=(d == 0), stop=False)
                        for d in range(2):
                            ins = pe.matmul(o, qbd[:, t, d, a, h, :], state_in[:, t, d, a, :], start=False, stop=(d == 1))
                ins.then_inc(S["o_done"], 1)
                pe.wait_ge(S["og_ready"], t + 1)
                if t >= 1:
                    pe.wait_ge(S["mixg_ready"], t)
                for h in range(HEADS):
                    ins = pe.transpose(ps[:, 3, h * P:(h + 1) * P], onorm[:, h * DV:(h + 1) * DV], ident[:, :])
                ins.then_inc(S["ot_done"], 1)
            for g in range(NG):
                pe.wait_ge(S["pooled"], g + 1)
                for h in range(2):
                    if g >= 1:
                        pe.wait_ge(S["mixp_ready"], 2 * (g - 1) + h + 1)
                    pe.matmul(ps[:, 4 + h, :], wp[:, g, :], uT[:, g, h * HALF:(h + 1) * HALF], start=True, stop=True)\
                        .then_inc(S["mixp_done"], 1)
            pe.wait_ge(S["mixp_ready"], 2 * NG)
            pe.wait_ge(S["mixg_ready"], NX)

            def route(t):
                pe.wait_ge(S["hx2_ready"], t + 1)
                if t >= 1:
                    pe.wait_ge(S["hx2T_ready"], 2 * t)
                for k in range(KC):
                    ins = pe.transpose(ps[:, 4 + k // 4, (k % 4) * P:(k % 4 + 1) * P], hx2[:, t % 2, k * P:(k + 1) * P], ident[:, :])
                ins.then_inc(S["hx2_turned"], 1)
                pe.wait_ge(S["hx2T_ready"], 2 * t + 2)
                for k in range(KC):
                    ins = pe.matmul(ps[:, 6, t * NE:(t + 1) * NE], hx2T[:, k * P:(k + 1) * P], w_rt[:, k, :],
                                    start=(k == 0), stop=(k == KC - 1))
                ins.then_inc(S["logit_done"], 1)

            for t in range(NX):
                for h in range(2):
                    w = unit_ready(pe, ("out", h))
                    if t >= 2:
                        pe.wait_ge(S["gated"], 2 * (t - 2) + h + 1)
                    for k in range(KC):
                        m = uT[:, k, t * P:(t + 1) * P] if k < NG else gate[:, t, (k - NG) * P:(k - NG + 1) * P]
                        ins = pe.matmul(ps[:, 2 * (t % 2) + h, :], m, w[:, k, :], start=(k == 0), stop=(k == KC - 1))
                    ins.then_inc(S["y_done"], 1)
                if t >= 1:
                    route(t - 1)
            route(NX - 1)
            pe.wait_ge(S["route_ready"], 1)
            pre = rt["pre"][:, :, :].rearrange("p t e -> p (t e)")
            pe.matmul(ps[:, 7, 0:NTE], strict[:, :], rt["sel"][:, :, :].rearrange("p t e -> p (t e)"), start=True, stop=False)
            pe.matmul(ps[:, 7, 0:NTE], ones[:, :], pre[:, 0:NTE], start=False, stop=True)
            pe.matmul(ps[:, 7, NTE:NTE + NE], ones[:, :], pre[:, NTE:NTE + NE], start=True, stop=True).then_inc(S["rank_done"], 1)
            for n in range(2 * NX):
                pe.wait_ge(S["slots_done"], n + 1)
                ins = pe.matmul(ps[:, 6, 256:256 + 2 * NB], onehot[:, n % 2, :], slotv[:, n % 2].rearrange("p w b -> p (w b)"),
                                start=(n == 0), stop=(n == 2 * NX - 1)).then_inc(S["rank_done"], 1)
            pe.wait_ge(S["table_ready"], 1)
            nb = pe.value_load(tabs[0:1, T_NB:T_NB + 1], min_val=1, max_val=MAXB)
            pe.sem_inc(S["x_turned"], 2)
            pe.sem_inc(S["hT_a"], 1)
            pe.sem_inc(S["hT_b"], 1)
            pe.sem_inc(S["hid_a"], 1)
            pe.sem_inc(S["hid_b"], 1)
            pe.sem_inc(S["y_ready"], 2)

            def turn_block(b, slot, gathers, slot_before=True):
                pe.wait_ge(gathered[slot], 16 * gathers)
                if slot_before:
                    pe.wait_ge(S["xT_ready"], b)
                    pe.wait_ge(S["xT_ready_v"], b)
                for k in range(KC):
                    ins = pe.transpose(ps[:, k // 4, (k % 4) * P:(k % 4 + 1) * P], xg[:, slot, k * P:(k + 1) * P], ident[:, :])
                ins.then_inc(S["x_turned"], 1)

            turn_block(0, 0, 1, slot_before=False)
            with pe.Fori(0, NB // 2) as pair:
                i = pair * 2
                for s in range(2):
                    with pe.If(i + s < nb):
                        b = i + s
                        loads = [pe.value_load(tabs[0:1, bass.ds(b + at_, 1)], min_val=0, max_val=NE // 2)
                                 for at_ in (T_EVEN, T_ODD)]
                        half = pe.value_load(tabs[0:1, bass.ds(b + T_PAR, 1)], min_val=0, max_val=1)
                        base = half * EXPERT

                        def first(q, banks, done):
                            for k in range(KC):
                                lhs = xT[:, s, k * P:(k + 1) * P]
                                for i3, bank in enumerate(banks):
                                    ins = pe.matmul(ps[:, bank, 0:256], lhs,
                                                    arena[:, bass.ds(base + (i3 * UNIT + k * HALF + q * 256), 256)],
                                                    start=(k == 0), stop=(k == KC - 1))
                                if q == 1 and k == 3:
                                    pe.wait_ge(S["hid_a"], b + 2)
                                    for m in range(2):
                                        h_ins = pe.transpose(ps[:, 2, m * P:(m + 1) * P], hid[:, m * P:(m + 1) * P], ident[:, :])
                                    h_ins.then_inc(S["hta"], 1)
                            ins.then_inc(S[done], 1)

                        def second(k, h):
                            return pe.matmul(ps[:, 6 + h, :], hT[:, k, :],
                                             arena[:, bass.ds(base + (2 * UNIT + k * D + h * HALF), HALF)],
                                             start=(k == 0), stop=(k == 3))

                        pe.wait_ge(S["xT_ready"], b + 1)
                        pe.wait_ge(S["xT_ready_v"], b + 1)
                        for par in range(2):
                            pe.wait_ge(moe_w13[par], 32 * loads[par] + 32)
                        pe.wait_ge(S["hT_a"], b + 1)
                        pe.wait_ge(S["hid_a"], b + 1)
                        first(0, (2, 3), "l1a")
                        turn_block(b + 1, 1 - s, pair + (s + 1))
                        pe.wait_ge(S["hT_b"], b + 1)
                        pe.wait_ge(S["hid_b"], b + 1)
                        first(1, (4, 5), "l1b")
                        for par in range(2):
                            pe.wait_ge(moe_w2[par], 16 * loads[par] + 16)
                        pe.wait_ge(S["hT_a"], b + 2)
                        pe.wait_ge(S["y_ready"], 2 * i + (2 * s + 2))
                        second(0, 0)
                        second(0, 1)
                        second(1, 0)
                        pe.wait_ge(S["hid_b"], b + 2)
                        for m in range(2):
                            ins = pe.transpose(ps[:, 4, m * P:(m + 1) * P], hid[:, (2 + m) * P:(3 + m) * P], ident[:, :])
                        ins.then_inc(S["htb"], 1)
                        second(1, 1)
                        pe.wait_ge(S["hT_b"], b + 2)
                        for k in (2, 3):
                            for h in range(2):
                                ins = second(k, h)
                        ins.then_inc(S["l2_done"], 1)


_INS = ["x", "c", "ctx", "c_ctx", "w_mod", "b_mod", "norm1", "norm2", "w_in", "w_gk2", "b_gk", "w_pool",
        "pool_scale", "gla_gain", "w_out", "w_router", "router_bias", "w1", "w3", "w2", "norm_f"]
_OUT = (1, NX * P, D)


def kernel(**inputs):
    import numpy as _np
    import concourse.bacc as _bacc
    from concourse import mybir as _mybir
    from concourse.bass_utils import run_bass_kernel_spmd as _run

    nc = _bacc.Bacc("TRN2", target_bir_lowering=False, num_devices=1)
    arrays, args = {}, []
    values = [(name, _np.ascontiguousarray(inputs[name])) for name in _INS] + [("inv_counts", box_inverse_counts())]
    for name, a in values:
        arrays[f"in_{name}_dram"] = a
        args.append(nc.dram_tensor(f"in_{name}_dram", a.shape, _mybir.dt.from_np(a.dtype), kind="ExternalInput").ap())
    args.append(nc.dram_tensor("out_dram", _OUT, F32, kind="ExternalOutput").ap())
    hybrid_block(nc, *args)
    r = _run(nc, [arrays], core_ids=[0])
    return r.results[0]["out_dram"]
```

```python
from contextlib import ExitStack

import numpy as np

import concourse.bass as bass
from concourse import mybir

F32 = mybir.dt.float32
I32 = mybir.dt.int32
ALU = mybir.AluOpType
ACT = mybir.ActivationFunctionType
AX = mybir.AxisListType

P = 128
D = 1024
KC = D // P
NX = 8
NCT = 2
NT = NX + NCT
N_MOD = 6
EPS = 1e-6
GRID_W = 64
GRID_H = NX * P // GRID_W
WINDOWS = (2, 4, 8, 16)
NG = len(WINDOWS)
HALF = 512
HEADS = 4
DV = 128
DK = 64
QK = HEADS * DK
RANK2 = 32
GATE_NORM = 16.0
COL_U, COL_Q, COL_V, COL_G, COL_R = 0, HALF, HALF + 2 * QK, 2 * HALF + 2 * QK, 3 * HALF + 2 * QK
MID = P // 2
NE = 16
NGR = 4
MAXB = 31
NB = MAXB + 1
UNIT = KC * HALF
EXPERT = 3 * UNIT
BIG = 1.0e30


def box_inverse_counts():
    out = np.zeros((NG, GRID_H + GRID_W), np.float32)
    for g, w in enumerate(WINDOWS):
        for base, n in ((0, GRID_H), (GRID_H, GRID_W)):
            i = np.arange(n)
            count = np.clip(i + w - w // 2, 0, n) - np.clip(i - w // 2, 0, n)
            out[g, base:base + n] = (1.0 / count).astype(np.float32)
    return out.reshape(1, -1)


def hybrid_block(nc, x, c, ctx_in, c_ctx, w_mod, b_mod, norm1, norm2, w_in, w_gk2, b_gk, w_pool,
                 pool_scale, gla_gain, w_out, w_router, router_bias, w1, w3, w2, norm_f, inv_counts, out):
    with ExitStack() as stack:
        def sb(name, shape, dt=F32):
            return stack.enter_context(nc.sbuf_tensor(name, shape, dt))

        def sem(name):
            return stack.enter_context(nc.semaphore(name))

        ARENA = 49152
        arena = sb("arena", [P, ARENA])

        def at(off, pattern=None, n=None, **dims):
            v = arena[:, off:off + n]
            return v.rearrange(pattern, **dims) if pattern else v

        RING = 2
        O_S = RING * UNIT
        LATE = RING
        ring = [at(s * UNIT, "p (k n) -> p k n", UNIT, k=KC) for s in range(RING + 1)]
        state_in = at(O_S, "p (t d a n) -> p t d a n", NX * HALF, t=NX, d=2, a=2)
        O_HX = O_S + NX * HALF
        hxT = at(O_HX, "p (k t) -> p k t", KC * NT * P, k=KC)
        O_F = O_HX + KC * NT * P
        O_Q = O_F + 4096
        qdec = at(O_Q, "p (t d a i) -> p t d a i", NX * HALF, t=NX, d=2, a=2)
        O_K = O_Q + NX * HALF
        kdec = at(O_K, "p (t d a i) -> p t d a i", NT * HALF, t=NT, d=2, a=2)
        O_V = O_K + NT * HALF
        vals = at(O_V, "p (t n) -> p t n", NT * HALF, t=NT)
        O_G = O_V + NT * HALF
        gate = at(O_G, "p (t n) -> p t n", NX * HALF, t=NX)
        O_U = O_G + NX * HALF
        uT = at(O_U, "p (g t) -> p g t", NG * NX * P, g=NG)
        rows = at(O_K, "p (s n) -> p s n", NT * D, s=NT)
        absl = at(O_G, "p (s n) -> p s n", 1024, s=2)
        minl = at(O_G + 1024, "p (s n) -> p s n", 1024, s=2)
        spl = at(O_G + 2048, "p (s n) -> p s n", 1024, s=2)
        mod_rows = at(O_G, None, 4 * HALF)[0:2]
        rT = at(O_U, None, NT * P)[0:33]
        w_r = at(O_U + 1280, "p (k n) -> p k n", KC * RANK2, k=KC)
        w_gk = at(O_U + 1536, "p (d n) -> p d n", 2 * QK, d=2)[0:33]
        small_rows = at(O_U + 2048, None, P)[0:85]
        sq0 = at(O_U + 2176, None, D)
        boxa = at(O_F, "p (r w) -> p r w", 2048, r=32)
        boxb = at(O_F + 2048, "p (r w) -> p r w", 2048, r=32)
        macc = at(O_G + 6 * HALF, None, HALF)
        mrow = at(O_G + 7 * HALF, None, HALF)[0:1]
        smask = at(O_K + NX * HALF, "p (h d n) -> p h d n", 1024, h=2, d=2)
        ssum = at(O_V + NX * HALF, "p (h n) -> p h n", HALF, h=2)
        onorm = at(O_V + NX * HALF + HALF, None, HALF)
        x2 = at(O_HX, "p (t n) -> p t n", NX * D, t=NX)
        g1b, a2b = (at(O_HX + NX * D + i * D, None, D) for i in range(2))
        s2b = at(O_F, None, D)
        hx2 = at(O_F + D, "p (s n) -> p s n", 2 * D, s=2)
        hx2T = at(O_F + 3 * D, None, D)
        cmpb = at(O_G, "p (b e) -> p b e", NB * NE, b=NB)
        onehot = at(O_G + D, "p (s n) -> p s n", 2 * NX * P, s=2 * NX)
        slotv = at(O_G + D + 2 * NX * P, "p (s w b) -> p s w b", 4 * NX * NB, s=2 * NX, w=2)
        HALF_AT = (O_Q, 0)
        O_E = O_Q + EXPERT
        g2b = at(O_HX + NX * D, None, D)
        assert O_HX >= EXPERT and O_E + 3 * D + HALF <= O_U
        xg = at(O_F, "p (s n) -> p s n", 2 * D, s=2)
        xT = at(O_F + 2 * D, "p (s n) -> p s n", 2 * D, s=2)
        hsil = at(O_E, None, HALF)
        hid = at(O_E + HALF, None, HALF)
        hT = at(O_E + D, "p (k n) -> p k n", HALF, k=4)
        ysb = at(O_E + D + HALF, "p (s n) -> p s n", 2 * D, s=2)
        y1 = at(O_F, "p (s n) -> p s n", 2 * D, s=2)
        y2 = at(O_F + 2 * D, "p (s n) -> p s n", 2 * D, s=2)
        fin = at(O_E, "p (s n) -> p s n", 2 * D, s=2)
        nfb = at(O_HX + (NX + 1) * D, None, D)
        sqf = at(0, None, D)

        ident = sb("ident", [P, P])
        mask = sb("mask", [P, 2, P])
        tri = sb("tri", [P, 2, P + 1])
        midc = sb("midc", [P, 2])
        small = sb("small", [P, 85])
        ktok = sb("ktok", [P, 2, 2, P])
        sqg = ktok[:, :, :, :].rearrange("p h a n -> p h (a n)")
        rlT = sb("rlT", [NE, P])
        logit = sb("logit", [P, NX, NE])
        silu_c = sb("silu_c", [P, KC, 2])
        mod = sb("mod", [P, 2, KC, 2])
        a1 = sb("a1", [P, KC, 2])
        stat = sb("stat", [P, 4 * NT + 8])
        expo = sb("expo", [P, 4])
        dec1 = sb("dec1", [P, NT, 2, 2])
        dec2 = sb("dec2", [P, NT, 2, 2])
        dec = sb("dec", [P, NT, 2, 2])
        state = sb("state", [P, 2, 2, DV])
        bmod_row = ktok[0:1].rearrange("p h a n -> p (h a n)")
        norm2_row = state[0:1].rearrange("p d a n -> p (d a n)")
        ost = sb("ost", [P, 12])
        wp = sb("wp", [P, NG, P])
        icnt = sb("icnt", [P, NG, GRID_H + GRID_W])
        w_rt = sb("w_rt", [P, KC, NE])
        bias_b = sb("bias_b", [P, NE])

        ps = stack.enter_context(nc.psum_tensor("ps", [P, 8, 512], F32))

        hx_dram = nc.dram_tensor("hx_rows", [NX * P, D], F32).ap()
        y_dram = nc.dram_tensor("y_rows", [NB * P, D], F32).ap()
        m_dram = nc.dram_tensor("mod_rows_dram", [8, HALF], F32).ap()

        names = """consts small_loaded small_turned small_ready silu_ready mod_used mod_row mod_turned mod_added mod_ready
            macc_ready mrow_done mrow_ready m_chain n2_loaded bmod_loaded mrow_stored bcast_loaded g2_loaded nf_loaded
            ss_ready pow_ready scaled turned hx_a hx_v
            rw_loaded gk_loaded r_done rT_ready lg_done lg_min lg_exp lg_ln sp_ready cum_done cum_read
            proj_done ev_a ev_v pool_w_loaded
            kt_done kt_ready kv_done state_step state_saved s_chain
            sc_done sc_masked s_summed o_done osq_ready oss_ready opow_ready on_ready og_ready ot_done mixg_ready
            box_chain pooled mixp_done mixp_ready
            y_done gated x2_ready ss2_ready pow2_ready hx2_ready hx2_turned hx2T_ready logit_done rl_ready rl_turned rl_out sig_ready
            r_chain route_ready rank_done slots_done table_ready
            tok_ready tok_seen x_turned xT_ready xT_ready_v l1a l1b silu_a silu_b hid_a hid_b hta htb hT_a hT_b
            l2_done y_filled y_ready
            fin_add fss_ready fpow_ready fout_ready""".split()
        S = {n: sem(n) for n in names}
        row_loaded = [sem(f"row_loaded{t}") for t in range(NT)]
        ring_loaded = [sem(f"ring_loaded{i}") for i in range(RING + 1)]
        hx2_stored, y_stored, fin_loaded, stored, moe_w13, moe_w2, gathered = (
            [sem(f"{n}{i}") for i in range(2)]
            for n in ("hx2_stored", "y_stored", "fin_loaded", "stored", "moe_w13_", "moe_w2_", "gathered"))

        def link(eng, chain, ins):
            name, count = chain
            count[0] += 1
            ins.then_inc(S[name], 1)
            eng.wait_ge(S[name], count[0])

        wmod_v = w_mod[0].rearrange("(k p) n -> p k n", p=P)
        win_v = w_in[0].rearrange("(k p) n -> p k n", p=P)
        wout_v = w_out[0].rearrange("(k p) n -> p k n", p=P)
        units = ([(("mod", j), j % 2) for j in range(4)] + [(("v", 0), 0), (("u", 0), 1)] + [(("mod", j), LATE) for j in range(4, 9)]
                 + [(("qk", 0), 0)] + [(("mod", j), LATE) for j in range(9, 12)] + [(("g", 0), 1), (("out", 0), 0), (("out", 1), 1)])
        unit_slot = dict(units)
        unit_turn = {u: [v for v, at_slot in units if at_slot == slot].index(u) for u, slot in units}

        def unit_src(u):
            kind, j = u
            if kind == "mod":
                return wmod_v[:, :, j * HALF:(j + 1) * HALF]
            if kind == "out":
                return wout_v[:, :, j * HALF:(j + 1) * HALF]
            col = {"v": COL_V, "qk": COL_Q, "g": COL_G, "u": COL_U}[kind]
            return win_v[:, :, col:col + HALF]

        def unit_used(u):
            if u[0] == "mod" and u[1] < 4:
                return S["mod_used"], u[1] + 1
            if u[0] == "mod":
                return S["macc_ready"], u[1] - 3
            last = {"v": ("v", NT - 1), "qk": ("q", 1, 1), "g": ("g", NX - 1), "u": ("u", NG - 1, 1)}[u[0]]
            return S["proj_done"], group_no[last] + 1

        def unit_ready(eng, u):
            eng.wait_ge(ring_loaded[unit_slot[u]], 16 * (unit_turn[u] + 1))
            return ring[unit_slot[u]]

        tok_groups = [(0, 4), (4, 4), (8, 2)]
        groups = ([("v", t) for t in range(NT)] + [("u", p, g) for p in range(NG) for g in range(2)]
                  + [("k", a, g) for g in range(3) for a in range(2)] + [("q", a, g) for g in range(2) for a in range(2)]
                  + [("g", t) for t in range(NX)])
        PB = 4
        evac = {}
        na = nv = 0
        for n, g in enumerate(groups):
            on_act = g[0] == "g" or (g[0] == "v" and g[1] % 2 == 0) or (g[0] == "u")
            if on_act:
                na += 1
                evac[n] = ("ev_a", na)
            else:
                nv += 1
                evac[n] = ("ev_v", nv)
        group_no = {g: n for n, g in enumerate(groups)}

        def evacuated(g):
            s, v = evac[group_no[g]]
            return S[s], v

        def steps():
            fwd = [NX, NX + 1] + list(range(NX))
            bwd = [NX + 1, NX] + list(range(NX - 1, -1, -1))
            return list(zip(fwd, bwd))

        NTE = NX * NE
        rt = {}
        rt_at = O_U
        for n, shape in dict(s=[NX, NE], sbias=[NX, NE], hi=[32, 2], lo=[32, 2], t1=[32, 1], t2=[32, 1],
                             gm=[NX, 1], geq=[NX, NGR], goh=[NX, NGR], mb=[NX, NE], mx=[NX, 1], eq=[NX, NE],
                             oh1=[NX, NE], oh2=[NX, NE], sel=[4 + NX, NE], pre=[4 + NX, NE], pre2=[4 + NX, NE], tot=[1, NE],
                             nbl=[1, NE], cb=[1, NE + 8], cb2=[1, NE + 8], base=[1, NE], rank=[NX, NE],
                             s12=[2, NX], ssum=[NX, 1], wk=[2, NX], dest=[2, NX],
                             blkf=[2, NX], posf=[2, NX], prior=[NX, 2 * NGR]).items():
            width = shape[0] * shape[1]
            rt[n] = at(rt_at, "p (a b) -> p a b", width, a=shape[0])
            rt_at += width
        assert rt_at <= ARENA
        cmp16 = at(O_G + HALF, "p (e k) -> p e k", NE * KC, e=NE)
        desti = sb("desti", [P, 2, NX], I32)
        blki = sb("blki", [P, 2, NX], I32)
        posi = sb("posi", [P, 2, NX], I32)
        iota_p = sb("iota_p", [P, P])
        iota_e = sb("iota_e", [P, NE])
        tokid = sb("tokid", [P, NX])
        thresh = sb("thresh", [P, KC])
        ones = sb("ones", [P, P])
        strict = sb("strict", [P, P])
        slot_tok = sb("slot_tok", [P, NB + 1], I32)
        block_tok = sb("block_tok", [P, 2], I32)
        slot_w = sb("slot_w", [P, NB])
        ebf = sb("ebf", [P, NB])
        tabs = sb("tabs", [P, 4 * NB + NE + 1], I32)
        T_E, T_PAR, T_EVEN, T_ODD, T_FIRST, T_NB = 0, NB, 2 * NB, 3 * NB, 4 * NB, 4 * NB + NE

        block = stack.enter_context(nc.Block())

        @block.sync
        def _(sp):
            sp.dma_start(small_rows[0:8, :], c.rearrange("o (k p) -> (o k) p", p=P)).then_inc(S["small_loaded"], 16)
            sp.dma_start(small_rows[8:16, :], c_ctx.rearrange("(k p) -> k p", p=P)).then_inc(S["small_loaded"], 16)
            sp.dma_start(small_rows[16:24, :], norm1.rearrange("o (k p) -> (o k) p", p=P)).then_inc(S["small_loaded"], 16)
            sp.dma_start(small_rows[24:32, :], norm2.rearrange("o (k p) -> (o k) p", p=P)).then_inc(S["small_loaded"], 16)
            sp.dma_start(small_rows[32:80, :], b_mod.rearrange("o (k p) -> (o k) p", p=P)).then_inc(S["small_loaded"], 16)
            sp.dma_start(small_rows[80:84, :], pool_scale.rearrange("o (k p) -> (o k) p", p=P)).then_inc(S["small_loaded"], 16)
            sp.dma_start(small_rows[84:85, :], gla_gain).then_inc(S["small_loaded"], 16)
            for n, (u, slot) in enumerate(units):
                before = [v for v, at_slot in units[:n] if at_slot == slot]
                if before:
                    sp.wait_ge(*unit_used(before[-1]))
                sp.dma_start(ring[slot], unit_src(u)).then_inc(ring_loaded[slot], 16)

            def load_expert(e, par):
                at_half = HALF_AT[par]
                for i, w in enumerate((w1, w3)):
                    sp.dma_start(at(at_half + i * UNIT, "p (k n) -> p k n", UNIT, k=KC),
                                 w[0, bass.ds(e, 1)].rearrange("o (k p) n -> p (o k) n", p=P)).then_inc(moe_w13[par], 16)
                sp.dma_start(at(at_half + 2 * UNIT, "p (k n) -> p k n", UNIT, k=4),
                             w2[0, bass.ds(e, 1)].rearrange("o (k p) n -> p (o k) n", p=P)).then_inc(moe_w2[par], 16)

            for par in range(2):
                sp.sem_inc(moe_w13[par], 32)
                sp.sem_inc(moe_w2[par], 16)
            sp.wait_ge(S["ot_done"], NX)
            load_expert(0, 0)
            sp.wait_ge(S["y_done"], 2 * NX)
            load_expert(1, 1)
            sp.wait_ge(S["table_ready"], 1)
            with sp.Fori(1, NE // 2) as pair:
                for par in range(2):
                    e = pair * 2 + par
                    first = sp.value_load(tabs[0:1, bass.ds(e + (T_FIRST - 1), 1)], min_val=1, max_val=MAXB)
                    sp.wait_ge(S["l2_done"], first)
                    load_expert(e, par)
            for t in range(NX):
                sp.wait_ge(S["fout_ready"], t + 1)
                sp.dma_start(out[0, t * P:(t + 1) * P, :], fin[:, t % 2, :]).then_inc(stored[t % 2], 16)
            for par in range(2):
                sp.wait_ge(stored[par], 16 * NX // 2)

        @block.gpsimd
        def _(pool):
            cc = ("consts", [0])
            link(pool, cc, pool.memset(ident[:, :], 0.0))
            link(pool, cc, pool.memset(mask[:, :, :], 1.0))
            link(pool, cc, pool.memset(tri[:, :, :], -1.0 / GATE_NORM))
            link(pool, cc, pool.memset(midc[:, :], 0.0))
            link(pool, cc, pool.memset(ones[:, :], 1.0))
            link(pool, cc, pool.memset(strict[:, :], 1.0))
            link(pool, cc, pool.memset(expo[:, :], -0.5))
            link(pool, cc, pool.memset(rT[32:33, :], 1.0))
            link(pool, cc, pool.memset(w_gk[0:32, :, :], 0.0))
            link(pool, cc, pool.iota(iota_p[:, :], pattern=[[1, P]], base=0, channel_multiplier=0,
                      allow_small_or_imprecise_dtypes=True))
            link(pool, cc, pool.iota(iota_e[:, :], pattern=[[-1, NE]], base=NE, channel_multiplier=0,
                      allow_small_or_imprecise_dtypes=True))
            link(pool, cc, pool.iota(tokid[:, :], pattern=[[P, NX]], base=0, channel_multiplier=1,
                      allow_small_or_imprecise_dtypes=True))
            link(pool, cc, pool.iota(thresh[:, :], pattern=[[P, KC]], base=0, channel_multiplier=0,
                      allow_small_or_imprecise_dtypes=True))
            link(pool, cc, pool.affine_select(out=ident[:, :], in_=ident[:, :], compare_op=ALU.not_equal, fill=1.0, base=0,
                               pattern=[[-1, P]], channel_multiplier=1))
            for m in (mask, tri[:, :, 0:P]):
                link(pool, cc, pool.affine_select(out=m[:, 0, :], in_=m[:, 0, :], compare_op=ALU.is_ge, fill=0.0, base=0,
                                   pattern=[[1, P]], channel_multiplier=-1))
                link(pool, cc, pool.affine_select(out=m[:, 1, :], in_=m[:, 1, :], compare_op=ALU.is_ge, fill=0.0, base=0,
                                   pattern=[[-1, P]], channel_multiplier=1))
            link(pool, cc, pool.affine_select(out=strict[:, :], in_=strict[:, :], compare_op=ALU.is_gt, fill=0.0, base=0,
                               pattern=[[1, P]], channel_multiplier=-1))
            link(pool, cc, pool.memset(midc[0:MID, 0:1], -1.0 / GATE_NORM))
            link(pool, cc, pool.memset(midc[MID:P, 1:2], -1.0 / GATE_NORM))
            for d in range(2):
                link(pool, cc, pool.tensor_scalar(tri[:, d, 0:P], tri[:, d, 0:P], midc[:, d:d + 1], None, ALU.subtract))
                link(pool, cc, pool.tensor_copy(tri[:, d, P:P + 1], midc[:, d:d + 1]))
            for d in range(2):
                pool.dma_start(w_gk[16 * d:16 * d + 16, d, :], w_gk2[0, d]).then_inc(S["gk_loaded"], 16)
            pool.dma_start(w_gk[32:33, :, :], b_gk).then_inc(S["gk_loaded"], 16)
            pool.dma_start(w_r[:, :, :], win_v[:, :, COL_R:COL_R + RANK2]).then_inc(S["rw_loaded"], 16)
            pool.dma_start(wp[:, :, :], w_pool[0].rearrange("g c n -> c g n")).then_inc(S["pool_w_loaded"], 16)
            pool.dma_start(icnt[:, :, :].rearrange("p g n -> p (g n)"),
                           inv_counts.partition_broadcast(P)).then_inc(S["pool_w_loaded"], 16)
            pool.dma_start(w_rt[:, :, :], w_router.rearrange("(k p) e -> p k e", p=P)).then_inc(S["pool_w_loaded"], 16)
            pool.dma_start(bias_b[:, :], router_bias.rearrange("(o e) -> o e", o=1).partition_broadcast(P))\
                .then_inc(S["pool_w_loaded"], 16)
            for t in range(NT):
                pool.wait_ge(S["ss_ready"], t + 1)
                pool.tensor_scalar(stat[:, NT + t:NT + t + 1], stat[:, t:t + 1], 1.0 / D, EPS, ALU.mult, ALU.add)\
                    .then_inc(S["box_chain"], 1)
                pool.wait_ge(S["box_chain"], t + 1)
                pool.tensor_tensor(stat[:, 2 * NT + t:2 * NT + t + 1], stat[:, NT + t:NT + t + 1], expo[:, 0:1], ALU.pow)\
                    .then_inc(S["pow_ready"], 1)
                pool.wait_ge(S["pow_ready"], t + 1)
            for i in range(8):
                pool.dma_start(bmod_row, b_mod[:, (4 + i) * HALF:(5 + i) * HALF]).then_inc(S["bmod_loaded"], 16)
                if i in (4, 5):
                    pool.dma_start(norm2_row, norm2[:, (i - 4) * HALF:(i - 3) * HALF]).then_inc(S["n2_loaded"], 16)
                pool.wait_ge(S["mrow_ready"], i + 1)
                pool.dma_start(m_dram[i:i + 1, :], mrow).then_inc(S["mrow_stored"], 16)
            bc = ("box_chain", [NT])
            for t in range(NX + 1):
                if t < NX:
                    pool.wait_ge(S["oss_ready"], t + 1)
                    link(pool, bc, pool.tensor_scalar(ost[:, 4:8], ost[:, 0:4], 1.0 / DV, EPS, ALU.mult, ALU.add))
                    pool.tensor_tensor(ost[:, 8:12], ost[:, 4:8], expo[:, 0:4], ALU.pow).then_inc(S["opow_ready"], 1)
                    pool.wait_ge(S["opow_ready"], t + 1)
                if t >= 1:
                    u = t - 1
                    pool.wait_ge(S["ss2_ready"], u + 1)
                    link(pool, bc, pool.tensor_scalar(stat[:, NT + u:NT + u + 1], stat[:, u:u + 1], 1.0 / D, EPS, ALU.mult, ALU.add))
                    pool.tensor_tensor(stat[:, 2 * NT + u:2 * NT + u + 1], stat[:, NT + u:NT + u + 1], expo[:, 0:1], ALU.pow)\
                        .then_inc(S["pow2_ready"], 1)
                    pool.wait_ge(S["pow2_ready"], u + 1)
            pool.wait_ge(S["table_ready"], 1)
            for par in range(2):
                pool.wait_ge(hx2_stored[par], 16 * NX // 2)
            nb = pool.value_load(tabs[0:1, T_NB:T_NB + 1], min_val=1, max_val=MAXB)

            def gather(b, slot):
                pool.wait_ge(S["x_turned"], b + 1)
                pool.tensor_copy(block_tok[:, slot:slot + 1], slot_tok[:, bass.ds(b, 1)]).then_inc(S["tok_ready"], 1)
                pool.wait_ge(S["tok_ready"], b + 1)
                pool.sem_inc(S["tok_seen"], 1)
                pool.indirect_dma_start(out=xg[:, slot, :], out_offset=None, in_=hx_dram,
                                        in_offset=bass.IndirectOffsetOnAxis(ap=block_tok[:, slot:slot + 1], axis=0))\
                    .then_inc(gathered[slot], 16)

            gather(0, 0)
            with pool.Fori(0, NB // 2) as pair:
                i = pair * 2
                for s in range(2):
                    with pool.If(i + s < nb):
                        gather(i + (s + 1), 1 - s)
            for par in range(2):
                pool.wait_ge(y_stored[par], 16 * NB // 2 + 16)
            for t in range(NX):
                if t >= 2:
                    pool.wait_ge(S["fin_add"], 2 * (t - 1))
                for k, buf in enumerate((y1, y2)):
                    pool.indirect_dma_start(out=buf[:, t % 2, :], out_offset=None, in_=y_dram,
                                            in_offset=bass.IndirectOffsetOnAxis(ap=desti[:, k, t:t + 1], axis=0))\
                        .then_inc(fin_loaded[t % 2], 16)
                if t >= 1:
                    pool.wait_ge(S["fss_ready"], t)
                    link(pool, bc, pool.tensor_scalar(stat[:, NT + t - 1:NT + t], stat[:, t - 1:t], 1.0 / D, EPS, ALU.mult, ALU.add))
                    pool.tensor_tensor(stat[:, 2 * NT + t - 1:2 * NT + t], stat[:, NT + t - 1:NT + t], expo[:, 0:1], ALU.pow)\
                        .then_inc(S["fpow_ready"], 1)
                    pool.wait_ge(S["fpow_ready"], t)
            t = NX
            pool.wait_ge(S["fss_ready"], t)
            link(pool, bc, pool.tensor_scalar(stat[:, NT + t - 1:NT + t], stat[:, t - 1:t], 1.0 / D, EPS, ALU.mult, ALU.add))
            pool.tensor_tensor(stat[:, 2 * NT + t - 1:2 * NT + t], stat[:, NT + t - 1:NT + t], expo[:, 0:1], ALU.pow)\
                .then_inc(S["fpow_ready"], 1)

        @block.scalar
        def _(act):
            def row_src(t):
                return x[0, t * P:(t + 1) * P, :] if t < NX else ctx_in[0, (t - NX) * P:(t - NX + 1) * P, :]

            for t in range(NT):
                act.dma_start(rows[:, t, :], row_src(t)).then_inc(row_loaded[t], 16)
            act.wait_ge(S["small_ready"], 1)
            act.activation(silu_c[:, :, :], small[:, 0:16].rearrange("p (w k) -> p k w", w=2), ACT.Silu)\
                .then_inc(S["silu_ready"], 1)
            for t in range(NT):
                act.wait_ge(row_loaded[t], 16)
                act.activation(sq0, rows[:, t, :], ACT.Square, accum_out=stat[:, t:t + 1])\
                    .then_inc(S["ss_ready"], 1)
                act.wait_ge(S["ss_ready"], t + 1)
            for j in range(4):
                act.wait_ge(S["mod_used"], j + 1)
                act.activation(mod_rows[:, j * HALF:(j + 1) * HALF], ps[0:2, 4 + j, :], ACT.Copy).then_inc(S["mod_row"], 1)
            act.wait_ge(S["mod_ready"], 2)
            for t in range(NT):
                which = 0 if t < NX else 1
                act.wait_ge(S["turned"], t + 1)
                for k in range(4, KC):
                    ins = act.activation(hxT[:, k, t * P:(t + 1) * P], ps[:, 2 * (t % 2) + 1, (k - 4) * P:(k - 3) * P],
                                         ACT.Identity, bias=mod[:, 0, k, which:which + 1], scale=a1[:, k, which:which + 1])
                ins.then_inc(S["hx_a"], 1)

            def ev(n):
                act.wait_ge(S["proj_done"], n + 1)

            def decays(t):
                act.wait_ge(S["lg_min"], 2 * (t + 1))
                act.activation(absl[:, t % 2, :], absl[:, t % 2, :], ACT.Exp, scale=-1.0).then_inc(S["lg_exp"], 1)
                act.wait_ge(S["lg_exp"], t + 1)
                act.activation(absl[:, t % 2, :], absl[:, t % 2, :], ACT.Ln, bias=1.0).then_inc(S["lg_ln"], 1)

            def decay_exp(t):
                act.wait_ge(S["cum_done"], t + 1)
                for d in range(2):
                    cum = ps[:, 5 + d, 0:2 * (P + 1)].rearrange("p (a i) -> p a i", a=2)
                    if t < NX:
                        act.activation(qdec[:, t, d], cum[:, :, 0:P], ACT.Exp)
                    act.activation(kdec[:, t, d], cum[:, :, 0:P], ACT.Exp, scale=-1.0)
                    end = P - 1 if d == 0 else 0
                    act.activation(dec2[:, t, d, :], cum[:, :, end], ACT.Exp)
                    ins = act.activation(dec1[:, t, d, :], cum[:, :, P], ACT.Exp)
                ins.then_inc(S["cum_read"], 1)

            decays(0)
            for t in range(NT):
                if t + 1 < NT:
                    decays(t + 1)
                if t % 2 == 0:
                    n = group_no[("v", t)]
                    ev(n)
                    if t == 0:
                        act.wait_ge(S["turned"], NT)
                    act.activation(vals[:, t, :], ps[:, n % PB, :], ACT.Copy).then_inc(S["ev_a"], 1)
                decay_exp(t)
            for n, g in enumerate(groups):
                if g[0] == "u":
                    ev(n)
                    act.activation(uT[:, g[1], g[2] * HALF:(g[2] + 1) * HALF], ps[:, n % PB, :], ACT.Copy)\
                        .then_inc(S["ev_a"], 1)
            for n in range(NT + 1):
                if n < NT:
                    act.wait_ge(S["kt_done"], n + 1)
                    if n >= 1:
                        act.wait_ge(S["kv_done"], n)
                    act.activation(ktok[:, :, :, :].rearrange("p d a n -> p (d a n)"), ps[:, 4, :], ACT.Copy).then_inc(S["kt_ready"], 1)
                if 1 <= n <= NX:
                    m = group_no[("g", n - 1)]
                    ev(m)
                    if n == 1:
                        act.wait_ge(S["mrow_stored"], 16 * 8)
                    act.activation(gate[:, n - 1, :], ps[:, m % PB, :], ACT.Silu).then_inc(S["ev_a"], 1)
            act.wait_ge(S["proj_done"], len(groups))
            for t in range(NX):
                act.dma_start(x2[:, t, :], row_src(t)).then_inc(row_loaded[t], 16)
            for first, dst in ((0, g1b), (4, a2b), (2, s2b)):
                act.dma_start(dst, m_dram[first:first + 2, :].rearrange("(o k) p -> o (k p)", o=1).partition_broadcast(P))\
                    .then_inc(S["bcast_loaded"], 16)

            def turned_out(u, h):
                act.wait_ge(S["hx2_turned"], 2 * u + h + 1)
                if h == 0 and u >= 1:
                    act.wait_ge(S["logit_done"], u)
                act.activation(hx2T[:, h * HALF:(h + 1) * HALF], ps[:, 7, :], ACT.Copy).then_inc(S["hx2T_ready"], 1)

            def mixed_pool(g):
                for h in range(2):
                    act.wait_ge(S["mixp_done"], 2 * g + h + 1)
                    act.activation(uT[:, g, h * HALF:(h + 1) * HALF], ps[:, 5 + h, :], ACT.Copy,
                                   scale=small[:, 80 + g:81 + g]).then_inc(S["mixp_ready"], 1)

            for t in range(NX + 2):
                u = t - 2
                if t == 0:
                    mixed_pool(0)
                    mixed_pool(1)
                if t >= 2:
                    act.wait_ge(S["hx2_ready"], u + 1)
                    act.dma_start(hx_dram[u * P:(u + 1) * P, :], hx2[:, u % 2, :]).then_inc(hx2_stored[u % 2], 16)
                    turned_out(u, 0)
                if t < NX:
                    for h in range(2):
                        act.wait_ge(S["o_done"], t + 1)
                        act.activation(sqg[:, h, :], ps[:, 2 + h, 0:256], ACT.Square).then_inc(S["osq_ready"], 1)
                if t == 0:
                    mixed_pool(2)
                    mixed_pool(3)
                if t >= 2:
                    turned_out(u, 1)
                if t < NX:
                    act.wait_ge(S["ot_done"], t + 1)
                    act.activation(gate[:, t, :], ps[:, 4, :], ACT.Copy, scale=small[:, 84:85]).then_inc(S["mixg_ready"], 1)
                if t >= 2:
                    act.wait_ge(S["logit_done"], u + 1)
                    act.activation(rlT[:, :], ps[0:NE, 7, 0:P], ACT.Copy).then_inc(S["rl_ready"], 1)
                    act.wait_ge(S["rl_turned"], u + 1)
                    act.activation(logit[:, u, :], ps[:, 7, P:P + NE], ACT.Copy).then_inc(S["rl_out"], 1)
                if 1 <= t <= NX:
                    w = t - 1
                    act.wait_ge(S["x2_ready"], 2 * (w + 1))
                    if w >= 2:
                        act.wait_ge(hx2_stored[w % 2], 16 * (w // 2))
                    act.activation(hx2[:, w % 2, :], x2[:, w, :], ACT.Square, accum_out=stat[:, w:w + 1]).then_inc(S["ss2_ready"], 1)
                    for blk in (NE + w, NE + NX + w):
                        act.dma_start(y_dram[blk * P:(blk + 1) * P, :], x2[:, w, :]).then_inc(S["y_filled"], 16)
            act.wait_ge(S["rl_out"], NX)
            act.activation(rt["s"], logit[:, :, :], ACT.Sigmoid).then_inc(S["sig_ready"], 1)
            act.dma_start(g2b, m_dram[6:8, :].rearrange("(o k) p -> o (k p)", o=1).partition_broadcast(P))\
                .then_inc(S["g2_loaded"], 16)
            act.dma_start(nfb, norm_f.rearrange("(o n) -> o n", o=1).partition_broadcast(P)).then_inc(S["nf_loaded"], 16)
            act.wait_ge(S["table_ready"], 1)
            nb = act.value_load(tabs[0:1, T_NB:T_NB + 1], min_val=1, max_val=MAXB)

            def turn_out(b, slot):
                act.wait_ge(S["x_turned"], b + 3)
                act.activation(xT[:, slot, HALF:D], ps[:, 1, :], ACT.Copy).then_inc(S["xT_ready"], 1)

            turn_out(0, 0)
            act.wait_ge(S["y_filled"], 16 * 2 * NX)
            for par in range(2):
                act.sem_inc(y_stored[par], 16)
            with act.Fori(0, NB // 2) as pair:
                i = pair * 2
                for s in range(2):
                    with act.If(i + s < nb):
                        b = i + s
                        act.wait_ge(S["l1a"], b + 1)
                        act.activation(hsil[:, 0:256], ps[:, 2, 0:256], ACT.Silu).then_inc(S["silu_a"], 1)
                        turn_out(b + 1, 1 - s)
                        act.wait_ge(S["hta"], b + 1)
                        act.activation(hT[:, 0:2, :].rearrange("p k n -> p (k n)"), ps[:, 2, 0:256], ACT.Copy).then_inc(S["hT_a"], 1)
                        act.wait_ge(S["l1b"], b + 1)
                        act.activation(hsil[:, 256:512], ps[:, 4, 0:256], ACT.Silu).then_inc(S["silu_b"], 1)
                        act.wait_ge(S["htb"], b + 1)
                        act.activation(hT[:, 2:4, :].rearrange("p k n -> p (k n)"), ps[:, 4, 0:256], ACT.Copy).then_inc(S["hT_b"], 1)
                        act.wait_ge(S["y_ready"], 2 * i + (2 * s + 4))
                        act.dma_start(y_dram[bass.ds(b * P, P), :], ysb[:, s, :]).then_inc(y_stored[s], 16)
                    with act.Else():
                        act.sem_inc(y_stored[s], 16)
            for par in range(2):
                act.wait_ge(y_stored[par], 16 * NB // 2 + 16)
            for t in range(NX):
                act.wait_ge(S["fin_add"], 2 * (t + 1))
                if t >= 1:
                    act.wait_ge(S["fss_ready"], t)
                act.activation(sqf, x2[:, t, :], ACT.Square, accum_out=stat[:, t:t + 1]).then_inc(S["fss_ready"], 1)

        @block.vector
        def _(dve):
            dve.wait_ge(S["small_turned"], 1)
            dve.tensor_copy(small[:, :], ps[:, 7, 0:85]).then_inc(S["small_ready"], 1)
            for t in range(NT):
                dve.wait_ge(S["pow_ready"], t + 1)
                dve.tensor_scalar(rows[:, t, :], rows[:, t, :], stat[:, 2 * NT + t:2 * NT + t + 1], None, ALU.mult)\
                    .then_inc(S["scaled"], 1)
            dve.wait_ge(S["mod_turned"], 1)
            b_cols = small[:, 32:80].rearrange("p (s k) -> p s k", s=N_MOD)
            for w in range(2):
                dve.tensor_tensor(mod[:, 0:2, :, w], ps[:, 4, 0:32].rearrange("p (s k w) -> p s k w", s=2, w=2)[:, :, :, w],
                                  b_cols[:, 0:2, :], ALU.add).then_inc(S["mod_added"], 1)
            dve.wait_ge(S["mod_added"], 2)
            for w in range(2):
                dve.scalar_tensor_tensor(out=a1[:, :, w], in0=mod[:, 1, :, w], scalar=1.0, in1=small[:, 16:24],
                                         op0=ALU.add, op1=ALU.mult).then_inc(S["mod_ready"], 1)
            dve.wait_ge(S["mod_ready"], 2)
            for t in range(NT):
                which = 0 if t < NX else 1
                dve.wait_ge(S["turned"], t + 1)
                for k in range(4):
                    ins = dve.tensor_scalar(hxT[:, k, t * P:(t + 1) * P], ps[:, 2 * (t % 2), k * P:(k + 1) * P],
                                            a1[:, k, which:which + 1], mod[:, 0, k, which:which + 1], ALU.mult, ALU.add)
                ins.then_inc(S["hx_v"], 1)
            for g, (t0, n) in enumerate(tok_groups):
                dve.wait_ge(S["r_done"], g + 1)
                dve.tensor_copy(rT[0:32, t0 * P:(t0 + n) * P], ps[0:32, g, 0:n * P]).then_inc(S["rT_ready"], 1)
            sc = ("s_chain", [0])
            mc = ("m_chain", [0])

            def late_sum(i):
                w = unit_ready(dve, ("mod", 4 + i))
                for k in range(KC):
                    if k == 0:
                        ins = dve.tensor_scalar(macc, w[:, k, :], silu_c[:, k, 0:1], None, ALU.mult)
                    else:
                        ins = dve.scalar_tensor_tensor(out=macc, in0=w[:, k, :], scalar=silu_c[:, k, 0:1],
                                                       in1=macc, op0=ALU.mult, op1=ALU.add)
                    if k < KC - 1:
                        link(dve, mc, ins)
                ins.then_inc(S["macc_ready"], 1)

            def late_row(i):
                dve.wait_ge(S["mrow_done"], i + 1)
                dve.wait_ge(S["bmod_loaded"], 16 * (i + 1))
                if i >= 1:
                    dve.wait_ge(S["mrow_stored"], 16 * i)
                ins = dve.tensor_tensor(mrow, ps[0:1, 7, :], bmod_row, ALU.add)
                if i in (4, 5):
                    link(dve, mc, ins)
                    dve.wait_ge(S["n2_loaded"], 16 * (i - 3))
                    ins = dve.scalar_tensor_tensor(out=mrow, in0=mrow, scalar=1.0,
                                                   in1=norm2_row, op0=ALU.add, op1=ALU.mult)
                ins.then_inc(S["mrow_ready"], 1)

            def min_and_abs(t):
                dve.wait_ge(S["lg_done"], t + 1)
                dve.tensor_scalar(minl[:, t % 2, :], ps[:, 4, :], 0.0, None, ALU.min).then_inc(S["lg_min"], 1)
                dve.wait_ge(S["lg_min"], 2 * t + 1)
                dve.scalar_tensor_tensor(out=absl[:, t % 2, :], in0=minl[:, t % 2, :], scalar=-2.0, in1=ps[:, 4, :],
                                         op0=ALU.mult, op1=ALU.add).then_inc(S["lg_min"], 1)

            min_and_abs(0)
            for t in range(NT):
                if t + 1 < NT:
                    min_and_abs(t + 1)
                dve.wait_ge(S["lg_ln"], t + 1)
                if t >= 2:
                    dve.wait_ge(S["cum_done"], t - 1)
                dve.tensor_tensor(spl[:, t % 2, :], absl[:, t % 2, :], minl[:, t % 2, :], ALU.subtract).then_inc(S["sp_ready"], 1)
                if t % 2 == 1:
                    n = group_no[("v", t)]
                    dve.wait_ge(S["proj_done"], n + 1)
                    dve.tensor_copy(vals[:, t, :], ps[:, n % PB, :]).then_inc(S["ev_v"], 1)
                    if t >= 3:
                        late_row(t // 2 - 1)
                    late_sum(t // 2)
            def pool_steps():
                dve.wait_ge(S["pool_w_loaded"], 64)
                for g, w in enumerate(WINDOWS):
                    h = w // 2
                    for part in range(2):
                        dve.wait_ge(*evacuated(("u", g, part)))
                    link(dve, sc, dve.memset(boxa[:, 8 - h:8, :], 0.0))
                    link(dve, sc, dve.memset(boxa[:, 8 + GRID_H:8 + GRID_H + h, :], 0.0))
                    link(dve, sc, dve.tensor_copy(boxa[:, 8:8 + GRID_H, :], uT[:, g, :].rearrange("p (r w) -> p r w", w=GRID_W)))
                    yield
                    src, dst, L = boxa, boxb, 2
                    while L <= w:
                        lo, n = 8 - h, GRID_H + w - L
                        link(dve, sc, dve.tensor_tensor(dst[:, lo:lo + n, :], src[:, lo:lo + n, :],
                                                        src[:, lo + L // 2:lo + L // 2 + n, :], ALU.add))
                        src, dst, L = dst, src, 2 * L
                        yield
                    wide, wide2 = (b.rearrange("p r w -> p (r w)")[:, 0:GRID_H * 80].rearrange("p (r w) -> p r w", w=80)
                                   for b in (dst, src))
                    link(dve, sc, dve.memset(wide[:, :, 8 - h:8], 0.0))
                    link(dve, sc, dve.memset(wide[:, :, 8 + GRID_W:8 + GRID_W + h], 0.0))
                    link(dve, sc, dve.tensor_tensor(
                        wide[:, :, 8:8 + GRID_W], src[:, 8 - h:8 - h + GRID_H, :],
                        icnt[:, g, 0:GRID_H].unsqueeze(2).broadcast_to([P, GRID_H, GRID_W]), ALU.mult))
                    yield
                    src, dst, L = wide, wide2, 2
                    while L <= w:
                        lo, n = 8 - h, GRID_W + w - L
                        link(dve, sc, dve.tensor_tensor(dst[:, :, lo:lo + n], src[:, :, lo:lo + n],
                                                        src[:, :, lo + L // 2:lo + L // 2 + n], ALU.add))
                        src, dst, L = dst, src, 2 * L
                        yield
                    link(dve, sc, dve.tensor_tensor(
                        dst[:, :, 0:GRID_W], src[:, :, 8 - h:8 - h + GRID_W],
                        icnt[:, g, GRID_H:].unsqueeze(1).broadcast_to([P, GRID_H, GRID_W]), ALU.mult))
                    ug = uT[:, g, :].rearrange("p (r w) -> p r w", w=GRID_W)
                    dve.tensor_tensor(ug, dst[:, :, 0:GRID_W], ug, ALU.subtract).then_inc(S["pooled"], 1)
                    dve.wait_ge(S["pooled"], g + 1)
                    yield

            pooling = pool_steps()
            for i in range(4, 8):
                late_row(i)
                if i < 7:
                    late_sum(i + 1)
                for _ in range(3):
                    next(pooling, None)
            dve.wait_ge(S["cum_read"], NT)
            for n, g in enumerate(groups):
                if g[0] in "kq":
                    a, gr = g[1], g[2]
                    t0, m = tok_groups[gr]
                    dve.wait_ge(S["proj_done"], n + 1)
                    for d in range(2):
                        proj_out = ps[:, n % PB, 0:m * P].rearrange("p (t i) -> p t i", i=P)
                        if g[0] == "k":
                            kd = kdec[:, t0:t0 + m, d, a, :]
                            ins = dve.tensor_tensor(kd, proj_out, kd, ALU.mult)
                        else:
                            qd = qdec[:, t0:t0 + m, d, a, :]
                            ins = dve.scalar_tensor_tensor(out=qd, in0=proj_out, scalar=DK ** -0.5, in1=qd,
                                                           op0=ALU.mult, op1=ALU.mult)
                    ins.then_inc(S["ev_v"], 1)
                    for _ in range(3):
                        next(pooling, None)
            link(dve, sc, dve.tensor_tensor(dec[:, :, :, :].rearrange("p t d a -> p (t d a)"), dec1[:, :, :, :].rearrange("p t d a -> p (t d a)"),
                                            dec2[:, :, :, :].rearrange("p t d a -> p (t d a)"), ALU.mult))

            for n, tt in enumerate(steps()):
                if n >= 1:
                    dve.wait_ge(S["state_step"], n)
                for d in range(2):
                    t = tt[d]
                    for a in range(2):
                        if n >= NCT:
                            ins = dve.tensor_scalar(state_in[:, t, d, a, :], state[:, d, a, :], dec1[:, t, d, a:a + 1], None, ALU.mult)
                            ins.then_inc(S["state_saved"], 1)
                if n >= 1:
                    for d in range(2):
                        for a in range(2):
                            ins = dve.tensor_scalar(state[:, d, a, :], state[:, d, a, :], dec[:, tt[d], d, a:a + 1], None, ALU.mult)
                    link(dve, sc, ins)
                dve.wait_ge(S["kv_done"], n + 1)
                for d in range(2):
                    t = tt[d]
                    for a in range(2):
                        kv = ps[:, 5, (2 * d + a) * P:(2 * d + a + 1) * P]
                        if n >= 1:
                            ins = dve.scalar_tensor_tensor(out=state[:, d, a, :], in0=kv, scalar=dec2[:, t, d, a:a + 1],
                                                           in1=state[:, d, a, :], op0=ALU.mult, op1=ALU.add)
                        else:
                            ins = dve.tensor_scalar(state[:, d, a, :], kv, dec2[:, t, d, a:a + 1], None, ALU.mult)
                ins.then_inc(S["state_step"], 1)
                next(pooling, None)
            for _ in pooling:
                pass
            def residual(u, h):
                cols = slice(h * HALF, (h + 1) * HALF)
                dve.wait_ge(S["y_done"], 2 * u + h + 1)
                dve.tensor_tensor(hx2[:, u % 2, cols], ps[:, 5 + h, :], g1b[:, cols], ALU.mult).then_inc(S["gated"], 1)
                dve.wait_ge(S["gated"], 2 * u + h + 1)
                dve.tensor_tensor(x2[:, u, cols], x2[:, u, cols], hx2[:, u % 2, cols], ALU.add).then_inc(S["x2_ready"], 1)

            for t in range(NX + 1):
                u = t - 1
                if t < NX:
                    dve.wait_ge(S["sc_done"], t + 1)
                    for h in range(2):
                        dve.tensor_tensor(smask[:, h].rearrange("p d (a i) -> p d a i", a=2), ps[:, h, :].rearrange("p (d a i) -> p d a i", d=2, a=2),
                                          mask[:, :, :].unsqueeze(2).broadcast_to([P, 2, 2, P]), ALU.mult).then_inc(S["sc_masked"], 1)
                    dve.wait_ge(S["sc_masked"], 2 * t + 2)
                    if t >= 1:
                        dve.wait_ge(S["o_done"], t)
                    dve.tensor_tensor(ssum, smask[:, :, 0, :], smask[:, :, 1, :], ALU.add).then_inc(S["s_summed"], 1)
                if t >= 1:
                    if u == 0:
                        dve.wait_ge(S["bcast_loaded"], 48)
                    dve.wait_ge(row_loaded[u], 32)
                    if u >= 2:
                        dve.wait_ge(hx2_stored[u % 2], 16 * (u // 2))
                        dve.wait_ge(S["hx2_turned"], 2 * (u - 1))
                    residual(u, 0)
                if t < NX:
                    dve.wait_ge(S["osq_ready"], 2 * t + 2)
                    dve.tensor_reduce(ost[:, 0:4], sqg.rearrange("p h (a n) -> p (h a) n", a=2), AX.X, ALU.add).then_inc(S["oss_ready"], 1)
                    dve.wait_ge(S["opow_ready"], t + 1)
                    if t >= 1:
                        dve.wait_ge(S["ot_done"], t)
                    on = onorm.rearrange("p (a h n) -> p a h n", a=2, h=2)
                    for h in range(2):
                        dve.tensor_tensor(on[:, :, h, :], ps[:, 2 + h, 0:256].rearrange("p (a n) -> p a n", a=2),
                                          ost[:, 8 + 2 * h:10 + 2 * h].unsqueeze(2).broadcast_to([P, 2, DV]), ALU.mult).then_inc(S["on_ready"], 1)
                    dve.wait_ge(S["on_ready"], 2 * t + 2)
                    dve.tensor_tensor(onorm, onorm, gate[:, t, :], ALU.mult).then_inc(S["og_ready"], 1)
                if t >= 1:
                    residual(u, 1)
                    dve.wait_ge(S["pow2_ready"], u + 1)
                    link(dve, sc, dve.scalar_tensor_tensor(out=hx2[:, u % 2, :], in0=x2[:, u, :], scalar=stat[:, 2 * NT + u:2 * NT + u + 1],
                                                           in1=a2b, op0=ALU.mult, op1=ALU.mult))
                    dve.tensor_tensor(hx2[:, u % 2, :], hx2[:, u % 2, :], s2b, ALU.add).then_inc(S["hx2_ready"], 1)
            rc = ("r_chain", [0])
            v = lambda ins: link(dve, rc, ins)
            R = rt
            dve.wait_ge(S["rl_out"], NX)
            for n in ("sel", "pre", "pre2"):
                dve.memset(R[n][:, 0:4, :], 0.0)
            dve.memset(R["cb"][:, :, 0:8], 0.0)
            v(dve.memset(R["cb2"][:, :, 0:8], 0.0))
            dve.wait_ge(S["sig_ready"], 1)
            v(dve.tensor_tensor(R["sbias"], R["s"], bias_b[:, :].unsqueeze(1).broadcast_to([P, NX, NE]), ALU.add))
            G = R["sbias"].rearrange("p t (g j) -> p (t g) j", j=4)
            v(dve.tensor_tensor(R["hi"], G[:, :, 0:2], G[:, :, 2:4], ALU.max))
            v(dve.tensor_tensor(R["lo"], G[:, :, 0:2], G[:, :, 2:4], ALU.min))
            v(dve.tensor_tensor(R["t1"], R["hi"][:, :, 0:1], R["hi"][:, :, 1:2], ALU.max))
            v(dve.tensor_tensor(R["t2"], R["hi"][:, :, 0:1], R["hi"][:, :, 1:2], ALU.min))
            v(dve.tensor_tensor(R["hi"][:, :, 0:1], R["lo"][:, :, 0:1], R["lo"][:, :, 1:2], ALU.max))
            v(dve.tensor_tensor(R["t2"], R["t2"], R["hi"][:, :, 0:1], ALU.max))
            v(dve.tensor_tensor(R["t1"], R["t1"], R["t2"], ALU.add))
            gsc = R["t1"].rearrange("p (t g) o -> p t (g o)", g=NGR)

            def first_best(oh, values, eq, weights, shape):
                v(dve.tensor_reduce(R["mx"], values, AX.X, ALU.max))
                v(dve.tensor_tensor(eq, values, R["mx"].broadcast_to(shape), ALU.is_equal))
                v(dve.tensor_tensor(eq, eq, weights.unsqueeze(1).broadcast_to(shape), ALU.mult))
                v(dve.tensor_reduce(R["mx"], eq, AX.X, ALU.max))
                v(dve.tensor_tensor(oh, eq, R["mx"].broadcast_to(shape), ALU.is_equal))

            first_best(R["goh"], gsc, R["geq"], iota_e[:, NE - NGR:NE], [P, NX, NGR])
            mb4 = R["mb"].rearrange("p t (g j) -> p (t g) j", j=4)
            goh = R["goh"].rearrange("p t g -> p (t g)").unsqueeze(2).broadcast_to([P, NX * NGR, 4])
            v(dve.tensor_tensor(mb4, G, goh, ALU.mult))
            v(dve.tensor_scalar(R["goh"], R["goh"], BIG, -BIG, ALU.mult, ALU.add))
            v(dve.tensor_tensor(mb4, mb4, goh, ALU.add))
            first_best(R["oh1"], R["mb"], R["eq"], iota_e[:, :], [P, NX, NE])
            v(dve.scalar_tensor_tensor(out=R["mb"], in0=R["oh1"], scalar=-BIG, in1=R["mb"], op0=ALU.mult, op1=ALU.add))
            first_best(R["oh2"], R["mb"], R["eq"], iota_e[:, :], [P, NX, NE])
            v(dve.tensor_tensor(R["sel"][:, 4:, :], R["oh1"], R["oh2"], ALU.add))
            for src, dst, sh in (("sel", "pre", 1), ("pre", "pre2", 2), ("pre2", "pre", 4)):
                v(dve.tensor_tensor(R[dst][:, 4:, :], R[src][:, 4:, :], R[src][:, 4 - sh:4 + NX - sh, :], ALU.add))
            dve.sem_inc(S["route_ready"], 1)
            for k, oh in enumerate(("oh1", "oh2")):
                v(dve.tensor_tensor(R["eq"], R["s"], R[oh], ALU.mult))
                v(dve.tensor_reduce(R["s12"][:, k, :], R["eq"], AX.X, ALU.add))
            v(dve.tensor_tensor(R["ssum"].rearrange("p t o -> p (t o)"), R["s12"][:, 0, :], R["s12"][:, 1, :], ALU.add))
            v(dve.reciprocal(R["ssum"], R["ssum"]))
            v(dve.tensor_tensor(R["wk"], R["s12"], R["ssum"].rearrange("p t o -> p (o t)").unsqueeze(1).broadcast_to([P, 2, NX]), ALU.mult))
            dve.wait_ge(S["rank_done"], 1)
            v(dve.tensor_copy(R["rank"].rearrange("p t e -> p (t e)"), ps[:, 7, 0:NTE]))
            v(dve.tensor_copy(R["tot"].rearrange("p o e -> p (o e)"), ps[:, 7, NTE:NTE + NE]))
            v(dve.tensor_tensor(cmp16[:, :, :], R["tot"].rearrange("p o e -> p (o e)").unsqueeze(2).broadcast_to([P, NE, KC]),
                                thresh[:, :].unsqueeze(1).broadcast_to([P, NE, KC]), ALU.is_gt))
            nbl = R["nbl"].rearrange("p o e -> p (o e)")
            v(dve.tensor_reduce(nbl, cmp16[:, :, :], AX.X, ALU.add))
            v(dve.tensor_scalar(nbl, nbl, 1.0, None, ALU.max))
            cb, cb2 = (R[n].rearrange("p o e -> p (o e)") for n in ("cb", "cb2"))
            v(dve.tensor_copy(cb[:, 8:], nbl))
            for sh in (1, 2, 4, 8):
                v(dve.tensor_tensor(cb2[:, 8:], cb[:, 8:], cb[:, 8 - sh:8 + NE - sh], ALU.add))
                cb, cb2 = cb2, cb
            first = R["base"].rearrange("p o e -> p (o e)")
            v(dve.tensor_tensor(first, cb[:, 8:], nbl, ALU.subtract))

            def tables():
                v(dve.tensor_copy(tabs[:, T_FIRST:T_FIRST + NE], first))
                v(dve.tensor_copy(tabs[:, T_NB:T_NB + 1], cb[:, 8 + NE - 1:8 + NE]))
                v(dve.tensor_tensor(cmpb, iota_p[:, 0:NB].unsqueeze(2).broadcast_to([P, NB, NE]),
                                    cb[:, 8:].unsqueeze(1).broadcast_to([P, NB, NE]), ALU.is_ge))
                v(dve.tensor_reduce(ebf[:, :], cmpb, AX.X, ALU.add))
                v(dve.tensor_scalar(tabs[:, T_E:T_E + NB], ebf[:, :], float(NE - 1), None, ALU.min))
                v(dve.tensor_scalar(tabs[:, T_PAR:T_PAR + NB], tabs[:, T_E:T_E + NB], 1, 1, ALU.bitwise_and, ALU.bitwise_xor))
                v(dve.tensor_scalar(tabs[:, T_EVEN:T_EVEN + NB], ebf[:, :], float(NE - 1), 2.0, ALU.min, ALU.add))
                v(dve.tensor_scalar(tabs[:, T_ODD:T_ODD + NB], ebf[:, :], float(NE - 1), 1.0, ALU.min, ALU.add))
                v(dve.tensor_scalar(tabs[:, T_EVEN:T_EVEN + 2 * NB], tabs[:, T_EVEN:T_EVEN + 2 * NB], 1, None,
                                    ALU.logical_shift_right))

            v(dve.scalar_tensor_tensor(out=R["rank"], in0=R["base"].broadcast_to([P, NX, NE]), scalar=float(P), in1=R["rank"],
                                       op0=ALU.mult, op1=ALU.add))
            for k, oh in enumerate(("oh1", "oh2")):
                v(dve.tensor_tensor(R["eq"], R["rank"], R[oh], ALU.mult))
                v(dve.tensor_reduce(R["dest"][:, k, :], R["eq"], AX.X, ALU.add))
            v(dve.tensor_copy(desti[:, :, :], R["dest"]))
            v(dve.tensor_scalar(blki[:, :, :], desti[:, :, :], 7, None, ALU.logical_shift_right))
            v(dve.tensor_scalar(posi[:, :, :], desti[:, :, :], P - 1, None, ALU.bitwise_and))
            v(dve.tensor_copy(R["blkf"], blki[:, :, :]))
            v(dve.tensor_copy(R["posf"], posi[:, :, :]))
            for k in range(2):
                here = slice(k * NX, (k + 1) * NX)
                blk, is_blk = R["blkf"][:, k, :].unsqueeze(2).broadcast_to([P, NX, NB]), slotv[:, here, 1, :]
                v(dve.tensor_tensor(is_blk, iota_p[:, 0:NB].unsqueeze(1).broadcast_to([P, NX, NB]), blk, ALU.is_equal))
                v(dve.tensor_tensor(slotv[:, here, 0, :], is_blk, tokid[:, :].unsqueeze(2).broadcast_to([P, NX, NB]), ALU.mult))
                v(dve.tensor_tensor(is_blk, is_blk, R["wk"][:, k, :].unsqueeze(2).broadcast_to([P, NX, NB]), ALU.mult))
                dve.tensor_tensor(onehot[:, here, :], iota_p[:, :].unsqueeze(1).broadcast_to([P, NX, P]),
                                  R["posf"][:, k, :].unsqueeze(2).broadcast_to([P, NX, P]), ALU.is_equal).then_inc(S["slots_done"], 1)
            tables()
            dve.wait_ge(S["rank_done"], 2)
            v(dve.tensor_copy(slot_tok[:, 0:NB], ps[:, 6, 256:256 + NB]))
            dve.tensor_copy(slot_w[:, :], ps[:, 6, 256 + NB:256 + 2 * NB]).then_inc(S["table_ready"], 1)
            dve.wait_ge(S["table_ready"], 1)
            nb = dve.value_load(tabs[0:1, T_NB:T_NB + 1], min_val=1, max_val=MAXB)

            def turn_out(b, slot):
                dve.wait_ge(S["x_turned"], b + 3)
                dve.tensor_copy(xT[:, slot, 0:HALF], ps[:, 0, :]).then_inc(S["xT_ready_v"], 1)

            turn_out(0, 0)
            dve.wait_ge(S["g2_loaded"], 16)
            with dve.Fori(0, NB // 2) as pair:
                i = pair * 2
                for s in range(2):
                    with dve.If(i + s < nb):
                        b = i + s
                        dve.wait_ge(S["silu_a"], b + 1)
                        dve.tensor_tensor(hid[:, 0:256], hsil[:, 0:256], ps[:, 3, 0:256], ALU.mult).then_inc(S["hid_a"], 1)
                        turn_out(b + 1, 1 - s)
                        dve.wait_ge(S["silu_b"], b + 1)
                        dve.tensor_tensor(hid[:, 256:512], hsil[:, 256:512], ps[:, 5, 0:256], ALU.mult).then_inc(S["hid_b"], 1)
                        dve.wait_ge(S["l2_done"], b + 1)
                        dve.wait_ge(y_stored[s], 16 * pair + 16)
                        for h in range(2):
                            cols = slice(h * HALF, (h + 1) * HALF)
                            dve.scalar_tensor_tensor(out=ysb[:, s, cols], in0=ps[:, 6 + h, :], scalar=slot_w[:, bass.ds(b, 1)],
                                                     in1=g2b[:, cols], op0=ALU.mult, op1=ALU.mult).then_inc(S["y_ready"], 1)
            for t in range(NX + 1):
                if t < NX:
                    dve.wait_ge(fin_loaded[t % 2], 32 * (t // 2 + 1))
                    for k, buf in enumerate((y1, y2)):
                        dve.tensor_tensor(x2[:, t, :], x2[:, t, :], buf[:, t % 2, :], ALU.add).then_inc(S["fin_add"], 1)
                        dve.wait_ge(S["fin_add"], 2 * t + k + 1)
                if t >= 1:
                    u = t - 1
                    dve.wait_ge(S["fpow_ready"], u + 1)
                    if u == 0:
                        dve.wait_ge(S["nf_loaded"], 16)
                    if u >= 2:
                        dve.wait_ge(stored[u % 2], 16 * (u // 2))
                    dve.scalar_tensor_tensor(out=fin[:, u % 2, :], in0=x2[:, u, :], scalar=stat[:, 2 * NT + u:2 * NT + u + 1],
                                             in1=nfb, op0=ALU.mult, op1=ALU.mult).then_inc(S["fout_ready"], 1)

        @block.tensor
        def _(pe):
            pe.wait_ge(S["small_loaded"], 16 * 7)
            pe.wait_ge(S["consts"], 23)
            pe.transpose(ps[:, 7, 0:85], small_rows[:, :], ident[0:85, 0:85]).then_inc(S["small_turned"], 1)

            def turn_rows(t):
                pe.wait_ge(S["scaled"], t + 1)
                if t >= 2:
                    pe.wait_ge(S["hx_a"], t - 1)
                    pe.wait_ge(S["hx_v"], t - 1)
                for k in range(KC):
                    ins = pe.transpose(ps[:, 2 * (t % 2) + k // 4, (k % 4) * P:(k % 4 + 1) * P],
                                       rows[:, t, k * P:(k + 1) * P], ident[:, :])
                ins.then_inc(S["turned"], 1)

            def modulation(j):
                w = unit_ready(pe, ("mod", j))
                if j == 3:
                    pe.wait_ge(S["small_ready"], 1)
                for k in range(KC):
                    ins = pe.matmul(ps[0:2, 4 + j, :], silu_c[:, k, :], w[:, k, :], start=(k == 0), stop=(k == KC - 1))
                ins.then_inc(S["mod_used"], 1)

            def turn_mod(j):
                pe.wait_ge(S["mod_row"], j + 1)
                for m in range(4):
                    col = 8 * j + 2 * m
                    ins = pe.transpose(ps[:, 4, col:col + 2], mod_rows[:, j * HALF + m * P:j * HALF + (m + 1) * P], ident[0:2, 0:2])
                if j == 3:
                    ins.then_inc(S["mod_turned"], 1)

            turn_rows(0)
            turn_rows(1)
            pe.wait_ge(S["silu_ready"], 1)
            for j in range(4):
                modulation(j)
                if j >= 1:
                    turn_mod(j - 1)
            turn_mod(3)
            for t in range(2, NT):
                turn_rows(t)

            pe.wait_ge(S["rw_loaded"], 16)
            for g, (t0, n) in enumerate(tok_groups):
                pe.wait_ge(S["hx_a"], NT)
                pe.wait_ge(S["hx_v"], NT)
                for k in range(KC):
                    ins = pe.matmul(ps[0:32, g, 0:n * P], w_r[:, k, :], hxT[:, k, t0 * P:(t0 + n) * P],
                                    start=(k == 0), stop=(k == KC - 1))
                ins.then_inc(S["r_done"], 1)
            pe.wait_ge(S["rT_ready"], 3)
            pe.wait_ge(S["gk_loaded"], 48)

            def proj(n):
                g = groups[n]
                if n >= PB:
                    s, v = evac[n - PB]
                    pe.wait_ge(S[s], v)
                bank = n % PB
                if g[0] in "vg":
                    w = unit_ready(pe, (g[0], 0))
                    for k in range(KC):
                        ins = pe.matmul(ps[:, bank, :], hxT[:, k, g[1] * P:(g[1] + 1) * P], w[:, k, :],
                                        start=(k == 0), stop=(k == KC - 1))
                else:
                    kind, a, gr = g
                    w = unit_ready(pe, ("u" if kind == "u" else "qk", 0))
                    col = {"q": 0, "k": QK, "u": 0}[kind] + a * P
                    t0, m = tok_groups[gr]
                    for k in range(KC):
                        ins = pe.matmul(ps[:, bank, 0:m * P], w[:, k, col:col + P], hxT[:, k, t0 * P:(t0 + m) * P],
                                        start=(k == 0), stop=(k == KC - 1))
                ins.then_inc(S["proj_done"], 1)

            def logits(t):
                if t >= 1:
                    pe.wait_ge(S["lg_min"], 2 * t)
                pe.matmul(ps[:, 4, :], rT[:, t * P:(t + 1) * P], w_gk[:, :, :].rearrange("p d n -> p (d n)"),
                          start=True, stop=True).then_inc(S["lg_done"], 1)

            def cumulate(t):
                pe.wait_ge(S["sp_ready"], t + 1)
                if t >= 1:
                    pe.wait_ge(S["cum_read"], t)
                for d in range(2):
                    for a in range(2):
                        col = (2 * d + a) * P
                        ins = pe.matmul(ps[:, 5 + d, a * (P + 1):(a + 1) * (P + 1)], spl[:, t % 2, col:col + P], tri[:, d, :],
                                        start=True, stop=True)
                ins.then_inc(S["cum_done"], 1)

            def late_turn(i):
                pe.wait_ge(S["macc_ready"], i + 1)
                if i >= 1:
                    pe.wait_ge(S["mrow_ready"], i)
                pe.matmul(ps[0:1, 7, :], ones[:, 0:1], macc, start=True, stop=True).then_inc(S["mrow_done"], 1)

            logits(0)
            logits(1)
            for t in range(NT):
                proj(t)
                cumulate(t)
                if t + 2 < NT:
                    logits(t + 2)
                if t >= 2 and t % 2 == 0:
                    late_turn(t // 2 - 1)
            for n in range(NT, group_no[("g", 0)]):
                proj(n)
                if n < NT + 8 and n % 2 == 1:
                    late_turn(4 + (n - NT) // 2)

            def turn_k(n):
                pe.wait_ge(S["ev_v"], nv)
                for d in range(2):
                    for a in range(2):
                        ins = pe.transpose(ps[:, 4, (2 * d + a) * P:(2 * d + a + 1) * P], kdec[:, steps()[n][d], d, a, :], ident[:, :])
                ins.then_inc(S["kt_done"], 1)

            turn_k(0)
            for n, tt in enumerate(steps()):
                pe.wait_ge(S["kt_ready"], n + 1)
                if n >= 1:
                    pe.wait_ge(S["state_step"], n)
                for d in range(2):
                    for a in range(2):
                        for h in range(2):
                            head = 2 * a + h
                            ins = pe.matmul(ps[DK * h:DK * h + DK, 5, (2 * d + a) * P:(2 * d + a + 1) * P],
                                            ktok[:, d, a, DK * h:DK * h + DK], vals[:, tt[d], head * DV:(head + 1) * DV],
                                            start=True, stop=True)
                ins.then_inc(S["kv_done"], 1)
                if n + 1 < NT:
                    turn_k(n + 1)
                if n < NX:
                    proj(group_no[("g", n)])
            pe.wait_ge(S["kt_ready"], NT)
            pe.wait_ge(S["state_step"], NT)
            pe.wait_ge(S["ev_a"], na)
            pe.wait_ge(S["mrow_ready"], 8)

            def mix_pooled(g):
                pe.wait_ge(S["pooled"], g + 1)
                for h in range(2):
                    if g >= 1:
                        pe.wait_ge(S["mixp_ready"], 2 * (g - 1) + h + 1)
                    pe.matmul(ps[:, 5 + h, :], wp[:, g, :], uT[:, g, h * HALF:(h + 1) * HALF], start=True, stop=True)\
                        .then_inc(S["mixp_done"], 1)

            def scores(t):
                if t >= 1:
                    pe.wait_ge(S["sc_masked"], 2 * t)
                for h in range(2):
                    r = slice(DK * h, DK * h + DK)
                    for d in range(2):
                        for a in range(2):
                            ins = pe.matmul(ps[:, h, (2 * d + a) * P:(2 * d + a + 1) * P], kdec[r, t, d, a, :], qdec[r, t, d, a, :],
                                            start=True, stop=True)
                ins.then_inc(S["sc_done"], 1)

            def outputs(t):
                pe.wait_ge(S["s_summed"], t + 1)
                if t >= 1:
                    pe.wait_ge(S["on_ready"], 2 * t)
                for h in range(2):
                    r = slice(DK * h, DK * h + DK)
                    for a in range(2):
                        head = 2 * a + h
                        o = ps[:, 2 + h, a * DV:(a + 1) * DV]
                        pe.matmul(o, ssum[:, h, a * P:(a + 1) * P], vals[:, t, head * DV:(head + 1) * DV], start=True, stop=False)
                        for d in range(2):
                            ins = pe.matmul(o, qdec[r, t, d, a, :], state_in[r, t, d, a, :], start=False, stop=(d == 1))
                ins.then_inc(S["o_done"], 1)

            def turn_outputs(t):
                pe.wait_ge(S["og_ready"], t + 1)
                if t >= 1:
                    pe.wait_ge(S["mixg_ready"], t)
                for h in range(HEADS):
                    ins = pe.transpose(ps[:, 4, h * P:(h + 1) * P], onorm[:, h * DV:(h + 1) * DV], ident[:, :])
                ins.then_inc(S["ot_done"], 1)

            def project_out(t, h):
                w = unit_ready(pe, ("out", h))
                if h == 0:
                    pe.wait_ge(S["mixg_ready"], t + 1)
                    if t == 0:
                        pe.wait_ge(S["mixp_ready"], 2 * NG)
                if t >= 1:
                    pe.wait_ge(S["gated"], 2 * (t - 1) + h + 1)
                for k in range(KC):
                    m = uT[:, k, t * P:(t + 1) * P] if k < NG else gate[:, t, (k - NG) * P:(k - NG + 1) * P]
                    ins = pe.matmul(ps[:, 5 + h, :], m, w[:, k, :], start=(k == 0), stop=(k == KC - 1))
                ins.then_inc(S["y_done"], 1)

            def turn_normed(u, h):
                if h == 0:
                    pe.wait_ge(S["hx2_ready"], u + 1)
                    if u >= 1:
                        pe.wait_ge(S["rl_out"], u)
                else:
                    pe.wait_ge(S["hx2T_ready"], 2 * u + 1)
                for k in range(4):
                    ins = pe.transpose(ps[:, 7, k * P:(k + 1) * P], hx2[:, u % 2, (4 * h + k) * P:(4 * h + k + 1) * P], ident[:, :])
                ins.then_inc(S["hx2_turned"], 1)

            def router(u):
                pe.wait_ge(S["hx2T_ready"], 2 * u + 2)
                for k in range(KC):
                    ins = pe.matmul(ps[0:NE, 7, 0:P], w_rt[:, k, :], hx2T[:, k * P:(k + 1) * P],
                                    start=(k == 0), stop=(k == KC - 1))
                ins.then_inc(S["logit_done"], 1)

            def turn_logits(u):
                pe.wait_ge(S["rl_ready"], u + 1)
                pe.transpose(ps[:, 7, P:P + NE], rlT[:, :], ident[0:NE, 0:NE]).then_inc(S["rl_turned"], 1)

            for t in range(NX + 2):
                if t < NX:
                    scores(t)
                if t == 0:
                    mix_pooled(0)
                    mix_pooled(1)
                if t >= 2:
                    turn_normed(t - 2, 0)
                if 1 <= t <= NX:
                    project_out(t - 1, 0)
                if t < NX:
                    outputs(t)
                if t >= 2:
                    turn_normed(t - 2, 1)
                if 1 <= t <= NX:
                    project_out(t - 1, 1)
                if t == 0:
                    mix_pooled(2)
                    mix_pooled(3)
                if t < NX:
                    turn_outputs(t)
                if t >= 2:
                    router(t - 2)
                    turn_logits(t - 2)
            pe.wait_ge(S["route_ready"], 1)
            pre = rt["pre"][:, 3:, :].rearrange("p t e -> p (t e)")
            pe.matmul(ps[:, 7, 0:NTE], strict[:, :], rt["sel"][:, 4:, :].rearrange("p t e -> p (t e)"), start=True, stop=False)
            pe.matmul(ps[:, 7, 0:NTE], ones[:, :], pre[:, 0:NTE], start=False, stop=True)
            pe.matmul(ps[:, 7, NTE:NTE + NE], ones[:, :], pre[:, NTE:NTE + NE], start=True, stop=True).then_inc(S["rank_done"], 1)
            for n in range(2 * NX):
                if n % NX == 0:
                    pe.wait_ge(S["slots_done"], n // NX + 1)
                ins = pe.matmul(ps[:, 6, 256:256 + 2 * NB], onehot[:, n, :], slotv[:, n].rearrange("p w b -> p (w b)"),
                                start=(n == 0), stop=(n == 2 * NX - 1))
            ins.then_inc(S["rank_done"], 1)
            pe.wait_ge(S["table_ready"], 1)
            nb = pe.value_load(tabs[0:1, T_NB:T_NB + 1], min_val=1, max_val=MAXB)
            pe.sem_inc(S["x_turned"], 2)
            pe.sem_inc(S["hT_a"], 1)
            pe.sem_inc(S["hT_b"], 1)
            pe.sem_inc(S["hid_a"], 1)
            pe.sem_inc(S["hid_b"], 1)
            pe.sem_inc(S["y_ready"], 2)

            def turn_block(b, slot, gathers, slot_before=True):
                pe.wait_ge(gathered[slot], 16 * gathers)
                if slot_before:
                    pe.wait_ge(S["xT_ready"], b)
                    pe.wait_ge(S["xT_ready_v"], b)
                for k in range(KC):
                    ins = pe.transpose(ps[:, k // 4, (k % 4) * P:(k % 4 + 1) * P], xg[:, slot, k * P:(k + 1) * P], ident[:, :])
                ins.then_inc(S["x_turned"], 1)

            turn_block(0, 0, 1, slot_before=False)
            with pe.Fori(0, NB // 2) as pair:
                i = pair * 2
                for s in range(2):
                    with pe.If(i + s < nb):
                        b = i + s
                        loads = [pe.value_load(tabs[0:1, bass.ds(b + at_, 1)], min_val=0, max_val=NE // 2)
                                 for at_ in (T_EVEN, T_ODD)]
                        half = pe.value_load(tabs[0:1, bass.ds(b + T_PAR, 1)], min_val=0, max_val=1)
                        base = half * O_Q

                        def first(q, banks, done):
                            for k in range(KC):
                                lhs = xT[:, s, k * P:(k + 1) * P]
                                for i3, bank in enumerate(banks):
                                    ins = pe.matmul(ps[:, bank, 0:256], lhs,
                                                    arena[:, bass.ds(base + (i3 * UNIT + k * HALF + q * 256), 256)],
                                                    start=(k == 0), stop=(k == KC - 1))
                                if q == 1 and k == 3:
                                    pe.wait_ge(S["hid_a"], b + 2)
                                    for m in range(2):
                                        h_ins = pe.transpose(ps[:, 2, m * P:(m + 1) * P], hid[:, m * P:(m + 1) * P], ident[:, :])
                                    h_ins.then_inc(S["hta"], 1)
                            ins.then_inc(S[done], 1)

                        def second(k, h):
                            return pe.matmul(ps[:, 6 + h, :], hT[:, k, :],
                                             arena[:, bass.ds(base + (2 * UNIT + k * D + h * HALF), HALF)],
                                             start=(k == 0), stop=(k == 3))

                        pe.wait_ge(S["xT_ready"], b + 1)
                        pe.wait_ge(S["xT_ready_v"], b + 1)
                        for par in range(2):
                            pe.wait_ge(moe_w13[par], 32 * loads[par] + 32)
                        pe.wait_ge(S["hT_a"], b + 1)
                        pe.wait_ge(S["hid_a"], b + 1)
                        first(0, (2, 3), "l1a")
                        turn_block(b + 1, 1 - s, pair + (s + 1))
                        pe.wait_ge(S["hT_b"], b + 1)
                        pe.wait_ge(S["hid_b"], b + 1)
                        first(1, (4, 5), "l1b")
                        for par in range(2):
                            pe.wait_ge(moe_w2[par], 16 * loads[par] + 16)
                        pe.wait_ge(S["hT_a"], b + 2)
                        pe.wait_ge(S["y_ready"], 2 * i + (2 * s + 2))
                        second(0, 0)
                        second(0, 1)
                        second(1, 0)
                        pe.wait_ge(S["hid_b"], b + 2)
                        for m in range(2):
                            ins = pe.transpose(ps[:, 4, m * P:(m + 1) * P], hid[:, (2 + m) * P:(3 + m) * P], ident[:, :])
                        ins.then_inc(S["htb"], 1)
                        second(1, 1)
                        pe.wait_ge(S["hT_b"], b + 2)
                        for k in (2, 3):
                            for h in range(2):
                                ins = second(k, h)
                        ins.then_inc(S["l2_done"], 1)


_INS = ["x", "c", "ctx", "c_ctx", "w_mod", "b_mod", "norm1", "norm2", "w_in", "w_gk2", "b_gk", "w_pool",
        "pool_scale", "gla_gain", "w_out", "w_router", "router_bias", "w1", "w3", "w2", "norm_f"]
_OUT = (1, NX * P, D)


def kernel(**inputs):
    import numpy as _np
    import concourse.bacc as _bacc
    from concourse import mybir as _mybir
    from concourse.bass_utils import run_bass_kernel_spmd as _run

    nc = _bacc.Bacc("TRN2", target_bir_lowering=False, num_devices=1)
    arrays, args = {}, []
    values = [(name, _np.ascontiguousarray(inputs[name])) for name in _INS] + [("inv_counts", box_inverse_counts())]
    for name, a in values:
        arrays[f"in_{name}_dram"] = a
        args.append(nc.dram_tensor(f"in_{name}_dram", a.shape, _mybir.dt.from_np(a.dtype), kind="ExternalInput").ap())
    args.append(nc.dram_tensor("out_dram", _OUT, F32, kind="ExternalOutput").ap())
    hybrid_block(nc, *args)
    r = _run(nc, [arrays], core_ids=[0])
    return r.results[0]["out_dram"]
```

```python
from contextlib import ExitStack

import numpy as np

import concourse.bass as bass
from concourse import mybir

F32 = mybir.dt.float32
I32 = mybir.dt.int32
F32R = mybir.dt.float32r
ALU = mybir.AluOpType
ACT = mybir.ActivationFunctionType
AX = mybir.AxisListType

P = 128
D = 1024
KC = D // P
NX = 8
NCT = 2
NT = NX + NCT
N_MOD = 6
EPS = 1e-6
GRID_W = 64
GRID_H = NX * P // GRID_W
WINDOWS = (2, 4, 8, 16)
NG = len(WINDOWS)
HALF = 512
HEADS = 4
DV = 128
DK = 64
QK = HEADS * DK
RANK2 = 32
GATE_NORM = 16.0
COL_U, COL_Q, COL_V, COL_G, COL_R = 0, HALF, HALF + 2 * QK, 2 * HALF + 2 * QK, 3 * HALF + 2 * QK
MID = P // 2
NE = 16
NGR = 4
MAXB = 31
NB = MAXB + 1
UNIT = KC * HALF
BIG = 1.0e30


def box_inverse_counts():
    out = np.zeros((NG, GRID_H + GRID_W), np.float32)
    for g, w in enumerate(WINDOWS):
        for base, n in ((0, GRID_H), (GRID_H, GRID_W)):
            i = np.arange(n)
            count = np.clip(i + w - w // 2, 0, n) - np.clip(i - w // 2, 0, n)
            out[g, base:base + n] = (1.0 / count).astype(np.float32)
    return out.reshape(1, -1)


def hybrid_block(nc, x, c, ctx_in, c_ctx, w_mod, b_mod, norm1, norm2, w_in, w_gk2, b_gk, w_pool,
                 pool_scale, gla_gain, w_out, w_router, router_bias, w1, w3, w2, norm_f, inv_counts, out):
    with ExitStack() as stack:
        def sb(name, shape, dt=F32):
            return stack.enter_context(nc.sbuf_tensor(name, shape, dt))

        def sem(name):
            return stack.enter_context(nc.semaphore(name))

        ARENA = 49152
        with nc.sbuf_tensor("arena", [P, ARENA], F32) as arena:
            pass

        def at(off, pattern=None, n=None, **dims):
            v = arena[:, off:off + n]
            return v.rearrange(pattern, **dims) if pattern else v

        RING = 2
        LATE, SPARE = RING, RING + 1
        O_HX = RING * UNIT
        O_S = O_HX + KC * NT * P
        ring = [at(off, "p (k n) -> p k n", UNIT, k=KC) for off in (0, UNIT, O_S, O_S + UNIT)]
        state_in = at(O_S, "p (t d a n) -> p t d a n", NX * HALF, t=NX, d=2, a=2)
        hxT = at(O_HX, "p (k t) -> p k t", KC * NT * P, k=KC)
        O_F = O_S + NX * HALF
        O_Q = O_F + 4096
        qdec = at(O_Q, "p (t d a i) -> p t d a i", NX * HALF, t=NX, d=2, a=2)
        O_K = O_Q + NX * HALF
        kdec = at(O_K, "p (t d a i) -> p t d a i", NT * HALF, t=NT, d=2, a=2)
        O_V = O_K + NT * HALF
        vals = at(O_V, "p (t n) -> p t n", NT * HALF, t=NT)
        O_G = O_V + NT * HALF
        gate = at(O_G, "p (t n) -> p t n", NX * HALF, t=NX)
        O_U = O_G + NX * HALF
        uT = at(O_U, "p (g t) -> p g t", NG * NX * P, g=NG)
        rows = at(O_K, "p (s n) -> p s n", NT * D, s=NT)
        absl = at(O_G, "p (s n) -> p s n", 1024, s=2)
        minl = at(O_G + 1024, "p (s n) -> p s n", 1024, s=2)
        spl = at(O_G + 2048, "p (s n) -> p s n", 1024, s=2)
        mod_rows = at(O_G, None, 4 * HALF)[0:2]
        rT = at(O_U, None, NT * P)[0:33]
        w_r = at(O_U + 1280, "p (k n) -> p k n", KC * RANK2, k=KC)
        w_gk = at(O_U + 1536, "p (d n) -> p d n", 2 * QK, d=2)[0:33]
        small_rows = at(O_U + 2048, None, P)[0:85]
        sq0 = at(O_U + 2176, None, D)
        boxa = at(O_F, "p (r w) -> p r w", 2048, r=32)
        boxb = at(O_F + 2048, "p (r w) -> p r w", 2048, r=32)
        macc = at(O_G + 6 * HALF, None, HALF)
        mrow = at(O_G + 7 * HALF, None, HALF)[0:1]
        smask = at(O_K + NX * HALF, "p (h d n) -> p h d n", 1024, h=2, d=2)
        ssum = at(O_V + NX * HALF, "p (h n) -> p h n", HALF, h=2)
        onorm = at(O_V + NX * HALF + HALF, None, HALF)
        x2 = at(O_HX, "p (t n) -> p t n", NX * D, t=NX)
        g1b, a2b = (at(O_HX + NX * D + i * D, None, D) for i in range(2))
        s2b = at(O_F, None, D)
        hx2 = at(O_F + D, "p (s n) -> p s n", 2 * D, s=2)
        hx2T = at(O_F + 3 * D, None, D)
        cmpb = at(O_G, "p (b e) -> p b e", NB * NE, b=NB)
        onehot = at(O_G + D, "p (s n) -> p s n", 2 * NX * P, s=2 * NX)
        slotv = at(O_G + D + 2 * NX * P, "p (s w b) -> p s w b", 4 * NX * NB, s=2 * NX, w=2)
        PLACES = 4
        raw = sb("raw", [P, PLACES * UNIT])
        sb("gain_columns", [P, D])
        xTh = sb("xTh", [P, D], F32R)
        w1h = sb("w1h", [P, UNIT], F32R)
        w3l = sb("w3l", [P, UNIT], F32R)
        w1l = sb("w1l", [P, UNIT], F32R)
        w3h = sb("w3h", [P, UNIT], F32R)
        w2h = sb("w2h", [P, UNIT], F32R)
        w2l = sb("w2l", [P, UNIT], F32R)
        xTl = sb("xTl", [P, D], F32R)
        hTh = sb("hTh", [P, HALF], F32R)
        hTl = sb("hTl", [P, HALF], F32R)
        O_E = O_U
        sb("row_columns", [P, ARENA - O_E])
        w_hi, w_lo = (w1h, w3h, w2h), (w1l, w3l, w2l)
        g2b = at(O_HX + NX * D, None, D)
        assert O_HX == 2 * UNIT and O_S == 4 * UNIT + 2 * D and O_Q == O_S + 2 * UNIT and O_U == O_Q + 4 * UNIT + 2 * D
        xg = at(O_E, None, D)
        hid = at(O_E + D, None, HALF)
        hsil = at(O_E + D + HALF, None, HALF)
        ysb = at(O_E + 2 * D, "p (s n) -> p s n", 2 * D, s=2)
        YS = 4
        y1 = at(O_Q, "p (s n) -> p s n", YS * D, s=YS)
        y2 = at(O_Q + YS * D, "p (s n) -> p s n", YS * D, s=YS)
        fin = at(4 * D, "p (s n) -> p s n", 2 * D, s=2)
        sqf = at(6 * D, None, D)
        nfb = at(7 * D, None, D)

        ident = sb("ident", [P, P])
        mask = sb("mask", [P, 2, P])
        tri = sb("tri", [P, 2, P + 1])
        midc = sb("midc", [P, 2])
        small = sb("small", [P, 85])
        ktok = sb("ktok", [P, 2, 2, P])
        sqg = ktok[:, :, :, :].rearrange("p h a n -> p h (a n)")
        rlT = sb("rlT", [NE, P])
        logit = sb("logit", [P, NX, NE])
        silu_c = sb("silu_c", [P, KC, 2])
        mod = sb("mod", [P, 2, KC, 2])
        a1 = sb("a1", [P, KC, 2])
        stat = sb("stat", [P, 4 * NT + 8])
        expo = sb("expo", [P, 4])
        dec1 = sb("dec1", [P, NT, 2, 2])
        dec2 = sb("dec2", [P, NT, 2, 2])
        dec = sb("dec", [P, NT, 2, 2])
        state = sb("state", [P, 2, 2, DV])
        bmod_row = ktok[0:1].rearrange("p h a n -> p (h a n)")
        norm2_row = state[0:1].rearrange("p d a n -> p (d a n)")
        ost = sb("ost", [P, 12])
        wp = sb("wp", [P, NG, P])
        icnt = sb("icnt", [P, NG, GRID_H + GRID_W])
        w_rt = sb("w_rt", [P, KC, NE])
        bias_b = sb("bias_b", [P, NE])

        ps = stack.enter_context(nc.psum_tensor("ps", [P, 8, 512], F32))

        hx_dram = nc.dram_tensor("hx_rows", [NX * P, D], F32).ap()
        x_dram = nc.dram_tensor("x_rows", [NX * P, D], F32).ap()
        y_dram = nc.dram_tensor("y_rows", [NB * P, D], F32).ap()
        m_dram = nc.dram_tensor("mod_rows_dram", [8, HALF], F32).ap()

        names = """consts small_loaded small_turned small_ready silu_ready mod_used mod_row mod_turned mod_added mod_ready
            macc_ready mrow_done mrow_ready m_chain n2_loaded bmod_loaded mrow_stored bcast_loaded g2_loaded nf_loaded
            ss_ready pow_ready scaled turned hx_a hx_v
            rw_loaded gk_loaded r_done rT_ready lg_done lg_min lg_exp lg_ln sp_ready cum_done cum_read
            proj_done ev_a ev_v pool_w_loaded
            kt_done kt_ready kv_done state_step state_saved s_chain
            sc_done sc_masked s_summed o_done osq_ready oss_ready opow_ready on_ready og_ready ot_done mixg_ready
            box_chain pooled mixp_done mixp_ready
            y_done gated x2_ready ss2_ready pow2_ready hx2_ready hx2_turned hx2T_ready logit_done rl_ready rl_turned rl_out sig_ready
            r_chain route_ready rank_done slots_done table_ready
            tok_ready tok_seen high_seen high_seen_pool split_seen load_seen w3b_split gathered x_turned xh_ready xT_ready l1a l1b l1c silu_done hid_a hid_b hta htb
            hTh_a hTh_b hT_a hT_b
            l2_done y_filled x2_stored x2_back y_ready
            fin_add fss_ready fpow_ready fout_ready""".split()
        S = {n: sem(n) for n in names}
        row_loaded = [sem(f"row_loaded{t}") for t in range(NT)]
        ring_loaded = [sem(f"ring_loaded{i}") for i in range(RING + 2)]
        hx2_stored, y_stored, stored = (
            [sem(f"{n}{i}") for i in range(2)]
            for n in ("hx2_stored", "y_stored", "stored"))
        fin_loaded = [sem(f"fin_loaded{i}") for i in range(YS)]

        w_loaded, w_high, w_split = ([sem(f"{n}_{w}") for w in ("w1", "w3", "w2")] for n in ("w_loaded", "w_high", "w_split"))

        def link(eng, chain, ins):
            name, count = chain
            count[0] += 1
            ins.then_inc(S[name], 1)
            eng.wait_ge(S[name], count[0])

        wmod_v = w_mod[0].rearrange("(k p) n -> p k n", p=P)
        win_v = w_in[0].rearrange("(k p) n -> p k n", p=P)
        wout_v = w_out[0].rearrange("(k p) n -> p k n", p=P)
        units = ([(("mod", 0), 0), (("mod", 1), 1), (("mod", 2), LATE), (("mod", 3), SPARE), (("v", 0), 0), (("u", 0), 1)]
                 + [(("mod", j), LATE) for j in range(4, 9)] + [(("qk", 0), 0)] + [(("mod", j), LATE) for j in range(9, 12)]
                 + [(("g", 0), 1), (("out", 0), 0), (("out", 1), 1)])
        unit_slot = dict(units)
        unit_turn = {u: [v for v, at_slot in units if at_slot == slot].index(u) for u, slot in units}

        def unit_src(u):
            kind, j = u
            if kind == "mod":
                return wmod_v[:, :, j * HALF:(j + 1) * HALF]
            if kind == "out":
                return wout_v[:, :, j * HALF:(j + 1) * HALF]
            col = {"v": COL_V, "qk": COL_Q, "g": COL_G, "u": COL_U}[kind]
            return win_v[:, :, col:col + HALF]

        def unit_used(u):
            if u[0] == "mod" and u[1] < 4:
                return S["mod_used"], u[1] + 1
            if u[0] == "mod":
                return S["macc_ready"], u[1] - 3
            last = {"v": ("v", NT - 1), "qk": ("q", 1, 1), "g": ("g", NX - 1), "u": ("u", NG - 1, 1)}[u[0]]
            return S["proj_done"], group_no[last] + 1

        def unit_ready(eng, u):
            eng.wait_ge(ring_loaded[unit_slot[u]], 16 * (unit_turn[u] + 1))
            return ring[unit_slot[u]]

        EARLY = 7

        tok_groups = [(0, 4), (4, 4), (8, 2)]
        groups = ([("v", t) for t in range(NT)] + [("u", p, g) for p in range(NG) for g in range(2)]
                  + [("k", a, g) for g in range(3) for a in range(2)] + [("q", a, g) for g in range(2) for a in range(2)]
                  + [("g", t) for t in range(NX)])
        PB = 4
        evac = {}
        na = nv = 0
        for n, g in enumerate(groups):
            on_act = g[0] == "g" or (g[0] == "v" and g[1] % 2 == 0) or (g[0] == "u")
            if on_act:
                na += 1
                evac[n] = ("ev_a", na)
            else:
                nv += 1
                evac[n] = ("ev_v", nv)
        group_no = {g: n for n, g in enumerate(groups)}

        def evacuated(g):
            s, v = evac[group_no[g]]
            return S[s], v

        def steps():
            fwd = [NX, NX + 1] + list(range(NX))
            bwd = [NX + 1, NX] + list(range(NX - 1, -1, -1))
            return list(zip(fwd, bwd))

        NTE = NX * NE
        rt = {}
        rt_at = O_U
        for n, shape in dict(s=[NX, NE], sbias=[NX, NE], hi=[32, 2], lo=[32, 2], t1=[32, 1], t2=[32, 1],
                             gm=[NX, 1], geq=[NX, NGR], goh=[NX, NGR], mb=[NX, NE], mx=[NX, 1], eq=[NX, NE],
                             oh1=[NX, NE], oh2=[NX, NE], sel=[4 + NX, NE], pre=[4 + NX, NE], pre2=[4 + NX, NE], tot=[1, NE],
                             nbl=[1, NE], cb=[1, NE + 8], cb2=[1, NE + 8], base=[1, NE], rank=[NX, NE],
                             s12=[2, NX], ssum=[NX, 1], wk=[2, NX], dest=[2, NX],
                             blkf=[2, NX], posf=[2, NX], prior=[NX, 2 * NGR]).items():
            width = shape[0] * shape[1]
            rt[n] = at(rt_at, "p (a b) -> p a b", width, a=shape[0])
            rt_at += width
        assert rt_at <= ARENA
        cmp16 = at(O_G + HALF, "p (e k) -> p e k", NE * KC, e=NE)
        desti = sb("desti", [P, 2, NX], I32)
        blki = sb("blki", [P, 2, NX], I32)
        posi = sb("posi", [P, 2, NX], I32)
        iota_p = sb("iota_p", [P, P])
        iota_e = sb("iota_e", [P, NE])
        tokid = sb("tokid", [P, NX])
        thresh = sb("thresh", [P, KC])
        ones = sb("ones", [P, P])
        strict = sb("strict", [P, P])
        slot_tok = sb("slot_tok", [P, NB + 2], I32)
        block_tok = sb("block_tok", [P, 1], I32)
        slot_w = sb("slot_w", [P, NB])
        ebf = sb("ebf", [P, NB])
        tabs = sb("tabs", [P, 5 * NB + 1], I32)
        T_E, T_PLACE, T_NEW, T_NB = 0, NB, 4 * NB, 5 * NB

        block = stack.enter_context(nc.Block())

        @block.sync
        def _(sp):
            sp.dma_start(small_rows[0:8, :], c.rearrange("o (k p) -> (o k) p", p=P)).then_inc(S["small_loaded"], 16)
            sp.dma_start(small_rows[8:16, :], c_ctx.rearrange("(k p) -> k p", p=P)).then_inc(S["small_loaded"], 16)
            sp.dma_start(small_rows[16:24, :], norm1.rearrange("o (k p) -> (o k) p", p=P)).then_inc(S["small_loaded"], 16)
            sp.dma_start(small_rows[24:32, :], norm2.rearrange("o (k p) -> (o k) p", p=P)).then_inc(S["small_loaded"], 16)
            sp.dma_start(small_rows[32:80, :], b_mod.rearrange("o (k p) -> (o k) p", p=P)).then_inc(S["small_loaded"], 16)
            sp.dma_start(small_rows[80:84, :], pool_scale.rearrange("o (k p) -> (o k) p", p=P)).then_inc(S["small_loaded"], 16)
            sp.dma_start(small_rows[84:85, :], gla_gain).then_inc(S["small_loaded"], 16)
            for n, (u, slot) in enumerate(units):
                before = [v for v, at_slot in units[:n] if at_slot == slot]
                if u == ("v", 0):
                    sp.wait_ge(row_loaded[NT - 1], 16)
                if before:
                    sp.wait_ge(*unit_used(before[-1]))
                sp.dma_start(ring[slot], unit_src(u)).then_inc(ring_loaded[slot], 16)

            def load_expert(e, turn, first=False):
                for j, w in enumerate((w1, w3, w2)):
                    n = 3 * turn + j
                    if first and n < 2:
                        sp.wait_ge(S["y_done"], 2 * (NX - 1) + j + 1)
                    elif first and n == 2:
                        sp.wait_ge(S["y_filled"], 16 * 2 * NX)
                        sp.wait_ge(S["x2_stored"], 16 * NX)
                        sp.wait_ge(S["hx2_ready"], NX)
                    elif not (first and n == 3):
                        if j == 2:
                            sp.wait_ge(w_split[1], e)
                            sp.sem_inc(S["split_seen"], 1)
                            sp.wait_ge(S["w3b_split"], e)
                        else:
                            sp.wait_ge(w_split[(j + 2) % 3], 2 * e - (2 if j == 0 else 0))
                        sp.sem_inc(S["split_seen"], 1)
                    if not (first and turn == 0):
                        sp.wait_ge(w_loaded[j], 16 * e)
                    k = KC if j < 2 else 4
                    sp.dma_start(raw[:, (n % PLACES) * UNIT:][:, 0:UNIT].rearrange("p (k n) -> p k n", k=k),
                                 w[0, bass.ds(e, 1)].rearrange("o (k p) n -> p (o k) n", p=P)).then_inc(w_loaded[j], 16)

            for e in range(PLACES):
                load_expert(e, e, first=True)
            with sp.Fori(1, NE // PLACES) as group:
                for turn in range(PLACES):
                    load_expert(group * PLACES + turn, turn)
            for done, count in ((w_split[0], 2 * NE), (w_split[1], NE), (S["w3b_split"], NE), (w_split[2], 2 * NE)):
                sp.wait_ge(done, count)
            sp.dma_start(x2, x_dram.rearrange("(t p) n -> p t n", p=P)).then_inc(S["x2_back"], 16)
            for t in range(NX):
                sp.wait_ge(S["fout_ready"], t + 1)
                sp.dma_start(out[0, t * P:(t + 1) * P, :], fin[:, t % 2, :]).then_inc(stored[t % 2], 16)
            for par in range(2):
                sp.wait_ge(stored[par], 16 * NX // 2)

        @block.gpsimd
        def _(pool):
            cc = ("consts", [0])
            link(pool, cc, pool.memset(ident[:, :], 0.0))
            link(pool, cc, pool.affine_select(out=ident[:, :], in_=ident[:, :], compare_op=ALU.not_equal, fill=1.0, base=0,
                               pattern=[[-1, P]], channel_multiplier=1))
            link(pool, cc, pool.memset(mask[:, :, :], 1.0))
            link(pool, cc, pool.memset(tri[:, :, :], -1.0 / GATE_NORM))
            link(pool, cc, pool.memset(midc[:, :], 0.0))
            link(pool, cc, pool.memset(ones[:, :], 1.0))
            link(pool, cc, pool.memset(strict[:, :], 1.0))
            link(pool, cc, pool.memset(expo[:, :], -0.5))
            link(pool, cc, pool.memset(rT[32:33, :], 1.0))
            link(pool, cc, pool.memset(w_gk[0:32, :, :], 0.0))
            link(pool, cc, pool.iota(iota_p[:, :], pattern=[[1, P]], base=0, channel_multiplier=0,
                      allow_small_or_imprecise_dtypes=True))
            link(pool, cc, pool.iota(iota_e[:, :], pattern=[[-1, NE]], base=NE, channel_multiplier=0,
                      allow_small_or_imprecise_dtypes=True))
            link(pool, cc, pool.iota(tokid[:, :], pattern=[[P, NX]], base=0, channel_multiplier=1,
                      allow_small_or_imprecise_dtypes=True))
            link(pool, cc, pool.iota(thresh[:, :], pattern=[[P, KC]], base=0, channel_multiplier=0,
                      allow_small_or_imprecise_dtypes=True))
            for m in (mask, tri[:, :, 0:P]):
                link(pool, cc, pool.affine_select(out=m[:, 0, :], in_=m[:, 0, :], compare_op=ALU.is_ge, fill=0.0, base=0,
                                   pattern=[[1, P]], channel_multiplier=-1))
                link(pool, cc, pool.affine_select(out=m[:, 1, :], in_=m[:, 1, :], compare_op=ALU.is_ge, fill=0.0, base=0,
                                   pattern=[[-1, P]], channel_multiplier=1))
            link(pool, cc, pool.affine_select(out=strict[:, :], in_=strict[:, :], compare_op=ALU.is_gt, fill=0.0, base=0,
                               pattern=[[1, P]], channel_multiplier=-1))
            link(pool, cc, pool.memset(midc[0:MID, 0:1], -1.0 / GATE_NORM))
            link(pool, cc, pool.memset(midc[MID:P, 1:2], -1.0 / GATE_NORM))
            for d in range(2):
                link(pool, cc, pool.tensor_scalar(tri[:, d, 0:P], tri[:, d, 0:P], midc[:, d:d + 1], None, ALU.subtract))
                link(pool, cc, pool.tensor_copy(tri[:, d, P:P + 1], midc[:, d:d + 1]))
            for d in range(2):
                pool.dma_start(w_gk[16 * d:16 * d + 16, d, :], w_gk2[0, d]).then_inc(S["gk_loaded"], 16)
            pool.dma_start(w_gk[32:33, :, :], b_gk).then_inc(S["gk_loaded"], 16)
            pool.dma_start(w_r[:, :, :], win_v[:, :, COL_R:COL_R + RANK2]).then_inc(S["rw_loaded"], 16)
            pool.dma_start(wp[:, :, :], w_pool[0].rearrange("g c n -> c g n")).then_inc(S["pool_w_loaded"], 16)
            pool.dma_start(icnt[:, :, :].rearrange("p g n -> p (g n)"),
                           inv_counts.partition_broadcast(P)).then_inc(S["pool_w_loaded"], 16)
            pool.dma_start(w_rt[:, :, :], w_router.rearrange("(k p) e -> p k e", p=P)).then_inc(S["pool_w_loaded"], 16)
            pool.dma_start(bias_b[:, :], router_bias.rearrange("(o e) -> o e", o=1).partition_broadcast(P))\
                .then_inc(S["pool_w_loaded"], 16)
            for t in range(NT):
                pool.wait_ge(S["ss_ready"], t + 1)
                pool.tensor_scalar(stat[:, NT + t:NT + t + 1], stat[:, t:t + 1], 1.0 / D, EPS, ALU.mult, ALU.add)\
                    .then_inc(S["box_chain"], 1)
                pool.wait_ge(S["box_chain"], t + 1)
                pool.tensor_tensor(stat[:, 2 * NT + t:2 * NT + t + 1], stat[:, NT + t:NT + t + 1], expo[:, 0:1], ALU.pow)\
                    .then_inc(S["pow_ready"], 1)
                pool.wait_ge(S["pow_ready"], t + 1)
            for i in range(8):
                pool.dma_start(bmod_row, b_mod[:, (4 + i) * HALF:(5 + i) * HALF]).then_inc(S["bmod_loaded"], 16)
                if i in (4, 5):
                    pool.dma_start(norm2_row, norm2[:, (i - 4) * HALF:(i - 3) * HALF]).then_inc(S["n2_loaded"], 16)
                pool.wait_ge(S["mrow_ready"], i + 1)
                pool.dma_start(m_dram[i:i + 1, :], mrow).then_inc(S["mrow_stored"], 16)
            bc = ("box_chain", [NT])
            for t in range(NX + 1):
                if t < NX:
                    pool.wait_ge(S["oss_ready"], t + 1)
                    link(pool, bc, pool.tensor_scalar(ost[:, 4:8], ost[:, 0:4], 1.0 / DV, EPS, ALU.mult, ALU.add))
                    pool.tensor_tensor(ost[:, 8:12], ost[:, 4:8], expo[:, 0:4], ALU.pow).then_inc(S["opow_ready"], 1)
                    pool.wait_ge(S["opow_ready"], t + 1)
                if t >= 1:
                    u = t - 1
                    pool.wait_ge(S["ss2_ready"], u + 1)
                    link(pool, bc, pool.tensor_scalar(stat[:, NT + u:NT + u + 1], stat[:, u:u + 1], 1.0 / D, EPS, ALU.mult, ALU.add))
                    pool.tensor_tensor(stat[:, 2 * NT + u:2 * NT + u + 1], stat[:, NT + u:NT + u + 1], expo[:, 0:1], ALU.pow)\
                        .then_inc(S["pow2_ready"], 1)
                    pool.wait_ge(S["pow2_ready"], u + 1)
            pool.wait_ge(S["rl_out"], NX)
            for par in range(2):
                pool.wait_ge(hx2_stored[par], 16 * NX // 2)
            for j in range(2):
                for k in range(2):
                    part = slice(k * UNIT // 2, (k + 1) * UNIT // 2)
                    pool.wait_ge(w_high[j], k + 1)
                    pool.tensor_tensor(w_lo[j][:, part], raw[:, j * UNIT:][:, part], w_hi[j][:, part].bitcast(F32), ALU.subtract)\
                        .then_inc(S["w3b_split"] if (j, k) == (1, 1) else w_split[j], 1)
                    if (j, k) == (1, 1):
                        pool.wait_ge(S["w3b_split"], 1)
                    else:
                        pool.wait_ge(w_split[j], k + 1)
            pool.wait_ge(S["table_ready"], 1)
            nb = pool.value_load(tabs[0:1, T_NB:T_NB + 1], min_val=1, max_val=MAXB)

            def gather(b):
                pool.tensor_copy(block_tok[:, :], slot_tok[:, bass.ds(b, 1)]).then_inc(S["tok_ready"], 1)
                pool.wait_ge(S["tok_ready"], b + 1)
                pool.sem_inc(S["tok_seen"], 1)
                pool.indirect_dma_start(out=xg, out_offset=None, in_=hx_dram,
                                        in_offset=bass.IndirectOffsetOnAxis(ap=block_tok[:, :], axis=0))\
                    .then_inc(S["gathered"], 16)

            gather(0)
            pool.wait_ge(S["x_turned"], 1)
            gather(1)
            with pool.Fori(0, NB // 2) as pair:
                i = pair * 2
                for s in range(2):
                    with pool.If(i + s < nb):
                        b = i + s
                        e, new, place3, place2 = (pool.value_load(tabs[0:1, bass.ds(b + at_, 1)], min_val=0, max_val=most)
                                                  for at_, most in ((T_E, NE - 1), (T_NEW, 1), (T_PLACE + NB, PLACES - 1),
                                                                    (T_PLACE + 2 * NB, PLACES - 1)))
                        with pool.If(b + 1 < nb):
                            pool.wait_ge(S["x_turned"], b + 2)
                            gather(b + 2)
                        with pool.If(new > 0):
                            half = slice(UNIT // 2, UNIT)
                            pool.wait_ge(w_high[1], 2 * e + 4)
                            pool.sem_inc(S["high_seen_pool"], 1)
                            pool.tensor_tensor(w3l[:, half], raw[:, bass.ds(place3 * UNIT + UNIT // 2, UNIT // 2)],
                                               w3h[:, half].bitcast(F32), ALU.subtract).then_inc(S["w3b_split"], 1)
                            pool.wait_ge(S["w3b_split"], e + 2)
                            for k in range(2):
                                part = slice(k * UNIT // 2, (k + 1) * UNIT // 2)
                                pool.wait_ge(w_high[2], 2 * e + (k + 3))
                                pool.sem_inc(S["high_seen_pool"], 1)
                                pool.tensor_tensor(w2l[:, part], raw[:, bass.ds(place2 * UNIT + k * (UNIT // 2), UNIT // 2)],
                                                   w2h[:, part].bitcast(F32), ALU.subtract).then_inc(w_split[2], 1)
                                pool.wait_ge(w_split[2], 2 * e + (k + 3))
            for par in range(2):
                pool.wait_ge(y_stored[par], 16 * NB // 2 + 16)

            def gather_results(t):
                if t >= YS:
                    pool.wait_ge(S["fin_add"], 2 * (t - YS + 1))
                for k, buf in enumerate((y1, y2)):
                    pool.indirect_dma_start(out=buf[:, t % YS, :], out_offset=None, in_=y_dram,
                                            in_offset=bass.IndirectOffsetOnAxis(ap=desti[:, k, t:t + 1], axis=0))\
                        .then_inc(fin_loaded[t % YS], 16)

            for t in range(YS):
                gather_results(t)
            for t in range(NX):
                pool.wait_ge(S["fss_ready"], t + 1)
                link(pool, bc, pool.tensor_scalar(stat[:, NT + t:NT + t + 1], stat[:, t:t + 1], 1.0 / D, EPS, ALU.mult, ALU.add))
                pool.tensor_tensor(stat[:, 2 * NT + t:2 * NT + t + 1], stat[:, NT + t:NT + t + 1], expo[:, 0:1], ALU.pow)\
                    .then_inc(S["fpow_ready"], 1)
                pool.wait_ge(S["fpow_ready"], t + 1)
                if t + YS < NX:
                    gather_results(t + YS)

        @block.scalar
        def _(act):
            def row_src(t):
                return x[0, t * P:(t + 1) * P, :] if t < NX else ctx_in[0, (t - NX) * P:(t - NX + 1) * P, :]

            act.wait_ge(S["small_ready"], 1)
            act.activation(silu_c[:, :, :], small[:, 0:16].rearrange("p (w k) -> p k w", w=2), ACT.Silu)\
                .then_inc(S["silu_ready"], 1)
            act.wait_ge(ring_loaded[1], 16)
            for t in range(NT):
                act.dma_start(rows[:, t, :], row_src(t)).then_inc(row_loaded[t], 16)
            def square(t):
                act.wait_ge(row_loaded[t], 16)
                act.activation(sq0, rows[:, t, :], ACT.Square, accum_out=stat[:, t:t + 1])\
                    .then_inc(S["ss_ready"], 1)
                act.wait_ge(S["ss_ready"], t + 1)

            for t in range(EARLY):
                square(t)
            for j in range(4):
                act.wait_ge(S["mod_used"], j + 1)
                act.activation(mod_rows[:, j * HALF:(j + 1) * HALF], ps[0:2, 4 + j, :], ACT.Copy).then_inc(S["mod_row"], 1)
            for t in range(NT):
                if t + EARLY < NT:
                    square(t + EARLY)
                if t == 0:
                    act.wait_ge(S["mod_ready"], 2)
                which = 0 if t < NX else 1
                act.wait_ge(S["turned"], t + 1)
                for k in range(4, KC):
                    ins = act.activation(hxT[:, k, t * P:(t + 1) * P], ps[:, 2 * (t % 2) + 1, (k - 4) * P:(k - 3) * P],
                                         ACT.Identity, bias=mod[:, 0, k, which:which + 1], scale=a1[:, k, which:which + 1])
                ins.then_inc(S["hx_a"], 1)

            def ev(n):
                act.wait_ge(S["proj_done"], n + 1)

            def decays(t):
                act.wait_ge(S["lg_min"], 2 * (t + 1))
                act.activation(absl[:, t % 2, :], absl[:, t % 2, :], ACT.Exp, scale=-1.0).then_inc(S["lg_exp"], 1)
                act.wait_ge(S["lg_exp"], t + 1)
                act.activation(absl[:, t % 2, :], absl[:, t % 2, :], ACT.Ln, bias=1.0).then_inc(S["lg_ln"], 1)

            def decay_exp(t):
                act.wait_ge(S["cum_done"], t + 1)
                for d in range(2):
                    cum = ps[:, 5 + d, 0:2 * (P + 1)].rearrange("p (a i) -> p a i", a=2)
                    if t < NX:
                        act.activation(qdec[:, t, d], cum[:, :, 0:P], ACT.Exp)
                    act.activation(kdec[:, t, d], cum[:, :, 0:P], ACT.Exp, scale=-1.0)
                    end = P - 1 if d == 0 else 0
                    act.activation(dec2[:, t, d, :], cum[:, :, end], ACT.Exp)
                    ins = act.activation(dec1[:, t, d, :], cum[:, :, P], ACT.Exp)
                ins.then_inc(S["cum_read"], 1)

            decays(0)
            for t in range(NT):
                if t + 1 < NT:
                    decays(t + 1)
                if t % 2 == 0:
                    n = group_no[("v", t)]
                    ev(n)
                    if t == 0:
                        act.wait_ge(S["turned"], NT)
                    act.activation(vals[:, t, :], ps[:, n % PB, :], ACT.Copy).then_inc(S["ev_a"], 1)
                decay_exp(t)
            for n, g in enumerate(groups):
                if g[0] == "u":
                    ev(n)
                    act.activation(uT[:, g[1], g[2] * HALF:(g[2] + 1) * HALF], ps[:, n % PB, :], ACT.Copy)\
                        .then_inc(S["ev_a"], 1)
            for n in range(NT + 1):
                if n < NT:
                    act.wait_ge(S["kt_done"], n + 1)
                    if n >= 1:
                        act.wait_ge(S["kv_done"], n)
                    act.activation(ktok[:, :, :, :].rearrange("p d a n -> p (d a n)"), ps[:, 4, :], ACT.Copy).then_inc(S["kt_ready"], 1)
                if 1 <= n <= NX:
                    m = group_no[("g", n - 1)]
                    ev(m)
                    if n == 1:
                        act.wait_ge(S["mrow_stored"], 16 * 8)
                    act.activation(gate[:, n - 1, :], ps[:, m % PB, :], ACT.Silu).then_inc(S["ev_a"], 1)
            act.wait_ge(S["proj_done"], len(groups))
            for t in range(NX):
                act.dma_start(x2[:, t, :], row_src(t)).then_inc(row_loaded[t], 16)
            for first, dst in ((0, g1b), (4, a2b), (2, s2b)):
                act.dma_start(dst, m_dram[first:first + 2, :].rearrange("(o k) p -> o (k p)", o=1).partition_broadcast(P))\
                    .then_inc(S["bcast_loaded"], 16)

            def turned_out(u, h):
                act.wait_ge(S["hx2_turned"], 2 * u + h + 1)
                if h == 0 and u >= 1:
                    act.wait_ge(S["logit_done"], u)
                act.activation(hx2T[:, h * HALF:(h + 1) * HALF], ps[:, 7, :], ACT.Copy).then_inc(S["hx2T_ready"], 1)

            def mixed_pool(g):
                for h in range(2):
                    act.wait_ge(S["mixp_done"], 2 * g + h + 1)
                    act.activation(uT[:, g, h * HALF:(h + 1) * HALF], ps[:, 5 + h, :], ACT.Copy,
                                   scale=small[:, 80 + g:81 + g]).then_inc(S["mixp_ready"], 1)

            def logits_out(u):
                act.wait_ge(S["rl_turned"], u + 1)
                act.activation(logit[:, u, :], ps[:, 7, P:P + NE], ACT.Copy).then_inc(S["rl_out"], 1)

            for t in range(NX + 2):
                u = t - 2
                if t >= 3:
                    logits_out(u - 1)
                if t == 0:
                    mixed_pool(0)
                    mixed_pool(1)
                if t >= 2:
                    act.wait_ge(S["hx2_ready"], u + 1)
                    act.dma_start(hx_dram[u * P:(u + 1) * P, :], hx2[:, u % 2, :]).then_inc(hx2_stored[u % 2], 16)
                    turned_out(u, 0)
                if t < NX:
                    for h in range(2):
                        act.wait_ge(S["o_done"], t + 1)
                        act.activation(sqg[:, h, :], ps[:, 2 + h, 0:256], ACT.Square).then_inc(S["osq_ready"], 1)
                if t == 0:
                    mixed_pool(2)
                    mixed_pool(3)
                if t >= 2:
                    turned_out(u, 1)
                if t < NX:
                    act.wait_ge(S["ot_done"], t + 1)
                    act.activation(gate[:, t, :], ps[:, 4, :], ACT.Copy, scale=small[:, 84:85]).then_inc(S["mixg_ready"], 1)
                if 1 <= t <= NX:
                    w = t - 1
                    act.wait_ge(S["x2_ready"], 2 * (w + 1))
                    if w >= 2:
                        act.wait_ge(hx2_stored[w % 2], 16 * (w // 2))
                    act.activation(hx2[:, w % 2, :], x2[:, w, :], ACT.Square, accum_out=stat[:, w:w + 1]).then_inc(S["ss2_ready"], 1)
                    for blk in (NE + w, NE + NX + w):
                        act.dma_start(y_dram[blk * P:(blk + 1) * P, :], x2[:, w, :]).then_inc(S["y_filled"], 16)
                    act.dma_start(x_dram[w * P:(w + 1) * P, :], x2[:, w, :]).then_inc(S["x2_stored"], 16)
                if t >= 2:
                    act.wait_ge(S["logit_done"], u + 1)
                    act.activation(rlT[:, :], ps[0:NE, 7, 0:P], ACT.Copy).then_inc(S["rl_ready"], 1)
            logits_out(NX - 1)
            act.wait_ge(S["rl_out"], NX)
            act.activation(rt["s"], logit[:, :, :], ACT.Sigmoid).then_inc(S["sig_ready"], 1)
            act.dma_start(g2b, m_dram[6:8, :].rearrange("(o k) p -> o (k p)", o=1).partition_broadcast(P))\
                .then_inc(S["g2_loaded"], 16)
            def high(j, base, halves=(0, 1)):
                for k in halves:
                    part = slice(k * UNIT // 2, (k + 1) * UNIT // 2)
                    act.activation(w_hi[j][:, part], raw[:, bass.ds(base + k * (UNIT // 2), UNIT // 2)], ACT.Copy).then_inc(w_high[j], 1)

            for j in range(2):
                act.wait_ge(w_loaded[j], 16)
                high(j, j * UNIT)
            act.wait_ge(w_loaded[2], 16)
            high(2, 2 * UNIT)
            act.wait_ge(S["table_ready"], 1)
            nb = act.value_load(tabs[0:1, T_NB:T_NB + 1], min_val=1, max_val=MAXB)

            def turn_out(b):
                act.wait_ge(S["x_turned"], b + 1)
                act.activation(xTh[:, :], ps[:, 0:2, :].rearrange("p h n -> p (h n)"), ACT.Copy).then_inc(S["xh_ready"], 1)

            turn_out(0)
            act.wait_ge(S["y_filled"], 16 * 2 * NX)
            for par in range(2):
                act.sem_inc(y_stored[par], 16)
            with act.Fori(0, NB // 2) as pair:
                i = pair * 2
                for s in range(2):
                    with act.If(i + s < nb):
                        b = i + s
                        e, new, *place = (act.value_load(tabs[0:1, bass.ds(b + at_, 1)], min_val=0, max_val=most)
                                          for at_, most in [(T_E, NE - 1), (T_NEW, 1)] + [(T_PLACE + j * NB, PLACES - 1) for j in range(3)])
                        act.wait_ge(S["l1a"], b + 1)
                        act.activation(hsil, ps[:, 2, :], ACT.Silu).then_inc(S["silu_done"], 1)
                        with act.If(new > 0):
                            act.wait_ge(w_loaded[0], 16 * e + 32)
                            high(0, place[0] * UNIT, (0,))
                        act.wait_ge(S["hta"], b + 1)
                        act.activation(hTh[:, 0:256], ps[:, 5, 0:256], ACT.Copy).then_inc(S["hTh_a"], 1)
                        with act.If(new > 0):
                            high(0, place[0] * UNIT, (1,))
                        act.wait_ge(S["l1c"], b + 1)
                        turn_out(b + 1)
                        act.wait_ge(S["htb"], b + 1)
                        act.activation(hTh[:, 256:512], ps[:, 5, 256:512], ACT.Copy).then_inc(S["hTh_b"], 1)
                        with act.If(new > 0):
                            act.wait_ge(w_loaded[1], 16 * e + 32)
                            high(1, place[1] * UNIT)
                            act.wait_ge(w_loaded[2], 16 * e + 32)
                            act.sem_inc(S["load_seen"], 1)
                            act.wait_ge(S["l2_done"], b + 1)
                            high(2, place[2] * UNIT)
                        act.wait_ge(S["y_ready"], 2 * i + (2 * s + 4))
                        act.dma_start(y_dram[bass.ds(b * P, P), :], ysb[:, s, :]).then_inc(y_stored[s], 16)
                    with act.Else():
                        act.sem_inc(y_stored[s], 16)
            for par in range(2):
                act.wait_ge(y_stored[par], 16 * NB // 2 + 16)
            act.dma_start(nfb, norm_f.rearrange("(o n) -> o n", o=1).partition_broadcast(P)).then_inc(S["nf_loaded"], 16)
            for t in range(NX):
                act.wait_ge(S["fin_add"], 2 * (t + 1))
                if t >= 1:
                    act.wait_ge(S["fss_ready"], t)
                act.activation(sqf, x2[:, t, :], ACT.Square, accum_out=stat[:, t:t + 1]).then_inc(S["fss_ready"], 1)

        @block.vector
        def _(dve):
            dve.wait_ge(S["small_turned"], 1)
            dve.tensor_copy(small[:, :], ps[:, 7, 0:85]).then_inc(S["small_ready"], 1)
            def scale_rows(t):
                dve.wait_ge(S["pow_ready"], t + 1)
                dve.tensor_scalar(rows[:, t, :], rows[:, t, :], stat[:, 2 * NT + t:2 * NT + t + 1], None, ALU.mult)\
                    .then_inc(S["scaled"], 1)

            for t in range(EARLY):
                scale_rows(t)
            dve.wait_ge(S["mod_turned"], 1)
            b_cols = small[:, 32:80].rearrange("p (s k) -> p s k", s=N_MOD)
            for w in range(2):
                dve.tensor_tensor(mod[:, 0:2, :, w], ps[:, 4, 0:32].rearrange("p (s k w) -> p s k w", s=2, w=2)[:, :, :, w],
                                  b_cols[:, 0:2, :], ALU.add).then_inc(S["mod_added"], 1)
            dve.wait_ge(S["mod_added"], 2)
            for w in range(2):
                dve.scalar_tensor_tensor(out=a1[:, :, w], in0=mod[:, 1, :, w], scalar=1.0, in1=small[:, 16:24],
                                         op0=ALU.add, op1=ALU.mult).then_inc(S["mod_ready"], 1)
            dve.wait_ge(S["mod_ready"], 2)
            for t in range(NT):
                if t + EARLY < NT:
                    scale_rows(t + EARLY)
                which = 0 if t < NX else 1
                dve.wait_ge(S["turned"], t + 1)
                for k in range(4):
                    ins = dve.tensor_scalar(hxT[:, k, t * P:(t + 1) * P], ps[:, 2 * (t % 2), k * P:(k + 1) * P],
                                            a1[:, k, which:which + 1], mod[:, 0, k, which:which + 1], ALU.mult, ALU.add)
                ins.then_inc(S["hx_v"], 1)
            for g, (t0, n) in enumerate(tok_groups):
                dve.wait_ge(S["r_done"], g + 1)
                dve.tensor_copy(rT[0:32, t0 * P:(t0 + n) * P], ps[0:32, 5 + g, 0:n * P]).then_inc(S["rT_ready"], 1)
            sc = ("s_chain", [0])
            mc = ("m_chain", [0])

            def late_sum(i):
                w = unit_ready(dve, ("mod", 4 + i))
                for k in range(KC):
                    if k == 0:
                        ins = dve.tensor_scalar(macc, w[:, k, :], silu_c[:, k, 0:1], None, ALU.mult)
                    else:
                        ins = dve.scalar_tensor_tensor(out=macc, in0=w[:, k, :], scalar=silu_c[:, k, 0:1],
                                                       in1=macc, op0=ALU.mult, op1=ALU.add)
                    if k < KC - 1:
                        link(dve, mc, ins)
                ins.then_inc(S["macc_ready"], 1)

            def late_row(i):
                dve.wait_ge(S["mrow_done"], i + 1)
                dve.wait_ge(S["bmod_loaded"], 16 * (i + 1))
                if i >= 1:
                    dve.wait_ge(S["mrow_stored"], 16 * i)
                ins = dve.tensor_tensor(mrow, ps[0:1, 7, :], bmod_row, ALU.add)
                if i in (4, 5):
                    link(dve, mc, ins)
                    dve.wait_ge(S["n2_loaded"], 16 * (i - 3))
                    ins = dve.scalar_tensor_tensor(out=mrow, in0=mrow, scalar=1.0,
                                                   in1=norm2_row, op0=ALU.add, op1=ALU.mult)
                ins.then_inc(S["mrow_ready"], 1)

            def min_and_abs(t):
                dve.wait_ge(S["lg_done"], t + 1)
                dve.tensor_scalar(minl[:, t % 2, :], ps[:, 4, :], 0.0, None, ALU.min).then_inc(S["lg_min"], 1)
                dve.wait_ge(S["lg_min"], 2 * t + 1)
                dve.scalar_tensor_tensor(out=absl[:, t % 2, :], in0=minl[:, t % 2, :], scalar=-2.0, in1=ps[:, 4, :],
                                         op0=ALU.mult, op1=ALU.add).then_inc(S["lg_min"], 1)

            min_and_abs(0)
            for t in range(NT):
                if t + 1 < NT:
                    min_and_abs(t + 1)
                dve.wait_ge(S["lg_ln"], t + 1)
                if t >= 2:
                    dve.wait_ge(S["cum_done"], t - 1)
                dve.tensor_tensor(spl[:, t % 2, :], absl[:, t % 2, :], minl[:, t % 2, :], ALU.subtract).then_inc(S["sp_ready"], 1)
                if t % 2 == 1:
                    n = group_no[("v", t)]
                    dve.wait_ge(S["proj_done"], n + 1)
                    dve.tensor_copy(vals[:, t, :], ps[:, n % PB, :]).then_inc(S["ev_v"], 1)
                    if t >= 3:
                        late_row(t // 2 - 1)
                    late_sum(t // 2)
            def pool_steps():
                dve.wait_ge(S["pool_w_loaded"], 64)
                for g, w in enumerate(WINDOWS):
                    h = w // 2
                    for part in range(2):
                        dve.wait_ge(*evacuated(("u", g, part)))
                    link(dve, sc, dve.memset(boxa[:, 8 - h:8, :], 0.0))
                    link(dve, sc, dve.memset(boxa[:, 8 + GRID_H:8 + GRID_H + h, :], 0.0))
                    link(dve, sc, dve.tensor_copy(boxa[:, 8:8 + GRID_H, :], uT[:, g, :].rearrange("p (r w) -> p r w", w=GRID_W)))
                    yield
                    src, dst, L = boxa, boxb, 2
                    while L <= w:
                        lo, n = 8 - h, GRID_H + w - L
                        link(dve, sc, dve.tensor_tensor(dst[:, lo:lo + n, :], src[:, lo:lo + n, :],
                                                        src[:, lo + L // 2:lo + L // 2 + n, :], ALU.add))
                        src, dst, L = dst, src, 2 * L
                        yield
                    wide, wide2 = (b.rearrange("p r w -> p (r w)")[:, 0:GRID_H * 80].rearrange("p (r w) -> p r w", w=80)
                                   for b in (dst, src))
                    link(dve, sc, dve.memset(wide[:, :, 8 - h:8], 0.0))
                    link(dve, sc, dve.memset(wide[:, :, 8 + GRID_W:8 + GRID_W + h], 0.0))
                    link(dve, sc, dve.tensor_tensor(
                        wide[:, :, 8:8 + GRID_W], src[:, 8 - h:8 - h + GRID_H, :],
                        icnt[:, g, 0:GRID_H].unsqueeze(2).broadcast_to([P, GRID_H, GRID_W]), ALU.mult))
                    yield
                    src, dst, L = wide, wide2, 2
                    while L <= w:
                        lo, n = 8 - h, GRID_W + w - L
                        link(dve, sc, dve.tensor_tensor(dst[:, :, lo:lo + n], src[:, :, lo:lo + n],
                                                        src[:, :, lo + L // 2:lo + L // 2 + n], ALU.add))
                        src, dst, L = dst, src, 2 * L
                        yield
                    link(dve, sc, dve.tensor_tensor(
                        dst[:, :, 0:GRID_W], src[:, :, 8 - h:8 - h + GRID_W],
                        icnt[:, g, GRID_H:].unsqueeze(1).broadcast_to([P, GRID_H, GRID_W]), ALU.mult))
                    ug = uT[:, g, :].rearrange("p (r w) -> p r w", w=GRID_W)
                    dve.tensor_tensor(ug, dst[:, :, 0:GRID_W], ug, ALU.subtract).then_inc(S["pooled"], 1)
                    dve.wait_ge(S["pooled"], g + 1)
                    yield

            pooling = pool_steps()
            for i in range(4, 8):
                late_row(i)
                if i < 7:
                    late_sum(i + 1)
                for _ in range(3):
                    next(pooling, None)
            dve.wait_ge(S["cum_read"], NT)
            for n, g in enumerate(groups):
                if g[0] in "kq":
                    a, gr = g[1], g[2]
                    t0, m = tok_groups[gr]
                    dve.wait_ge(S["proj_done"], n + 1)
                    for d in range(2):
                        proj_out = ps[:, n % PB, 0:m * P].rearrange("p (t i) -> p t i", i=P)
                        if g[0] == "k":
                            kd = kdec[:, t0:t0 + m, d, a, :]
                            ins = dve.tensor_tensor(kd, proj_out, kd, ALU.mult)
                        else:
                            qd = qdec[:, t0:t0 + m, d, a, :]
                            ins = dve.scalar_tensor_tensor(out=qd, in0=proj_out, scalar=DK ** -0.5, in1=qd,
                                                           op0=ALU.mult, op1=ALU.mult)
                    ins.then_inc(S["ev_v"], 1)
                    for _ in range(3):
                        next(pooling, None)
            link(dve, sc, dve.tensor_tensor(dec[:, :, :, :].rearrange("p t d a -> p (t d a)"), dec1[:, :, :, :].rearrange("p t d a -> p (t d a)"),
                                            dec2[:, :, :, :].rearrange("p t d a -> p (t d a)"), ALU.mult))

            for n, tt in enumerate(steps()):
                if n >= 1:
                    dve.wait_ge(S["state_step"], n)
                for d in range(2):
                    t = tt[d]
                    for a in range(2):
                        if n >= NCT:
                            ins = dve.tensor_scalar(state_in[:, t, d, a, :], state[:, d, a, :], dec1[:, t, d, a:a + 1], None, ALU.mult)
                            ins.then_inc(S["state_saved"], 1)
                if n >= 1:
                    for d in range(2):
                        for a in range(2):
                            ins = dve.tensor_scalar(state[:, d, a, :], state[:, d, a, :], dec[:, tt[d], d, a:a + 1], None, ALU.mult)
                    link(dve, sc, ins)
                dve.wait_ge(S["kv_done"], n + 1)
                for d in range(2):
                    t = tt[d]
                    for a in range(2):
                        kv = ps[:, 5, (2 * d + a) * P:(2 * d + a + 1) * P]
                        if n >= 1:
                            ins = dve.scalar_tensor_tensor(out=state[:, d, a, :], in0=kv, scalar=dec2[:, t, d, a:a + 1],
                                                           in1=state[:, d, a, :], op0=ALU.mult, op1=ALU.add)
                        else:
                            ins = dve.tensor_scalar(state[:, d, a, :], kv, dec2[:, t, d, a:a + 1], None, ALU.mult)
                ins.then_inc(S["state_step"], 1)
                next(pooling, None)
            for _ in pooling:
                pass
            def residual(u, h):
                cols = slice(h * HALF, (h + 1) * HALF)
                dve.wait_ge(S["y_done"], 2 * u + h + 1)
                dve.tensor_tensor(hx2[:, u % 2, cols], ps[:, 5 + h, :], g1b[:, cols], ALU.mult).then_inc(S["gated"], 1)
                dve.wait_ge(S["gated"], 2 * u + h + 1)
                dve.tensor_tensor(x2[:, u, cols], x2[:, u, cols], hx2[:, u % 2, cols], ALU.add).then_inc(S["x2_ready"], 1)

            for t in range(NX + 1):
                u = t - 1
                if t < NX:
                    dve.wait_ge(S["sc_done"], t + 1)
                    for h in range(2):
                        dve.tensor_tensor(smask[:, h].rearrange("p d (a i) -> p d a i", a=2), ps[:, h, :].rearrange("p (d a i) -> p d a i", d=2, a=2),
                                          mask[:, :, :].unsqueeze(2).broadcast_to([P, 2, 2, P]), ALU.mult).then_inc(S["sc_masked"], 1)
                    dve.wait_ge(S["sc_masked"], 2 * t + 2)
                    if t >= 1:
                        dve.wait_ge(S["o_done"], t)
                    dve.tensor_tensor(ssum, smask[:, :, 0, :], smask[:, :, 1, :], ALU.add).then_inc(S["s_summed"], 1)
                if t >= 1:
                    if u == 0:
                        dve.wait_ge(S["bcast_loaded"], 48)
                    dve.wait_ge(row_loaded[u], 32)
                    if u >= 2:
                        dve.wait_ge(hx2_stored[u % 2], 16 * (u // 2))
                        dve.wait_ge(S["hx2_turned"], 2 * (u - 1))
                    residual(u, 0)
                if t < NX:
                    dve.wait_ge(S["osq_ready"], 2 * t + 2)
                    dve.tensor_reduce(ost[:, 0:4], sqg.rearrange("p h (a n) -> p (h a) n", a=2), AX.X, ALU.add).then_inc(S["oss_ready"], 1)
                    dve.wait_ge(S["opow_ready"], t + 1)
                    if t >= 1:
                        dve.wait_ge(S["ot_done"], t)
                    on = onorm.rearrange("p (a h n) -> p a h n", a=2, h=2)
                    for h in range(2):
                        dve.tensor_tensor(on[:, :, h, :], ps[:, 2 + h, 0:256].rearrange("p (a n) -> p a n", a=2),
                                          ost[:, 8 + 2 * h:10 + 2 * h].unsqueeze(2).broadcast_to([P, 2, DV]), ALU.mult).then_inc(S["on_ready"], 1)
                    dve.wait_ge(S["on_ready"], 2 * t + 2)
                    dve.tensor_tensor(onorm, onorm, gate[:, t, :], ALU.mult).then_inc(S["og_ready"], 1)
                if t >= 1:
                    residual(u, 1)
                    dve.wait_ge(S["pow2_ready"], u + 1)
                    link(dve, sc, dve.scalar_tensor_tensor(out=hx2[:, u % 2, :], in0=x2[:, u, :], scalar=stat[:, 2 * NT + u:2 * NT + u + 1],
                                                           in1=a2b, op0=ALU.mult, op1=ALU.mult))
                    dve.tensor_tensor(hx2[:, u % 2, :], hx2[:, u % 2, :], s2b, ALU.add).then_inc(S["hx2_ready"], 1)
            rc = ("r_chain", [0])
            v = lambda ins: link(dve, rc, ins)
            R = rt
            dve.wait_ge(S["rl_out"], NX)
            for n in ("sel", "pre", "pre2"):
                dve.memset(R[n][:, 0:4, :], 0.0)
            dve.memset(R["cb"][:, :, 0:8], 0.0)
            v(dve.memset(R["cb2"][:, :, 0:8], 0.0))
            dve.wait_ge(S["sig_ready"], 1)
            v(dve.tensor_tensor(R["sbias"], R["s"], bias_b[:, :].unsqueeze(1).broadcast_to([P, NX, NE]), ALU.add))
            G = R["sbias"].rearrange("p t (g j) -> p (t g) j", j=4)
            v(dve.tensor_tensor(R["hi"], G[:, :, 0:2], G[:, :, 2:4], ALU.max))
            v(dve.tensor_tensor(R["lo"], G[:, :, 0:2], G[:, :, 2:4], ALU.min))
            v(dve.tensor_tensor(R["t1"], R["hi"][:, :, 0:1], R["hi"][:, :, 1:2], ALU.max))
            v(dve.tensor_tensor(R["t2"], R["hi"][:, :, 0:1], R["hi"][:, :, 1:2], ALU.min))
            v(dve.tensor_tensor(R["hi"][:, :, 0:1], R["lo"][:, :, 0:1], R["lo"][:, :, 1:2], ALU.max))
            v(dve.tensor_tensor(R["t2"], R["t2"], R["hi"][:, :, 0:1], ALU.max))
            v(dve.tensor_tensor(R["t1"], R["t1"], R["t2"], ALU.add))
            gsc = R["t1"].rearrange("p (t g) o -> p t (g o)", g=NGR)

            def first_best(oh, values, eq, weights, shape):
                v(dve.tensor_reduce(R["mx"], values, AX.X, ALU.max))
                v(dve.tensor_tensor(eq, values, R["mx"].broadcast_to(shape), ALU.is_equal))
                v(dve.tensor_tensor(eq, eq, weights.unsqueeze(1).broadcast_to(shape), ALU.mult))
                v(dve.tensor_reduce(R["mx"], eq, AX.X, ALU.max))
                v(dve.tensor_tensor(oh, eq, R["mx"].broadcast_to(shape), ALU.is_equal))

            first_best(R["goh"], gsc, R["geq"], iota_e[:, NE - NGR:NE], [P, NX, NGR])
            mb4 = R["mb"].rearrange("p t (g j) -> p (t g) j", j=4)
            goh = R["goh"].rearrange("p t g -> p (t g)").unsqueeze(2).broadcast_to([P, NX * NGR, 4])
            v(dve.tensor_tensor(mb4, G, goh, ALU.mult))
            v(dve.tensor_scalar(R["goh"], R["goh"], BIG, -BIG, ALU.mult, ALU.add))
            v(dve.tensor_tensor(mb4, mb4, goh, ALU.add))
            first_best(R["oh1"], R["mb"], R["eq"], iota_e[:, :], [P, NX, NE])
            v(dve.scalar_tensor_tensor(out=R["mb"], in0=R["oh1"], scalar=-BIG, in1=R["mb"], op0=ALU.mult, op1=ALU.add))
            first_best(R["oh2"], R["mb"], R["eq"], iota_e[:, :], [P, NX, NE])
            v(dve.tensor_tensor(R["sel"][:, 4:, :], R["oh1"], R["oh2"], ALU.add))
            for src, dst, sh in (("sel", "pre", 1), ("pre", "pre2", 2), ("pre2", "pre", 4)):
                v(dve.tensor_tensor(R[dst][:, 4:, :], R[src][:, 4:, :], R[src][:, 4 - sh:4 + NX - sh, :], ALU.add))
            dve.sem_inc(S["route_ready"], 1)
            for k, oh in enumerate(("oh1", "oh2")):
                v(dve.tensor_tensor(R["eq"], R["s"], R[oh], ALU.mult))
                v(dve.tensor_reduce(R["s12"][:, k, :], R["eq"], AX.X, ALU.add))
            v(dve.tensor_tensor(R["ssum"].rearrange("p t o -> p (t o)"), R["s12"][:, 0, :], R["s12"][:, 1, :], ALU.add))
            v(dve.reciprocal(R["ssum"], R["ssum"]))
            v(dve.tensor_tensor(R["wk"], R["s12"], R["ssum"].rearrange("p t o -> p (o t)").unsqueeze(1).broadcast_to([P, 2, NX]), ALU.mult))
            dve.wait_ge(S["rank_done"], 1)
            v(dve.tensor_copy(R["rank"].rearrange("p t e -> p (t e)"), ps[:, 7, 0:NTE]))
            v(dve.tensor_copy(R["tot"].rearrange("p o e -> p (o e)"), ps[:, 7, NTE:NTE + NE]))
            v(dve.tensor_tensor(cmp16[:, :, :], R["tot"].rearrange("p o e -> p (o e)").unsqueeze(2).broadcast_to([P, NE, KC]),
                                thresh[:, :].unsqueeze(1).broadcast_to([P, NE, KC]), ALU.is_gt))
            nbl = R["nbl"].rearrange("p o e -> p (o e)")
            v(dve.tensor_reduce(nbl, cmp16[:, :, :], AX.X, ALU.add))
            v(dve.tensor_scalar(nbl, nbl, 1.0, None, ALU.max))
            cb, cb2 = (R[n].rearrange("p o e -> p (o e)") for n in ("cb", "cb2"))
            v(dve.tensor_copy(cb[:, 8:], nbl))
            for sh in (1, 2, 4, 8):
                v(dve.tensor_tensor(cb2[:, 8:], cb[:, 8:], cb[:, 8 - sh:8 + NE - sh], ALU.add))
                cb, cb2 = cb2, cb
            first = R["base"].rearrange("p o e -> p (o e)")
            v(dve.tensor_tensor(first, cb[:, 8:], nbl, ALU.subtract))

            def tables():
                v(dve.tensor_copy(tabs[:, T_NB:T_NB + 1], cb[:, 8 + NE - 1:8 + NE]))
                v(dve.tensor_tensor(cmpb, iota_p[:, 0:NB].unsqueeze(2).broadcast_to([P, NB, NE]),
                                    cb[:, 8:].unsqueeze(1).broadcast_to([P, NB, NE]), ALU.is_ge))
                v(dve.tensor_reduce(ebf[:, :], cmpb, AX.X, ALU.add))
                v(dve.tensor_scalar(ebf[:, :], ebf[:, :], float(NE - 1), None, ALU.min))
                v(dve.tensor_copy(tabs[:, T_E:T_E + NB], ebf[:, :]))
                for j in range(3):
                    v(dve.tensor_scalar(tabs[:, T_PLACE + j * NB:T_PLACE + (j + 1) * NB], ebf[:, :], 3.0, 3.0 + j, ALU.mult, ALU.add))
                place = tabs[:, T_PLACE:T_PLACE + 3 * NB]
                v(dve.tensor_scalar(place, place, PLACES - 1, None, ALU.bitwise_and))
                v(dve.tensor_tensor(tabs[:, T_NEW:T_NEW + NB - 1], ebf[:, 1:NB], ebf[:, 0:NB - 1], ALU.subtract))

            v(dve.scalar_tensor_tensor(out=R["rank"], in0=R["base"].broadcast_to([P, NX, NE]), scalar=float(P), in1=R["rank"],
                                       op0=ALU.mult, op1=ALU.add))
            for k, oh in enumerate(("oh1", "oh2")):
                v(dve.tensor_tensor(R["eq"], R["rank"], R[oh], ALU.mult))
                v(dve.tensor_reduce(R["dest"][:, k, :], R["eq"], AX.X, ALU.add))
            v(dve.tensor_copy(desti[:, :, :], R["dest"]))
            v(dve.tensor_scalar(blki[:, :, :], desti[:, :, :], 7, None, ALU.logical_shift_right))
            v(dve.tensor_scalar(posi[:, :, :], desti[:, :, :], P - 1, None, ALU.bitwise_and))
            v(dve.tensor_copy(R["blkf"], blki[:, :, :]))
            v(dve.tensor_copy(R["posf"], posi[:, :, :]))
            for k in range(2):
                here = slice(k * NX, (k + 1) * NX)
                blk, is_blk = R["blkf"][:, k, :].unsqueeze(2).broadcast_to([P, NX, NB]), slotv[:, here, 1, :]
                v(dve.tensor_tensor(is_blk, iota_p[:, 0:NB].unsqueeze(1).broadcast_to([P, NX, NB]), blk, ALU.is_equal))
                v(dve.tensor_tensor(slotv[:, here, 0, :], is_blk, tokid[:, :].unsqueeze(2).broadcast_to([P, NX, NB]), ALU.mult))
                v(dve.tensor_tensor(is_blk, is_blk, R["wk"][:, k, :].unsqueeze(2).broadcast_to([P, NX, NB]), ALU.mult))
                dve.tensor_tensor(onehot[:, here, :], iota_p[:, :].unsqueeze(1).broadcast_to([P, NX, P]),
                                  R["posf"][:, k, :].unsqueeze(2).broadcast_to([P, NX, P]), ALU.is_equal).then_inc(S["slots_done"], 1)
            tables()
            dve.wait_ge(S["rank_done"], 2)
            v(dve.tensor_copy(slot_tok[:, 0:NB], ps[:, 6, 256:256 + NB]))
            dve.tensor_copy(slot_w[:, :], ps[:, 6, 256 + NB:256 + 2 * NB]).then_inc(S["table_ready"], 1)
            dve.wait_ge(S["table_ready"], 1)
            nb = dve.value_load(tabs[0:1, T_NB:T_NB + 1], min_val=1, max_val=MAXB)

            def turn_out(b):
                dve.wait_ge(S["xh_ready"], b + 1)
                dve.tensor_tensor(xTl[:, :], ps[:, 0:2, :].rearrange("p h n -> p (h n)"), xTh[:, :].bitcast(F32), ALU.subtract)\
                    .then_inc(S["xT_ready"], 1)

            def low(j, base, e, k):
                part = slice(k * UNIT // 2, (k + 1) * UNIT // 2)
                dve.wait_ge(w_high[j], 2 * e + (k + 1))
                dve.sem_inc(S["high_seen"], 1)
                dve.tensor_tensor(w_lo[j][:, part], raw[:, bass.ds(base + k * (UNIT // 2), UNIT // 2)],
                                  w_hi[j][:, part].bitcast(F32), ALU.subtract).then_inc(w_split[j], 1)

            turn_out(0)
            dve.wait_ge(S["g2_loaded"], 16)
            low(2, 2 * UNIT, 0, 0)
            low(2, 2 * UNIT, 0, 1)
            with dve.Fori(0, NB // 2) as pair:
                i = pair * 2
                for s in range(2):
                    with dve.If(i + s < nb):
                        b = i + s
                        e, new, *place = (dve.value_load(tabs[0:1, bass.ds(b + at_, 1)], min_val=0, max_val=most)
                                          for at_, most in [(T_E, NE - 1), (T_NEW, 1)] + [(T_PLACE + j * NB, PLACES - 1) for j in range(2)])
                        dve.wait_ge(S["l1b"], b + 1)
                        dve.wait_ge(S["silu_done"], b + 1)
                        dve.tensor_tensor(hid[:, 0:256], hsil[:, 0:256], ps[:, 3, 0:256], ALU.mult).then_inc(S["hid_a"], 1)
                        dve.wait_ge(S["hTh_a"], b + 1)
                        dve.tensor_tensor(hTl[:, 0:256], ps[:, 5, 0:256], hTh[:, 0:256].bitcast(F32), ALU.subtract).then_inc(S["hT_a"], 1)
                        dve.wait_ge(S["l1c"], b + 1)
                        dve.tensor_tensor(hid[:, 256:512], hsil[:, 256:512], ps[:, 4, 0:256], ALU.mult).then_inc(S["hid_b"], 1)
                        with dve.If(new > 0):
                            low(0, place[0] * UNIT, e + 1, 0)
                        dve.wait_ge(S["hTh_b"], b + 1)
                        dve.tensor_tensor(hTl[:, 256:512], ps[:, 5, 256:512], hTh[:, 256:512].bitcast(F32), ALU.subtract).then_inc(S["hT_b"], 1)
                        turn_out(b + 1)
                        with dve.If(new > 0):
                            low(0, place[0] * UNIT, e + 1, 1)
                        dve.wait_ge(S["l2_done"], b + 1)
                        dve.wait_ge(y_stored[s], 16 * pair + 16)
                        for h in range(2):
                            cols = slice(h * HALF, (h + 1) * HALF)
                            dve.scalar_tensor_tensor(out=ysb[:, s, cols], in0=ps[:, 6 + h, :], scalar=slot_w[:, bass.ds(b, 1)],
                                                     in1=g2b[:, cols], op0=ALU.mult, op1=ALU.mult).then_inc(S["y_ready"], 1)
                        with dve.If(new > 0):
                            low(1, place[1] * UNIT, e + 1, 0)
            for t in range(NX + 1):
                if t < NX:
                    dve.wait_ge(fin_loaded[t % YS], 32 * (t // YS + 1))
                    if t == 0:
                        dve.wait_ge(S["x2_back"], 16)
                    for k, buf in enumerate((y1, y2)):
                        dve.tensor_tensor(x2[:, t, :], x2[:, t, :], buf[:, t % YS, :], ALU.add).then_inc(S["fin_add"], 1)
                        dve.wait_ge(S["fin_add"], 2 * t + k + 1)
                if t >= 1:
                    u = t - 1
                    dve.wait_ge(S["fpow_ready"], u + 1)
                    if u == 0:
                        dve.wait_ge(S["nf_loaded"], 16)
                    if u >= 2:
                        dve.wait_ge(stored[u % 2], 16 * (u // 2))
                    dve.scalar_tensor_tensor(out=fin[:, u % 2, :], in0=x2[:, u, :], scalar=stat[:, 2 * NT + u:2 * NT + u + 1],
                                             in1=nfb, op0=ALU.mult, op1=ALU.mult).then_inc(S["fout_ready"], 1)

        @block.tensor
        def _(pe):
            pe.wait_ge(S["small_loaded"], 16 * 7)
            pe.wait_ge(S["consts"], 2)
            pe.transpose(ps[:, 7, 0:85], small_rows[:, :], ident[0:85, 0:85]).then_inc(S["small_turned"], 1)

            def turn_rows(t):
                pe.wait_ge(S["scaled"], t + 1)
                if t >= 2:
                    pe.wait_ge(S["hx_a"], t - 1)
                    pe.wait_ge(S["hx_v"], t - 1)
                for k in range(KC):
                    ins = pe.transpose(ps[:, 2 * (t % 2) + k // 4, (k % 4) * P:(k % 4 + 1) * P],
                                       rows[:, t, k * P:(k + 1) * P], ident[:, :])
                ins.then_inc(S["turned"], 1)

            def modulation(j):
                w = unit_ready(pe, ("mod", j))
                if j == 3:
                    pe.wait_ge(S["small_ready"], 1)
                for k in range(KC):
                    ins = pe.matmul(ps[0:2, 4 + j, :], silu_c[:, k, :], w[:, k, :], start=(k == 0), stop=(k == KC - 1))
                ins.then_inc(S["mod_used"], 1)

            def turn_mod(j):
                pe.wait_ge(S["mod_row"], j + 1)
                for m in range(4):
                    col = 8 * j + 2 * m
                    ins = pe.transpose(ps[:, 4, col:col + 2], mod_rows[:, j * HALF + m * P:j * HALF + (m + 1) * P], ident[0:2, 0:2])
                if j == 3:
                    ins.then_inc(S["mod_turned"], 1)

            pe.wait_ge(S["silu_ready"], 1)
            for j in range(4):
                modulation(j)
            turn_rows(0)
            turn_rows(1)
            for j in range(4):
                turn_mod(j)
            for t in range(2, NT):
                turn_rows(t)

            pe.wait_ge(S["rw_loaded"], 16)
            for g, (t0, n) in enumerate(tok_groups):
                pe.wait_ge(S["hx_a"], NT)
                pe.wait_ge(S["hx_v"], NT)
                for k in range(KC):
                    ins = pe.matmul(ps[0:32, 5 + g, 0:n * P], w_r[:, k, :], hxT[:, k, t0 * P:(t0 + n) * P],
                                    start=(k == 0), stop=(k == KC - 1))
                ins.then_inc(S["r_done"], 1)
            pe.wait_ge(S["gk_loaded"], 48)
            pe.wait_ge(S["consts"], 25)

            def proj(n):
                g = groups[n]
                if n >= PB:
                    s, v = evac[n - PB]
                    pe.wait_ge(S[s], v)
                bank = n % PB
                if g[0] in "vg":
                    w = unit_ready(pe, (g[0], 0))
                    for k in range(KC):
                        ins = pe.matmul(ps[:, bank, :], hxT[:, k, g[1] * P:(g[1] + 1) * P], w[:, k, :],
                                        start=(k == 0), stop=(k == KC - 1))
                else:
                    kind, a, gr = g
                    w = unit_ready(pe, ("u" if kind == "u" else "qk", 0))
                    col = {"q": 0, "k": QK, "u": 0}[kind] + a * P
                    t0, m = tok_groups[gr]
                    for k in range(KC):
                        ins = pe.matmul(ps[:, bank, 0:m * P], w[:, k, col:col + P], hxT[:, k, t0 * P:(t0 + m) * P],
                                        start=(k == 0), stop=(k == KC - 1))
                ins.then_inc(S["proj_done"], 1)

            def logits(t):
                pe.wait_ge(S["rT_ready"], t // 4 + 1)
                if t >= 1:
                    pe.wait_ge(S["lg_min"], 2 * t)
                pe.matmul(ps[:, 4, :], rT[:, t * P:(t + 1) * P], w_gk[:, :, :].rearrange("p d n -> p (d n)"),
                          start=True, stop=True).then_inc(S["lg_done"], 1)

            def cumulate(t):
                pe.wait_ge(S["sp_ready"], t + 1)
                if t == 0:
                    pe.wait_ge(S["rT_ready"], 3)
                if t >= 1:
                    pe.wait_ge(S["cum_read"], t)
                for d in range(2):
                    for a in range(2):
                        col = (2 * d + a) * P
                        ins = pe.matmul(ps[:, 5 + d, a * (P + 1):(a + 1) * (P + 1)], spl[:, t % 2, col:col + P], tri[:, d, :],
                                        start=True, stop=True)
                ins.then_inc(S["cum_done"], 1)

            def late_turn(i):
                pe.wait_ge(S["macc_ready"], i + 1)
                if i >= 1:
                    pe.wait_ge(S["mrow_ready"], i)
                pe.matmul(ps[0:1, 7, :], ones[:, 0:1], macc, start=True, stop=True).then_inc(S["mrow_done"], 1)

            logits(0)
            logits(1)
            for t in range(NT):
                proj(t)
                cumulate(t)
                if t + 2 < NT:
                    logits(t + 2)
                if t >= 2 and t % 2 == 0:
                    late_turn(t // 2 - 1)
            for n in range(NT, group_no[("g", 0)]):
                proj(n)
                if n < NT + 8 and n % 2 == 1:
                    late_turn(4 + (n - NT) // 2)

            def turn_k(n):
                pe.wait_ge(S["ev_v"], nv)
                for d in range(2):
                    for a in range(2):
                        ins = pe.transpose(ps[:, 4, (2 * d + a) * P:(2 * d + a + 1) * P], kdec[:, steps()[n][d], d, a, :], ident[:, :])
                ins.then_inc(S["kt_done"], 1)

            turn_k(0)
            for n, tt in enumerate(steps()):
                pe.wait_ge(S["kt_ready"], n + 1)
                if n >= 1:
                    pe.wait_ge(S["state_step"], n)
                for d in range(2):
                    for a in range(2):
                        for h in range(2):
                            head = 2 * a + h
                            ins = pe.matmul(ps[DK * h:DK * h + DK, 5, (2 * d + a) * P:(2 * d + a + 1) * P],
                                            ktok[:, d, a, DK * h:DK * h + DK], vals[:, tt[d], head * DV:(head + 1) * DV],
                                            start=True, stop=True)
                ins.then_inc(S["kv_done"], 1)
                if n + 1 < NT:
                    turn_k(n + 1)
                if n < NX:
                    proj(group_no[("g", n)])
            pe.wait_ge(S["kt_ready"], NT)
            pe.wait_ge(S["state_step"], NT)
            pe.wait_ge(S["ev_a"], na)
            pe.wait_ge(S["mrow_ready"], 8)

            def mix_pooled(g):
                pe.wait_ge(S["pooled"], g + 1)
                for h in range(2):
                    if g >= 1:
                        pe.wait_ge(S["mixp_ready"], 2 * (g - 1) + h + 1)
                    pe.matmul(ps[:, 5 + h, :], wp[:, g, :], uT[:, g, h * HALF:(h + 1) * HALF], start=True, stop=True)\
                        .then_inc(S["mixp_done"], 1)

            def scores(t):
                if t >= 1:
                    pe.wait_ge(S["sc_masked"], 2 * t)
                for h in range(2):
                    r = slice(DK * h, DK * h + DK)
                    for d in range(2):
                        for a in range(2):
                            ins = pe.matmul(ps[:, h, (2 * d + a) * P:(2 * d + a + 1) * P], kdec[r, t, d, a, :], qdec[r, t, d, a, :],
                                            start=True, stop=True)
                ins.then_inc(S["sc_done"], 1)

            def outputs(t):
                pe.wait_ge(S["s_summed"], t + 1)
                if t >= 1:
                    pe.wait_ge(S["on_ready"], 2 * t)
                for h in range(2):
                    r = slice(DK * h, DK * h + DK)
                    for a in range(2):
                        head = 2 * a + h
                        o = ps[:, 2 + h, a * DV:(a + 1) * DV]
                        pe.matmul(o, ssum[:, h, a * P:(a + 1) * P], vals[:, t, head * DV:(head + 1) * DV], start=True, stop=False)
                        for d in range(2):
                            ins = pe.matmul(o, qdec[r, t, d, a, :], state_in[r, t, d, a, :], start=False, stop=(d == 1))
                ins.then_inc(S["o_done"], 1)

            def turn_outputs(t):
                pe.wait_ge(S["og_ready"], t + 1)
                if t >= 1:
                    pe.wait_ge(S["mixg_ready"], t)
                for h in range(HEADS):
                    ins = pe.transpose(ps[:, 4, h * P:(h + 1) * P], onorm[:, h * DV:(h + 1) * DV], ident[:, :])
                ins.then_inc(S["ot_done"], 1)

            def project_out(t, h):
                w = unit_ready(pe, ("out", h))
                if h == 0:
                    pe.wait_ge(S["mixg_ready"], t + 1)
                    if t == 0:
                        pe.wait_ge(S["mixp_ready"], 2 * NG)
                if t >= 1:
                    pe.wait_ge(S["gated"], 2 * (t - 1) + h + 1)
                for k in range(KC):
                    m = uT[:, k, t * P:(t + 1) * P] if k < NG else gate[:, t, (k - NG) * P:(k - NG + 1) * P]
                    ins = pe.matmul(ps[:, 5 + h, :], m, w[:, k, :], start=(k == 0), stop=(k == KC - 1))
                ins.then_inc(S["y_done"], 1)

            def turn_normed(u, h):
                if h == 0:
                    pe.wait_ge(S["hx2_ready"], u + 1)
                    if u >= 1:
                        pe.wait_ge(S["rl_out"], u)
                else:
                    pe.wait_ge(S["hx2T_ready"], 2 * u + 1)
                for k in range(4):
                    ins = pe.transpose(ps[:, 7, k * P:(k + 1) * P], hx2[:, u % 2, (4 * h + k) * P:(4 * h + k + 1) * P], ident[:, :])
                ins.then_inc(S["hx2_turned"], 1)

            def router(u):
                pe.wait_ge(S["hx2T_ready"], 2 * u + 2)
                for k in range(KC):
                    ins = pe.matmul(ps[0:NE, 7, 0:P], w_rt[:, k, :], hx2T[:, k * P:(k + 1) * P],
                                    start=(k == 0), stop=(k == KC - 1))
                ins.then_inc(S["logit_done"], 1)

            def turn_logits(u):
                pe.wait_ge(S["rl_ready"], u + 1)
                pe.transpose(ps[:, 7, P:P + NE], rlT[:, :], ident[0:NE, 0:NE]).then_inc(S["rl_turned"], 1)

            for t in range(NX + 2):
                if t < NX:
                    scores(t)
                if t == 0:
                    mix_pooled(0)
                    mix_pooled(1)
                if t >= 3:
                    turn_logits(t - 3)
                if 1 <= t <= NX:
                    project_out(t - 1, 0)
                if t >= 2:
                    turn_normed(t - 2, 0)
                if t < NX:
                    outputs(t)
                if t >= 2:
                    turn_normed(t - 2, 1)
                if 1 <= t <= NX:
                    project_out(t - 1, 1)
                if t == 0:
                    mix_pooled(2)
                    mix_pooled(3)
                if t < NX:
                    turn_outputs(t)
                if t >= 2:
                    router(t - 2)
            turn_logits(NX - 1)
            pe.wait_ge(S["route_ready"], 1)
            pre = rt["pre"][:, 3:, :].rearrange("p t e -> p (t e)")
            pe.matmul(ps[:, 7, 0:NTE], strict[:, :], rt["sel"][:, 4:, :].rearrange("p t e -> p (t e)"), start=True, stop=False)
            pe.matmul(ps[:, 7, 0:NTE], ones[:, :], pre[:, 0:NTE], start=False, stop=True)
            pe.matmul(ps[:, 7, NTE:NTE + NE], ones[:, :], pre[:, NTE:NTE + NE], start=True, stop=True).then_inc(S["rank_done"], 1)
            for n in range(2 * NX):
                if n % NX == 0:
                    pe.wait_ge(S["slots_done"], n // NX + 1)
                ins = pe.matmul(ps[:, 6, 256:256 + 2 * NB], onehot[:, n, :], slotv[:, n].rearrange("p w b -> p (w b)"),
                                start=(n == 0), stop=(n == 2 * NX - 1))
            ins.then_inc(S["rank_done"], 1)
            pe.wait_ge(S["table_ready"], 1)
            nb = pe.value_load(tabs[0:1, T_NB:T_NB + 1], min_val=1, max_val=MAXB)
            pe.sem_inc(S["y_ready"], 2)

            def turn_block(b):
                pe.wait_ge(S["gathered"], 16 * b + 16)
                for k in range(KC):
                    ins = pe.transpose(ps[:, k // 4, (k % 4) * P:(k % 4 + 1) * P], xg[:, k * P:(k + 1) * P], ident[:, :])
                ins.then_inc(S["x_turned"], 1)

            def product(out_ap, parts, lhs, w_parts, cols, start, stop):
                for n, (l, w) in enumerate(((0, 0), (0, 1), (1, 0))):
                    ins = pe.matmul(out_ap, parts[l][:, lhs], w_parts[w][:, cols], start=start and n == 0, stop=stop and n == 2)
                return ins

            turn_block(0)
            with pe.Fori(0, NB // 2) as pair:
                i = pair * 2
                for s in range(2):
                    with pe.If(i + s < nb):
                        b = i + s
                        e = pe.value_load(tabs[0:1, bass.ds(b + T_E, 1)], min_val=0, max_val=NE - 1)
                        x_parts, h_parts = (xTh, xTl), (hTh, hTl)
                        pe.wait_ge(S["xT_ready"], b + 1)
                        for k in range(KC):
                            if k % 4 == 0:
                                pe.wait_ge(w_split[0], 2 * e + (k // 4 + 1))
                            ins = product(ps[:, 2, :], x_parts, slice(k * P, (k + 1) * P), (w1h, w1l),
                                          slice(k * HALF, (k + 1) * HALF), k == 0, k == KC - 1)
                        ins.then_inc(S["l1a"], 1)
                        for q, done in enumerate(("l1b", "l1c")):
                            for k in range(KC):
                                if q == 0 and k % 4 == 0:
                                    pe.wait_ge(w_split[1] if k == 0 else S["w3b_split"], e + 1)
                                col = k * HALF + q * 256
                                ins = product(ps[:, 3 + q, 0:256], x_parts, slice(k * P, (k + 1) * P), (w3h, w3l),
                                              slice(col, col + 256), k == 0, k == KC - 1)
                                if q == 1 and k == 3:
                                    pe.wait_ge(S["hid_a"], b + 1)
                                    for m in range(2):
                                        h_ins = pe.transpose(ps[:, 5, m * P:(m + 1) * P], hid[:, m * P:(m + 1) * P], ident[:, :])
                                    h_ins.then_inc(S["hta"], 1)
                            ins.then_inc(S[done], 1)
                        turn_block(b + 1)
                        pe.wait_ge(S["hT_a"], b + 1)
                        pe.wait_ge(S["y_ready"], 2 * i + (2 * s + 2))
                        for k in range(4):
                            if k % 2 == 0:
                                pe.wait_ge(w_split[2], 2 * e + (k // 2 + 1))
                            if k == 2:
                                pe.wait_ge(S["hT_b"], b + 1)
                            for h in range(2):
                                col = k * D + h * HALF
                                ins = product(ps[:, 6 + h, :], h_parts, slice(k * P, (k + 1) * P), (w2h, w2l),
                                              slice(col, col + HALF), k == 0, k == 3)
                            if k == 0:
                                pe.wait_ge(S["hid_b"], b + 1)
                                for m in range(2):
                                    h_ins = pe.transpose(ps[:, 5, (2 + m) * P:(3 + m) * P], hid[:, (2 + m) * P:(3 + m) * P], ident[:, :])
                                h_ins.then_inc(S["htb"], 1)
                        ins.then_inc(S["l2_done"], 1)


_INS = ["x", "c", "ctx", "c_ctx", "w_mod", "b_mod", "norm1", "norm2", "w_in", "w_gk2", "b_gk", "w_pool",
        "pool_scale", "gla_gain", "w_out", "w_router", "router_bias", "w1", "w3", "w2", "norm_f"]
_OUT = (1, NX * P, D)


def kernel(**inputs):
    import numpy as _np
    import concourse.bacc as _bacc
    from concourse import mybir as _mybir
    from concourse.bass_utils import run_bass_kernel_spmd as _run

    nc = _bacc.Bacc("TRN2", target_bir_lowering=False, num_devices=1)
    arrays, args = {}, []
    values = [(name, _np.ascontiguousarray(inputs[name])) for name in _INS] + [("inv_counts", box_inverse_counts())]
    for name, a in values:
        arrays[f"in_{name}_dram"] = a
        args.append(nc.dram_tensor(f"in_{name}_dram", a.shape, _mybir.dt.from_np(a.dtype), kind="ExternalInput").ap())
    args.append(nc.dram_tensor("out_dram", _OUT, F32, kind="ExternalOutput").ap())
    hybrid_block(nc, *args)
    r = _run(nc, [arrays], core_ids=[0])
    return r.results[0]["out_dram"]
```
